# Optimizing a Trainium2 kernel written in Bass

```python
import jax
import jax.numpy as jnp
from jax import lax
import numpy as np

D_MODEL = 1024
BATCH = 1
SEQ = 256
DEPTH = 2
DEC_BATCH = 8
DEC_SEQ = 8
PAST_LEN = 1024
PAGE_SIZE = 128

ATTN_WIDTH = D_MODEL // 2
N_HEADS = 8
HEAD_DIM = ATTN_WIDTH // N_HEADS
CONV_WIDTH = D_MODEL - ATTN_WIDTH
CONV_K = 31
MIX_WIDTH = ATTN_WIDTH + CONV_WIDTH
IN_COLS = 3 * ATTN_WIDTH + N_HEADS + 2 * CONV_WIDTH
Q_BLOCK = 128
FORGET_BIAS_LO = 1.0
FORGET_BIAS_HI = 9.0
N_MEM = 256
X_HEADS = 4
X_HEAD_DIM = D_MODEL // 8
X_WIDTH = X_HEADS * X_HEAD_DIM
D_FF = ((8 * D_MODEL // 3 + 127) // 128) * 128
N_EXPERTS = 8
TOP_K = 2
E_FF = 7 * D_MODEL // 2
N_DENSE = (DEPTH + 1) // 2
N_MOE = DEPTH // 2
EPS = 1e-6

kernel_name = 'fox_conformer_parallel_heads_decode_step'

def rmsnorm(x, g):
    xf = x.astype(jnp.float32)
    y = xf * lax.rsqrt(jnp.mean(xf * xf, axis=-1, keepdims=True) + EPS)
    return (y * g.astype(jnp.float32)).astype(x.dtype)

def layernorm(x, g, b):
    xf = x.astype(jnp.float32)
    xc = xf - jnp.mean(xf, axis=-1, keepdims=True)
    y = xc * lax.rsqrt(jnp.mean(xc * xc, axis=-1, keepdims=True) + EPS)
    return (y * g.astype(jnp.float32) + b.astype(jnp.float32)).astype(x.dtype)

def causal_dwconv(u_hist, w, b):
    out = lax.conv_general_dilated(u_hist, w[:, None, :].astype(u_hist.dtype), window_strides=(1,),
                                   padding='VALID', dimension_numbers=('NWC', 'WIO', 'NWC'),
                                   feature_group_count=u_hist.shape[-1])
    return out + b.astype(out.dtype)

def fox_prompt(q, k, v, c):
    n, s, h, dh = q.shape
    nb = s // Q_BLOCK
    scale = HEAD_DIM ** -0.5
    qb = q.reshape(n, nb, Q_BLOCK, h, dh).swapaxes(0, 1)
    cb = c.reshape(n, nb, Q_BLOCK, h).swapaxes(0, 1)
    ck = c.transpose(0, 2, 1)[:, :, None, :]
    kpos = jnp.arange(s)

    def block(args):
        qi, ci, i = args
        sc = jnp.einsum('bqhd,bkhd->bhqk', qi, k).astype(jnp.float32) * scale
        sc = sc + ci.transpose(0, 2, 1)[..., None] - ck
        qpos = i * Q_BLOCK + jnp.arange(Q_BLOCK)
        sc = jnp.where(kpos[None, :] <= qpos[:, None], sc, -jnp.inf)
        p = jax.nn.softmax(sc, axis=-1).astype(v.dtype)
        return jnp.einsum('bhqk,bkhd->bqhd', p, v)

    o = lax.map(block, (qb, cb, jnp.arange(nb)))
    return o.swapaxes(0, 1).reshape(n, s, h * dh)

def fox_sample(q, k, v, logf, k_past, v_past, lf_past):
    n, t = q.shape[0], q.shape[1]
    p_len = k_past.shape[1]
    scale = HEAD_DIM ** -0.5
    c_new = jnp.cumsum(logf, axis=1).transpose(0, 2, 1)
    d_past = (lax.cumsum(lf_past, axis=1, reverse=True) - lf_past).transpose(0, 2, 1)
    s_past = (jnp.einsum('bthd,bshd->bhts', q, k_past).astype(jnp.float32) * scale
              + c_new[..., None] + d_past[:, :, None, :])
    s_new = (jnp.einsum('bthd,bshd->bhts', q, k).astype(jnp.float32) * scale
             + c_new[..., None] - c_new[:, :, None, :])
    s_new = jnp.where(jnp.tril(jnp.ones((t, t), dtype=bool)), s_new, -jnp.inf)
    p = jax.nn.softmax(jnp.concatenate([s_past, s_new], axis=-1), axis=-1)
    o = (jnp.einsum('bhts,bshd->bthd', p[..., :p_len].astype(v_past.dtype), v_past)
         + jnp.einsum('bhts,bshd->bthd', p[..., p_len:].astype(v.dtype), v))
    return o.reshape(n, t, ATTN_WIDTH)

def cross_attend(h, mk, mv, w_cq, w_co):
    n, t, _ = h.shape
    q = (h @ w_cq).reshape(n, t, X_HEADS, X_HEAD_DIM)
    s = jnp.einsum('bthd,bmhd->bhtm', q, mk.astype(q.dtype)).astype(jnp.float32) * (X_HEAD_DIM ** -0.5)
    p = jax.nn.softmax(s, axis=-1).astype(mv.dtype)
    o = jnp.einsum('bhtm,bmhd->bthd', p, mv).reshape(n, t, X_WIDTH)
    return o @ w_co

def memory_kv(mem, g_mem, w_ckv):
    n, m, _ = mem.shape
    kv = rmsnorm(mem, g_mem) @ w_ckv
    mk = kv[..., :X_WIDTH].reshape(n, m, X_HEADS, X_HEAD_DIM)
    mv = kv[..., X_WIDTH:].reshape(n, m, X_HEADS, X_HEAD_DIM)
    return mk, mv

def swiglu(h, w_gu, w_down):
    d = w_down.shape[0]
    gu = h @ w_gu
    return (jax.nn.silu(gu[..., :d]) * gu[..., d:]) @ w_down

def moe_swiglu(h, w_router, b_router, w_e_gu, w_e_down):
    logits = (h @ w_router).astype(jnp.float32) + b_router.astype(jnp.float32)
    probs = jax.nn.softmax(logits, axis=-1)
    top_v, top_i = lax.top_k(probs, TOP_K)
    top_v = top_v / jnp.sum(top_v, axis=-1, keepdims=True)
    gates = jnp.sum(jax.nn.one_hot(top_i, N_EXPERTS, dtype=jnp.float32) * top_v[..., None], axis=-2)
    gates = gates.astype(h.dtype)
    y = jnp.zeros_like(h)
    for e in range(N_EXPERTS):
        y = y + gates[..., e:e + 1] * swiglu(h, w_e_gu[e], w_e_down[e])
    return y

def mixer_projections(x, P, l):
    n, t, _ = x.shape
    a = ATTN_WIDTH
    proj = rmsnorm(x, P['g_mix'][l]) @ P['w_in'][l]
    q = proj[..., :a].reshape(n, t, N_HEADS, HEAD_DIM)
    k = proj[..., a:2 * a].reshape(n, t, N_HEADS, HEAD_DIM)
    v = proj[..., 2 * a:3 * a].reshape(n, t, N_HEADS, HEAD_DIM)
    f_logit = proj[..., 3 * a:3 * a + N_HEADS]
    glu = proj[..., 3 * a + N_HEADS:]
    logf = jax.nn.log_sigmoid(f_logit.astype(jnp.float32) + P['b_fgate'][l].astype(jnp.float32))
    u = glu[..., :CONV_WIDTH] * jax.nn.sigmoid(glu[..., CONV_WIDTH:])
    return q, k, v, logf, u

def layer_rest(x, o_attn, u_hist, mk, mv, P, l):
    z = causal_dwconv(u_hist, P['w_dw'][l], P['b_dw'][l])
    o_conv = jax.nn.silu(layernorm(z, P['g_cln'][l], P['b_cln'][l]))
    merged = jnp.concatenate([rmsnorm(o_attn, P['g_attn_out'][l]), rmsnorm(o_conv, P['g_conv_out'][l])], axis=-1)
    x = x + merged @ P['w_out'][l]
    x = x + cross_attend(rmsnorm(x, P['g_cross'][l]), mk, mv, P['w_cq'][l], P['w_co'][l])
    h = rmsnorm(x, P['g_ffn'][l])
    if l % 2 == 0:
        x = x + swiglu(h, P['w_ff_gu'][l // 2], P['w_ff_down'][l // 2])
    else:
        x = x + moe_swiglu(h, P['w_router'][l // 2], P['b_router'][l // 2], P['w_e_gu'][l // 2], P['w_e_down'][l // 2])
    return x

def setup_inputs(seed: int = 0) -> dict:
    key = jax.random.key(seed)
    keys = list(jax.random.split(key, 40))

    def nrm(shape, scale):
        return jax.random.normal(keys.pop(), shape, jnp.float32) * scale

    def gain(shape):
        return 1.0 + nrm(shape, 0.02)

    n_pages = PAST_LEN // PAGE_SIZE
    n_used = DEC_BATCH * n_pages
    n_phys = n_used + max(1, n_used // 4)
    perm = jax.random.permutation(keys.pop(), n_phys)
    page_table = perm[:n_used].reshape(DEC_BATCH, n_pages).astype(jnp.int32)
    head_bias = jnp.linspace(FORGET_BIAS_LO, FORGET_BIAS_HI, N_HEADS, dtype=jnp.float32)
    D = D_MODEL
    return {
        'x_prompt': nrm((BATCH, SEQ, D), 1.0),
        'x_sample': nrm((DEC_BATCH, DEC_SEQ, D), 1.0),
        'cache_k': nrm((DEPTH, n_phys, PAGE_SIZE, N_HEADS, HEAD_DIM), 1.0),
        'cache_v': nrm((DEPTH, n_phys, PAGE_SIZE, N_HEADS, HEAD_DIM), 1.0),
        'cache_logf': jax.nn.log_sigmoid(head_bias + nrm((DEPTH, n_phys, PAGE_SIZE, N_HEADS), 1.0)),
        'cache_conv': nrm((DEPTH, DEC_BATCH, CONV_K - 1, CONV_WIDTH), 0.5),
        'cache_mem_k': nrm((DEPTH, DEC_BATCH, N_MEM, X_HEADS, X_HEAD_DIM), 1.0),
        'cache_mem_v': nrm((DEPTH, DEC_BATCH, N_MEM, X_HEADS, X_HEAD_DIM), 1.0),
        'page_table': page_table,
        'mem_prompt': nrm((BATCH, N_MEM, D), 1.0),
        'g_mix': gain((DEPTH, D)),
        'w_in': nrm((DEPTH, D, IN_COLS), D ** -0.5),
        'b_fgate': head_bias + nrm((DEPTH, N_HEADS), 0.1),
        'w_dw': nrm((DEPTH, CONV_K, CONV_WIDTH), CONV_K ** -0.5),
        'b_dw': nrm((DEPTH, CONV_WIDTH), 0.02),
        'g_cln': gain((DEPTH, CONV_WIDTH)),
        'b_cln': nrm((DEPTH, CONV_WIDTH), 0.02),
        'g_attn_out': gain((DEPTH, ATTN_WIDTH)),
        'g_conv_out': gain((DEPTH, CONV_WIDTH)),
        'w_out': nrm((DEPTH, MIX_WIDTH, D), MIX_WIDTH ** -0.5),
        'g_cross': gain((DEPTH, D)),
        'g_mem': gain((DEPTH, D)),
        'w_cq': nrm((DEPTH, D, X_WIDTH), D ** -0.5),
        'w_ckv': nrm((DEPTH, D, 2 * X_WIDTH), D ** -0.5),
        'w_co': nrm((DEPTH, X_WIDTH, D), X_WIDTH ** -0.5),
        'g_ffn': gain((DEPTH, D)),
        'w_ff_gu': nrm((N_DENSE, D, 2 * D_FF), D ** -0.5),
        'w_ff_down': nrm((N_DENSE, D_FF, D), D_FF ** -0.5),
        'w_router': nrm((N_MOE, D, N_EXPERTS), D ** -0.5),
        'b_router': nrm((N_MOE, N_EXPERTS), 0.01),
        'w_e_gu': nrm((N_MOE, N_EXPERTS, D, 2 * E_FF), D ** -0.5),
        'w_e_down': nrm((N_MOE, N_EXPERTS, E_FF, D), E_FF ** -0.5),
        'g_final': gain((D,)),
    }

def reference(x_prompt, x_sample, cache_k, cache_v, cache_logf, cache_conv, cache_mem_k, cache_mem_v,
              page_table, mem_prompt, g_mix, w_in, b_fgate, w_dw, b_dw, g_cln, b_cln, g_attn_out,
              g_conv_out, w_out, g_cross, g_mem, w_cq, w_ckv, w_co, g_ffn, w_ff_gu, w_ff_down,
              w_router, b_router, w_e_gu, w_e_down, g_final):
    P = dict(g_mix=g_mix, w_in=w_in, b_fgate=b_fgate, w_dw=w_dw, b_dw=b_dw, g_cln=g_cln, b_cln=b_cln,
             g_attn_out=g_attn_out, g_conv_out=g_conv_out, w_out=w_out, g_cross=g_cross, w_cq=w_cq,
             w_co=w_co, g_ffn=g_ffn, w_ff_gu=w_ff_gu, w_ff_down=w_ff_down, w_router=w_router,
             b_router=b_router, w_e_gu=w_e_gu, w_e_down=w_e_down)

    x = x_prompt
    kp, vp, lfp, cvp, mkp, mvp = [], [], [], [], [], []
    for l in range(DEPTH):
        q, k, v, logf, u = mixer_projections(x, P, l)
        o_attn = fox_prompt(q, k, v, jnp.cumsum(logf, axis=1))
        u_hist = jnp.pad(u, ((0, 0), (CONV_K - 1, 0), (0, 0)))
        mk, mv = memory_kv(mem_prompt, g_mem[l], w_ckv[l])
        x = layer_rest(x, o_attn, u_hist, mk, mv, P, l)
        kp.append(k)
        vp.append(v)
        lfp.append(logf)
        cvp.append(u_hist[:, -(CONV_K - 1):])
        mkp.append(mk)
        mvp.append(mv)
    y_prompt = rmsnorm(x, g_final)

    x = x_sample
    n_dec = x_sample.shape[0]
    ks, vs, lfs, cvs = [], [], [], []
    for l in range(DEPTH):
        q, k, v, logf, u = mixer_projections(x, P, l)
        k_past = cache_k[l][page_table].reshape(n_dec, -1, N_HEADS, HEAD_DIM)
        v_past = cache_v[l][page_table].reshape(n_dec, -1, N_HEADS, HEAD_DIM)
        lf_past = cache_logf[l][page_table].reshape(n_dec, -1, N_HEADS).astype(jnp.float32)
        o_attn = fox_sample(q, k, v, logf, k_past, v_past, lf_past)
        u_hist = jnp.concatenate([cache_conv[l].astype(u.dtype), u], axis=1)
        x = layer_rest(x, o_attn, u_hist, cache_mem_k[l], cache_mem_v[l], P, l)
        ks.append(k)
        vs.append(v)
        lfs.append(logf)
        cvs.append(u_hist[:, -(CONV_K - 1):])
    y_sample = rmsnorm(x, g_final)

    return (y_prompt, y_sample,
            jnp.stack(kp), jnp.stack(vp), jnp.stack(lfp), jnp.stack(cvp), jnp.stack(mkp), jnp.stack(mvp),
            jnp.stack(ks), jnp.stack(vs), jnp.stack(lfs), jnp.stack(cvs))


_drawn_inputs = setup_inputs


def setup_inputs(seed=0):
    import zlib

    import numpy as np

    out = dict(_drawn_inputs(seed))
    spreads = {}
    factors = {'g_cross': 4.309, 'g_mem': 2.843, 'b_router': 8.246, 'g_final': 8.148}
    for name, (base, spread) in spreads.items():
        noise = np.random.default_rng([zlib.crc32(name.encode()), seed]).standard_normal(out[name].shape)
        drawn = base * np.exp(spread * noise) if base else spread * noise
        out[name] = jnp.asarray(drawn.astype(out[name].dtype))
    for name, factor in factors.items():
        out[name] = (out[name] * factor).astype(out[name].dtype)
    return out
```

```python
from contextlib import ExitStack

import concourse.bass as bass
from concourse import mybir

F32 = mybir.dt.float32
F32R = mybir.dt.float32r
I32 = mybir.dt.int32
U32 = mybir.dt.uint32
ALU = mybir.AluOpType
ACT = mybir.ActivationFunctionType
AX = mybir.AxisListType

P = 128
NEG = -1.0e30
EPS = 1e-6


def build_program(nc, d):
    DEPTH, N_PHYS, PAGE, NH, DH = d["cache_k"].shape
    _, SEQ, D = d["x_prompt"].shape
    DB, DS, _ = d["x_sample"].shape
    NPG = d["page_table"].shape[1]
    PAST = NPG * PAGE
    AW = NH * DH
    CONV_K, CW = d["w_dw"].shape[1:]
    HIST = CONV_K - 1
    XH = d["cache_mem_k"].shape[3]
    NMEM = d["cache_mem_k"].shape[2]
    XW = XH * P
    FF = d["w_ff_down"].shape[1]
    NE, EF = d["w_e_down"].shape[1:3]
    NS = DB * DS
    assert SEQ == 2 * P and NS == 64 and D == 1024 and AW == CW == XW == 512 and PAGE == P
    assert NMEM == 2 * P and DH == 64 and DS == 8 and DB == 8 and DEPTH == 2 and NPG == 8
    KD = D // P
    ROWS = [P, P, NS]
    COLS = [slice(0, P), slice(P, 2 * P), slice(2 * P, 2 * P + NS)]
    NTOK = SEQ + NS
    NFG = FF // 256
    NEG_G = EF // 256
    MAX_ITEMS = NE + 4
    X_SCALE = float(P) ** -0.5
    Q_SCALE = float(DH) ** -0.5
    PAIRS, QUADS = DB // 2, DB // 4
    RING = 4
    MOE_RING = 7
    SPLIT = 3
    DVE_COLS = 1664
    SLOT = 4096
    HALF = SLOT // 2
    STAGES = [(l, s) for l in range(DEPTH) for s in ("mix", "merged", "cross", "ffn")]
    STAGE_AT = {k: n for n, k in enumerate(STAGES)}
    NORMS = [(l, s) for l in range(DEPTH) for s in ("mix", "cross", "ffn")]
    NORM_AT = {k: n for n, k in enumerate(NORMS)}
    GAIN_AT = {"mix": 0, "merged": 8, "cross": 16, "mem": 24, "ffn": 32}
    N_GAINS = 40

    ctx = ExitStack()
    with ctx:
        def sb(name, shape, dt=F32):
            return ctx.enter_context(nc.sbuf_tensor(name, shape, dt))

        def sb_at(name, base, at, shape):
            return nc.alloc_sbuf_tensor_at(name, shape, F32R, offset=base + 4 * at)

        def sem(name):
            return ctx.enter_context(nc.semaphore(name))

        ring = sb("ring", [P, RING * SLOT])
        x = sb("x", [P, 3, D])
        h = sb("h", [P, 3, D])
        hT = sb("hT", [P, KD, NTOK])
        mem_base = nc.sbuf_base
        memT = sb("memT", [P, KD, NMEM])
        ARENA = 20728
        arena_base = nc.sbuf_base
        arena = sb("arena", [P, ARENA])
        past_decay = sb("past_decay", [P, PAST])
        ident = sb("ident", [P, P])
        ones = sb("ones", [P, P])
        upto = sb("upto", [P, P])
        before = sb("before", [P, P])
        causal = sb("causal", [P, P])
        block_upto = sb("block_upto", [NS, NS])
        new_mask = sb("new_mask", [P, PAIRS, NS])
        pair_rows = sb("pair_rows", [P, PAIRS, NS])
        quad_rows = sb("quad_rows", [P, QUADS, NS])
        own_head = sb("own_head", [P, NH])
        own_xhead = sb("own_xhead", [P, XH])
        note = sb("note", [P, 24])
        step_of = sb("step_of", [NS, DS])
        batch_of = sb("batch_of", [NS, DB])
        gains = sb("gains", [P, DEPTH * N_GAINS])
        conv_w = sb("conv_w", [P, DEPTH, P])
        forget_w = sb("forget_w", [P, DEPTH, KD, NH])
        router_w = sb("router_w", [P, KD, NE])
        forget_b = sb("forget_b", [P, DEPTH, NH])
        router_b = sb("router_b", [P, NE])
        decay_rows = sb("decay_rows", [P, DEPTH, DB, NS])
        eps = sb("eps", [P, 1])
        item_ids = sb("item_ids", [P, MAX_ITEMS])
        iota8 = sb("iota8", [P, NE])
        stats = sb("stats", [P, 512])
        logf = sb("logf", [P, 3, NH])
        log_tmp = sb("log_tmp", [P, 2, 3, NH])
        cumT = sb("cumT", [NH, SEQ])
        neg_cumT = sb("neg_cumT", [NH, SEQ])
        cum_rows = sb("cum_rows", [NS, NH, DS])
        neg_cum_rows = sb("neg_cum_rows", [NS, NH, DS])
        cum_s = sb("cum_s", [NS, NH])
        own_cum = sb("own_cum", [P, PAIRS])


        def carve(at, *shape, rows=P):
            n = 1
            for s in shape:
                n *= s
            assert at + n <= ARENA, (at, n)
            v = arena[0:rows, at:at + n]
            names = " ".join(f"d{i}" for i in range(len(shape)))
            return v if len(shape) == 1 else v.rearrange(
                f"p ({names}) -> p {names}", **{f"d{i}": s for i, s in enumerate(shape)})

        qkv = carve(0, 3, 3 * AW)
        u = carve(4608, 3, CW)
        up = carve(6144, 4, HIST + SEQ)
        us = carve(7288, 4, DB, HIST + DS)
        q_heads = carve(8504, NH, SEQ)
        conv_z = carve(8504, 4, NTOK)
        q_rows = carve(10552, 4, DB, NH * DS)
        kT = carve(12600, 4, NTOK)
        KT = carve(13880, 2, 4, 512)
        conv_norm = carve(13880, 2, CW)
        p_prompt = [carve(13880, NH, P), carve(13880 + NH * P, NH, 2 * P)]
        PT = carve(17976, 9, P)
        probs = carve(19128, PAST + NS)
        o_masked = carve(20216, AW)
        hist_in = carve(17976, 2, CW)
        lf_pages = carve(0, PAGE, NH)
        lf_sum = carve(1024, NH, PAGE)
        lf_decay = carve(2048, NH, PAGE)
        gain_rows = carve(3072, P)
        dw_rows = carve(3200, DEPTH, P)
        mem = carve(3456, 2, D)
        page_suffix = carve(5504, P)
        spread8 = carve(5632, P, rows=DS)
        small8 = carve(5760, 2, DB, DS, rows=DS)
        mem_g = carve(0, KD, NMEM)
        mkv = carve(2048, 2, 2 * XW)
        mkT = carve(4096, XH, NMEM)
        xq = carve(5120, 3, XW)
        xqT = carve(6656, XH, SEQ)
        xq_rows = carve(7680, XH, DB, XH * DS)
        xKT = carve(8704, 2, XH, NMEM)
        xp = carve(10752, QUADS, NMEM)
        xp_prompt = carve(11264, 2, XH, NMEM)
        xPT = carve(13312, 4, 4, P)
        xo_masked = carve(15360, QUADS, XW)
        xo = carve(16384, 3, XW)
        silu = carve(0, 2, 3, 256)
        mid = carve(1536, 2, 3, 256)
        midT = carve(3072, FF // P, NTOK)
        raw_half = [ring[:, s * HALF:(s + 1) * HALF] for s in range(MOE_RING)]
        w_hi = [sb_at(f"w_hi{s}", arena_base, s * HALF, [P, HALF]) for s in range(SPLIT)]
        w_lo = [sb_at(f"w_lo{s}", arena_base, (SPLIT + s) * HALF, [P, HALF]) for s in range(SPLIT)]
        M0 = 2 * SPLIT * HALF
        e_midT_hi = sb_at("e_midT_hi", arena_base, M0, [P, EF // P, P])
        e_midT_lo = sb_at("e_midT_lo", arena_base, M0 + EF, [P, EF // P, P])
        e_xT_hi = sb_at("e_xT_hi", mem_base, 0, [P, KD, P])
        e_xT_lo = sb_at("e_xT_lo", mem_base, D, [P, KD, P])
        e_y = past_decay[:, :].rearrange("p (f n) -> p f n", f=2)
        e_rows = decay_rows[:, :, :, :].rearrange("p l b t -> p (l b t)").rearrange("p (m g n) -> p m g n", m=2, g=2)
        e_silu, e_mid = e_rows[:, 0, :, :], e_rows[:, 1, :, :]
        spare = ring[:, MOE_RING * HALF:RING * SLOT]
        e_pick, e_give, e_giveT = [spare[:, n * 3 * P:(n + 1) * 3 * P].rearrange("p (c t) -> p c t", c=3) for n in range(3)]
        iota_row = spare[:, 9 * P:10 * P]
        R0 = M0 + 2 * EF
        route = [carve(R0 + 24 * i, 3, NE) for i in range(12)]
        cnt = carve(R0 + 288, NE)
        nch = carve(R0 + 296, NE)
        ends = carve(R0 + 304, NE)
        starts = carve(R0 + 312, NE)
        item_e = carve(R0 + 320, MAX_ITEMS)
        item_c = carve(R0 + 332, MAX_ITEMS)
        item_oh = carve(R0 + 344, MAX_ITEMS, NE)
        item_t = carve(R0 + 440, MAX_ITEMS, NE)
        rank_i = carve(R0 + 536, 3, MAX_ITEMS)
        gate_i = carve(R0 + 572, 3, MAX_ITEMS)
        route4 = carve(R0 + 608, 3, MAX_ITEMS, NE)
        items = sb("items", [1, 2 + MAX_ITEMS], I32)
        page_idx = sb("page_idx", [P, 1], I32)
        scratch = nc.dram_tensor("decay_scratch", [P, NH * PAGE], F32, kind="Internal").ap()

        psum = [ctx.enter_context(nc.psum_tensor(f"bank{b}", [P, 512], F32)) for b in range(8)]

        bank_filled = [sem(f"bank_filled{b}") for b in range(8)]
        bank_emptied = [sem(f"bank_emptied{b}") for b in range(8)]
        slot_landed = [sem(f"slot_landed{s}") for s in range(RING)]
        down_read = sem("down_read")
        e_landed = [sem(f"expert_half_landed{s}") for s in range(MOE_RING)]
        w_hi_made = sem("w_hi_made")
        w_lo_made = [sem("w_lo_made_by_vector"), sem("w_lo_made_by_pool")]
        w_read = sem("w_read")
        xT_ready = sem("expert_columns_ready")
        column_step = sem("expert_column_step")
        midT_hi_made = sem("midT_hi_made")
        x_loaded = sem("x_loaded")
        mem_loaded = sem("mem_loaded")
        rows_loaded = sem("rows_loaded")
        small_loaded = sem("small_loaded")
        idx_loaded = sem("idx_loaded")
        idx_ready = sem("idx_ready")
        pages_gathered = sem("pages_gathered")
        decay_made = sem("decay_made")
        decay_stored = sem("decay_stored")
        decay_loaded = sem("decay_loaded")
        consts_made = sem("consts_made")
        masks_spread = sem("masks_spread")
        masks_made = sem("masks_made")
        pool_step = sem("pool_step")
        vector_step = sem("vector_step")
        scalar_step = sem("scalar_step")
        x_ready = sem("x_ready")
        std_ready = sem("std_ready")
        h_ready = sem("h_ready")
        mem_std = sem("mem_std")
        mem_ready = sem("mem_ready")
        mem_g_ready = sem("mem_g_ready")
        abs_ready = sem("abs_ready")
        softplus_ready = sem("softplus_ready")
        logf_ready = sem("logf_ready")
        cum_ready = sem("cum_ready")
        q_zeroed = sem("q_zeroed")
        conv_hist_loaded = sem("conv_hist_loaded")
        conv_norm_loaded = sem("conv_norm_loaded")
        u_stored = sem("u_stored")
        kv_stored = sem("kv_stored")
        mkv_stored = sem("mkv_stored")
        pmax_ready = sem("pmax_ready")
        smax_ready = sem("smax_ready")
        sexp_ready = sem("sexp_ready")
        conv_done = sem("conv_done")
        zvar_ready = sem("zvar_ready")
        zstd_ready = sem("zstd_ready")
        znorm_ready = sem("znorm_ready")
        oconv_ready = sem("oconv_ready")
        oattn_ready = sem("oattn_ready")
        mstd_ready = sem("mstd_ready")
        xmax_ready = sem("xmax_ready")
        silu_ready = sem("silu_ready")
        rmax_ready = sem("rmax_ready")
        rexp_ready = sem("rexp_ready")
        picks_ready = sem("picks_ready")
        items_ready = sem("items_ready")
        e_pick_ready = sem("expert_picks_ready")
        e_silu_ready = sem("expert_silu_ready")
        gfin_loaded = sem("gfin_loaded")
        hist_ready = sem("hist_ready")
        iota_made = sem("iota_made")
        out_ready = sem("out_ready")
        out_stored = sem("out_stored")

        units = []
        for l in range(DEPTH):
            units += [(("w_in", l, g), 1) for g in ("q", "k", "v", "gate", "value")]
            kv = [("K", l, 0), ("K", l, 1)]
            for p in range(1, PAIRS):
                kv += [("K", l, 2 * p), ("K", l, 2 * p + 1), ("V", l, 2 * p - 2), ("V", l, 2 * p - 1)]
            kv += [("V", l, DB - 2), ("V", l, DB - 1)]
            units += [(k, NPG) for k in kv]
            units += [(("w_out", l, g), 1) for g in range(2)]
            units += [(("w_ckv", l, g), 1) for g in range(2)]
            units += [(("w_cq", l), 1)]
            units += [(("mem_kv", l, b), 4) for b in range(0, DB, 2)]
            units += [(("w_co", l), 1)]
            if l % 2 == 0:
                units += [(("ff_up", l, g), 2) for g in range(NFG)]
                units += [(("ff_down", l, k), 1) for k in range((FF // P + 3) // 4)]
        unit_at, landed_at, per_slot = {}, {}, [0] * RING
        for n, (key, dmas) in enumerate(units):
            per_slot[n % RING] += 16 * dmas
            unit_at[key] = n
            landed_at[key] = per_slot[n % RING]

        jobs, per_bank = {}, [0] * 8
        freed_by = {}

        def filled(eng, key):
            bank, n = jobs[key]
            eng.wait_ge(bank_filled[bank], n + 1)
            return bank

        e_plan = [(("take", 0), 6), (("take", 1), 7), (("giveT",), 2)]
        for g in range(NEG_G):
            e_plan.append((("up", g), g % 2))
            if g:
                e_plan.append((("midT", g - 1), 2 + g % 2))
        e_plan += [(("midT", NEG_G - 1), 2 + NEG_G % 2), (("down", 0), 4), (("down", 1), 5)]
        e_plan += [(("give", c, f), (0, 1, 2, 3, 6, 7)[2 * c + f]) for c in range(3) for f in range(2)]
        e_jobs, e_per = {}, [0] * 8
        for key, bank in e_plan:
            e_jobs[key] = (bank, e_per[bank])
            e_per[bank] += 1
        UP_HALVES = 2 * NEG_G
        HALVES = UP_HALVES + EF // 256
        assert HALVES % MOE_RING == 0 and HALVES % SPLIT == 0
        W_READS = NEG_G + EF // 256 - 1
        W_CREDIT = 2

        def e_filled_wait(eng, key, i):
            bank, n = e_jobs[key]
            eng.wait_ge(bank_filled[bank], i * e_per[bank] + (per_bank[bank] + n + 1))
            return bank

        e_bytes, e_done = [0] * MOE_RING, {}
        for m in range(HALVES):
            e_bytes[m % MOE_RING] += 16 * (2 if m < UP_HALVES else 1)
            e_done[m] = e_bytes[m % MOE_RING]
        COLUMN_STEPS = 4

        def half_read_wait(eng, i, m):
            if m < 0:
                i, m = i - 1, m + HALVES
            if m == HALVES - 1:
                e_filled_wait(eng, ("down", 1), i)
            elif m < UP_HALVES and m % 2:
                e_filled_wait(eng, ("up", m // 2), i)
            else:
                eng.wait_ge(w_read, i * W_READS + W_CREDIT + (m // 2 + 1 if m < UP_HALVES else m + 1 - NEG_G))

        g_final = memT[:, 0:KD // 2, :].rearrange("p k t -> p (k t)")
        kv_waits, u_waits = 16 * (2 + 6), 16 * (1 + DB + 1)
        note2 = sb("note2", [P, 1])
        stat_at = {}

        def stat(key, n=1, rows=P):
            if key not in stat_at:
                used = sum(m for _, m in stat_at.values())
                assert used + n <= 512
                stat_at[key] = (used, n)
            at, m = stat_at[key]
            assert m == n
            return stats[0:rows, at:at + n]

        block = ctx.enter_context(nc.Block())

        @block.tensor
        def _(pe):
            used = [0]
            turn = [0]

            def job(key, bank):
                n = per_bank[bank]
                jobs[key] = (bank, n)
                per_bank[bank] = n + 1
                if n:
                    pe.wait_ge(bank_emptied[bank], n)
                return psum[bank]

            def emptied(*keys):
                for key in keys:
                    bank, n = jobs[key]
                    pe.wait_ge(bank_emptied[bank], n + 1)

            def unit(key):
                n = unit_at[key]
                if n == used[0]:
                    used[0] += 1
                    pe.wait_ge(slot_landed[n % RING], landed_at[key])
                assert n < used[0], (key, n, used[0])
                return ring[:, (n % RING) * SLOT:(n % RING + 1) * SLOT]

            def transposes(key, parts):
                turn[0] += 1
                bank = 6 + turn[0] % 2
                ps = job(key, bank)
                at = 0
                for a, rows in parts:
                    last = nc.tensor.transpose(ps[0:a.shape[1], at:at + rows], a, ident[0:rows, 0:rows])
                    at += rows
                last.then_inc(bank_filled[bank], 1)

            def product(out, pairs):
                for n, (a, b) in enumerate(pairs):
                    last = nc.tensor.matmul(out, a, b, start=(n == 0), stop=(n == len(pairs) - 1))
                return last

            def turn_rows(name, src, ready, first, halves=KD // 4):
                for c in range(3):
                    pe.wait_ge(ready, first + c + 1)
                    for f in range(halves):
                        transposes((name, c, f), [(src[0:ROWS[c], c, (4 * f + q) * P:(4 * f + q + 1) * P], ROWS[c])
                                                  for q in range(4)])

            def turn_stage(l, s):
                turn_rows(("hT", l, s), h, h_ready, 3 * STAGE_AT[(l, s)])

            def project(name, key, g, src, n_k, weights, done=True, chunks=range(3), stage=None):
                for c in chunks:
                    bank = 3 * (g % 2) + c
                    if stage and g == 0:
                        emptied(*[(stage, c, f) for f in range(n_k // 4)])
                    ps = job((name, c), bank)
                    last = product(ps[0:ROWS[c], :], [(src[:, k, COLS[c]], weights[:, k, :]) for k in range(n_k)])
                    last.then_inc(bank_filled[bank], 1)

            def last_read(key, job_key):
                freed_by[key] = job_key

            pe.wait_ge(consts_made, 1)
            pe.wait_ge(rows_loaded, 16 * (12 + 4))
            transposes("gains", [(gain_rows[0:DEPTH * N_GAINS, :], DEPTH * N_GAINS)])
            transposes("conv_w", [(dw_rows[:, l, :], P) for l in range(DEPTH)])
            ps = job("masks", 0)
            nc.tensor.matmul(ps[:, 0:2 * NS], spread8, small8[:, :, :, :].rearrange("t a b s -> t (a b s)"),
                             start=True, stop=True).then_inc(bank_filled[0], 1)
            ps = job("suffix", 1)
            pe.wait_ge(decay_made, 1)
            nc.tensor.matmul(ps[:, 0:NH], page_suffix, lf_sum[:, :, PAGE - 1],
                             start=True, stop=True).then_inc(bank_filled[1], 1)
            for c in range(2):
                pe.wait_ge(mem_ready, c + 1)
                for f in range(2):
                    transposes(("memT", c, f), [(mem[:, c, (4 * f + q) * P:(4 * f + q + 1) * P], P) for q in range(4)])
            pe.wait_ge(masks_made, 1)
            pe.wait_ge(decay_loaded, 16 * 2 * DB)

            for l in range(DEPTH):
                turn_stage(l, "mix")
                for g, part in enumerate(("q", "k", "v", "gate", "value")):
                    w = unit(("w_in", l, part)).rearrange("p (k n) -> p k n", k=KD)
                    if part == "value":
                        emptied(*[(("gate", l), c) for c in range(3)])
                    project((part, l), None, g, hT, KD, w, stage=("hT", l, "mix"))
                    last_read(("w_in", l, part), ((part, l), 2))
                    if g == 0:
                        ps = job(("forget", l), 5)
                        for c in range(3):
                            last = product(ps[0:ROWS[c], c * NH:(c + 1) * NH],
                                           [(hT[:, k, COLS[c]], forget_w[:, l, k, :]) for k in range(KD)])
                        last.then_inc(bank_filled[5], 1)

                pe.wait_ge(logf_ready, l + 1)
                ps = job(("cumT", l), 0)
                product(ps[0:NH, 0:P], [(logf[:, 0, :], upto[:, :])])
                product(ps[0:NH, P:2 * P], [(logf[:, 0, :], ones[:, :]), (logf[:, 1, :], upto[:, :])])\
                    .then_inc(bank_filled[0], 1)
                ps = job(("cum_s", l), 1)
                product(ps[0:NS, 0:NH], [(block_upto[:, :], logf[0:NS, 2, :])]).then_inc(bank_filled[1], 1)
                for part, at in (("q", 0), ("k", AW)):
                    for c in range(3):
                        emptied(((part, l), c))
                        if part == "k":
                            emptied((("v", l), c))
                        transposes((part + "T", l, c), [(qkv[0:ROWS[c], c, at + j * P:at + (j + 1) * P], ROWS[c])
                                                        for j in range(4)])
                for c in range(3):
                    emptied((("value", l), c))
                    transposes(("uT", l, c), [(u[0:ROWS[c], c, j * P:(j + 1) * P], ROWS[c]) for j in range(4)])
                pe.wait_ge(conv_hist_loaded, 32 * (l + 1))
                for b in range(2):
                    transposes(("histT", l, b), [(hist_in[0:4 * HIST, b, j * P:(j + 1) * P], 4 * HIST) for j in range(4)])
                pe.wait_ge(cum_ready, l + 1)
                ps = job(("own_cum", l), 2)
                for b2 in range(2):
                    last = product(ps[b2 * NS:(b2 + 1) * NS, 0:PAIRS],
                                   [(cum_rows[:, :, :].rearrange("p h t -> p (h t)"), batch_of[:, b2:DB:2])])
                last.then_inc(bank_filled[2], 1)

                emptied(*[(n, l, c) for n in ("qT", "kT") for c in range(2)], ("cumT", l))
                n = 0
                for i in range(2):
                    keys = (i + 1) * P
                    per = 512 // keys
                    for g in range(NH // per):
                        bank = 3 + n % 3
                        ps = job(("scores", l, i, g), bank)
                        for a in range(per):
                            hd = g * per + a
                            pick = ident[0:NH, hd:hd + 1]
                            last = product(ps[:, a * keys:(a + 1) * keys],
                                           [(q_heads[:, hd, i * P:(i + 1) * P], kT[:, hd // 2, 0:keys]),
                                            (pick.to_broadcast([NH, P]), neg_cumT[:, 0:keys]),
                                            (cumT[:, i * P:(i + 1) * P], pick.to_broadcast([NH, keys]))])
                        last.then_inc(bank_filled[bank], 1)
                        n += 1
                turns = [(i, t) for i in range(2) for t in range(2 * (i + 1))]
                for n in range(len(turns) + 1):
                    if n < len(turns):
                        i, t = turns[n]
                        emptied(("scores", l, i, t))
                        if i == 0:
                            parts = [(p_prompt[0][:, 4 * t + a, :], P) for a in range(4)]
                        else:
                            parts = [(p_prompt[1][:, 2 * t + a, kk * P:(kk + 1) * P], P) for a in range(2) for kk in range(2)]
                        transposes(("pT", l, n), parts)
                    if n:
                        i, t = turns[n - 1]
                        emptied(("pT", l, n - 1))
                        if t == 0:
                            ps = job(("o_prompt", l, i), 1 + i)
                        at = 4 * ((n - 1) % 2)
                        per = 4 // (i + 1)
                        for a in range(per):
                            hd = t * per + a
                            last = product(ps[:, hd * DH:(hd + 1) * DH],
                                           [(PT[:, at + a * (i + 1) + kk, :], qkv[:, kk, 2 * AW + hd * DH:2 * AW + (hd + 1) * DH])
                                            for kk in range(i + 1)])
                        if t == 2 * (i + 1) - 1:
                            last.then_inc(bank_filled[1 + i], 1)

                def key_columns(l, n):
                    b, half = n // 2, n % 2
                    K = unit(("K", l, b)).rearrange("p (g n) -> p g n", g=NPG)
                    for pg in range(4 * half, 4 * half + 4):
                        transposes(("KT", l, b, pg), [(K[:, pg, j * P:(j + 1) * P], P) for j in range(4)])
                    last_read(("K", l, b), ("KT", l, b, NPG - 1))

                def past_scores(l, n):
                    b, half = n // 2, n % 2
                    p, b2 = b // 2, b % 2
                    rows = slice(b2 * NS, (b2 + 1) * NS)
                    if b2 == 0:
                        job(("past", l, p, half), half)
                    emptied(*[("KT", l, b, pg) for pg in range(4 * half, 4 * half + 4)])
                    last = product(psum[half][rows, :],
                                   [(q_rows[:, j, b, :], KT[:, n % 2, j, :]) for j in range(4)]
                                   + [(decay_rows[:, l, b, :],
                                       past_decay[:, half * 512:(half + 1) * 512])])
                    if b2 == 1:
                        last.then_inc(bank_filled[half], 1)

                def new_scores(l, p):
                    ps = job(("new", l, p), 2)
                    for b2 in range(2):
                        last = product(ps[b2 * NS:(b2 + 1) * NS, 0:NS],
                                       [(q_rows[:, j, 2 * p + b2, :], kT[:, j, SEQ:NTOK]) for j in range(4)]
                                       + [(neg_cum_rows[:, :, :].rearrange("p h t -> p (h t)"), ident[0:NS, 0:NS])])
                    last.then_inc(bank_filled[2], 1)

                def probs_columns(l, p):
                    pe.wait_ge(sexp_ready, PAIRS * l + p + 1)
                    for t in range(2):
                        transposes(("PT", l, p, t), [(probs[:, (4 * t + q) * P:(4 * t + q + 1) * P], P) for q in range(4)])
                    transposes(("PT", l, p, 2), [(probs[:, PAST:PAST + NS], P)])

                def weigh_values(l, p):
                    emptied(*[("PT", l, p, t) for t in range(3)])
                    ps = job(("o_pair", l, p), 3)
                    for b2 in range(2):
                        V = unit(("V", l, 2 * p + b2)).rearrange("p (g n) -> p g n", g=NPG)
                        rows = slice(b2 * NS, (b2 + 1) * NS)
                        last = product(ps[rows, :], [(PT[:, pg, rows], V[:, pg, :]) for pg in range(NPG)]
                                       + [(PT[0:NS, 8, rows], qkv[0:NS, 2, 2 * AW:3 * AW])])
                        if b2 == 1:
                            last.then_inc(bank_filled[3], 1)
                        last_read(("V", l, 2 * p + b2), ("o_pair", l, p))

                def gather_rows(l, p):
                    emptied(("o_pair", l, p))
                    if p == 0:
                        job(("o_sample", l), 4)
                    last = nc.tensor.matmul(psum[4][0:NS, :], pair_rows[:, p, :], o_masked[:, :],
                                            start=(p == 0), stop=(p == PAIRS - 1))
                    if p == PAIRS - 1:
                        last.then_inc(bank_filled[4], 1)

                emptied(("qT", l, 2), ("kT", l, 2))
                key_columns(l, 0)
                for p in range(PAIRS + 1):
                    if p < PAIRS:
                        for n in range(4 * p, 4 * p + 4):
                            if n % 4 == 2:
                                if p:
                                    probs_columns(l, p - 1)
                                new_scores(l, p)
                            if n + 1 < 4 * p + 4:
                                key_columns(l, n + 1)
                            past_scores(l, n)
                        if p + 1 < PAIRS and p == 0:
                            key_columns(l, 4)
                    else:
                        probs_columns(l, p - 1)
                    if p:
                        if p >= 2:
                            gather_rows(l, p - 2)
                        weigh_values(l, p - 1)
                        if p + 1 < PAIRS:
                            key_columns(l, 4 * (p + 1))
                gather_rows(l, PAIRS - 1)

                pe.wait_ge(conv_done, l + 1)
                for c in range(3):
                    turn[0] += 1
                    bank = 6 + turn[0] % 2
                    ps = job(("z", l, c), bank)
                    for j in range(4):
                        last = nc.tensor.transpose(ps[0:ROWS[c], j * P:(j + 1) * P], conv_z[:, j, COLS[c]], ident[:, :])
                    last.then_inc(bank_filled[bank], 1)
                turn_stage(l, "merged")
                for g in range(2):
                    w = unit(("w_out", l, g)).rearrange("p (k n) -> p k n", k=KD)
                    project(("out", l, g), None, g, hT, KD, w, stage=("hT", l, "merged"))
                    last_read(("w_out", l, g), (("out", l, g), 2))

                pe.wait_ge(mem_g_ready, l + 1)
                for g in range(2):
                    w = unit(("w_ckv", l, g)).rearrange("p (k n) -> p k n", k=KD)
                    project(("mkv", l, g), None, g, mem_g, KD, w, chunks=range(2))
                    last_read(("w_ckv", l, g), (("mkv", l, g), 1))
                turn_stage(l, "cross")
                w = unit(("w_cq", l)).rearrange("p (k n) -> p k n", k=KD)
                project(("xq", l), None, 0, hT, KD, w, stage=("hT", l, "cross"))
                last_read(("w_cq", l), (("xq", l), 2))
                for m in range(2):
                    emptied((("mkv", l, 0), m), (("mkv", l, 1), m))
                    transposes(("mkT", l, m), [(mkv[:, m, j * P:(j + 1) * P], P) for j in range(XH)])
                for c in range(3):
                    emptied((("xq", l), c))
                    transposes(("xqT", l, c), [(xq[0:ROWS[c], c, j * P:(j + 1) * P], ROWS[c]) for j in range(XH)])

                def memory_columns(l, b):
                    kv = unit(("mem_kv", l, b - b % 2)).rearrange("p (s n) -> p s n", s=8)
                    for m in range(2):
                        transposes(("xKT", l, b, m), [(kv[:, 4 * (b % 2) + m, j * P:(j + 1) * P], P) for j in range(XH)])

                memory_columns(l, 0)
                emptied(("xqT", l, 2))
                for b in range(DB):
                    if b + 1 < DB:
                        memory_columns(l, b + 1)
                    quad, b4 = b // 4, b % 4
                    if b4 == 0:
                        job(("xs", l, quad), quad)
                    emptied(("xKT", l, b, 0), ("xKT", l, b, 1))
                    last = product(psum[quad][32 * b4:32 * b4 + 32, 0:NMEM],
                                   [(xq_rows[:, j, b, :], xKT[:, b % 2, j, :]) for j in range(XH)])
                    if b4 == 3:
                        last.then_inc(bank_filled[quad], 1)
                emptied(("xqT", l, 0), ("xqT", l, 1), ("mkT", l, 0), ("mkT", l, 1))
                for i in range(2):
                    for g in range(2):
                        bank = 2 + (2 * i + g) % 4
                        ps = job(("xscores", l, i, g), bank)
                        for a in range(2):
                            last = product(ps[:, a * NMEM:(a + 1) * NMEM],
                                           [(xqT[:, 2 * g + a, i * P:(i + 1) * P], mkT[:, 2 * g + a, :])])
                        last.then_inc(bank_filled[bank], 1)
                for quad in range(QUADS):
                    emptied(("xs", l, quad))
                    transposes(("xPT", l, quad), [(xp[:, quad, m * P:(m + 1) * P], P) for m in range(2)])
                for b in range(DB):
                    quad, b4 = b // 4, b % 4
                    if b4 == 0:
                        emptied(("xPT", l, quad))
                        job(("xo_quad", l, quad), quad)
                    if b % 2 == 0:
                        kv = unit(("mem_kv", l, b)).rearrange("p (s n) -> p s n", s=8)
                    last = product(psum[quad][32 * b4:32 * b4 + 32, :],
                                   [(xPT[:, quad, m, 32 * b4:32 * b4 + 32], kv[:, 4 * (b % 2) + 2 + m, :]) for m in range(2)])
                    if b4 == 3:
                        last.then_inc(bank_filled[quad], 1)
                    last_read(("mem_kv", l, b - b % 2), ("xo_quad", l, quad))
                for n in range(5):
                    if n < 4:
                        i, g = n // 2, n % 2
                        emptied(("xscores", l, i, g))
                        transposes(("xpT", l, n), [(xp_prompt[:, i, 2 * g + a, m * P:(m + 1) * P], P)
                                                   for a in range(2) for m in range(2)])
                    if n:
                        i, g = (n - 1) // 2, (n - 1) % 2
                        emptied(("xpT", l, n - 1), (("mkv", l, 1), 0), (("mkv", l, 1), 1))
                        if g == 0:
                            ps = job(("xo_prompt", l, i), 2 + i)
                        for a in range(2):
                            hd = 2 * g + a
                            last = product(ps[:, hd * P:(hd + 1) * P],
                                           [(xPT[:, 2 + (n - 1) % 2, 2 * a + m, :], mkv[:, m, XW + hd * P:XW + (hd + 1) * P])
                                            for m in range(2)])
                        if g == 1:
                            last.then_inc(bank_filled[2 + i], 1)
                job(("xo_sample", l), 4)
                emptied(("xo_quad", l, 0), ("xo_quad", l, 1))
                product(psum[4][0:NS, :], [(quad_rows[:, q, :], xo_masked[:, q, :]) for q in range(QUADS)])\
                    .then_inc(bank_filled[4], 1)
                for c in range(3):
                    emptied(("xo_prompt", l, c) if c < 2 else ("xo_sample", l))
                    transposes(("xoT", l, c), [(xo[0:ROWS[c], c, j * P:(j + 1) * P], ROWS[c]) for j in range(XH)])
                w = unit(("w_co", l)).rearrange("p (k n) -> p k n", k=XH)
                emptied(*[("xoT", l, c) for c in range(3)])
                for g in range(2):
                    project(("co", l, g), None, g, hT, XH, w[:, :, g * 512:(g + 1) * 512])
                last_read(("w_co", l), (("co", l, 1), 2))

                turn_stage(l, "ffn")
                if l % 2 == 0:
                    for g in range(NFG + 1):
                        if g < NFG:
                            w = unit(("ff_up", l, g)).rearrange("p (k n) -> p k n", k=KD)
                            project(("ff", l, g), None, g, hT, KD, w, stage=("hT", l, "ffn"))
                            last_read(("ff_up", l, g), (("ff", l, g), 2))
                        if g:
                            for c in range(3):
                                emptied((("ff", l, g - 1), c))
                                transposes(("ffT", l, g - 1, c),
                                           [(mid[0:ROWS[c], (g - 1) % 2, c, j * P:(j + 1) * P], ROWS[c]) for j in range(2)])
                    for c in range(3):
                        for f in range(2):
                            job(("ff_out", l, c, f), 2 * c + f)
                    NK = FF // P
                    for k in range(NK):
                        if k % 4 == 0:
                            w = unit(("ff_down", l, k // 4)).rearrange("p (k n) -> p k n", k=4)
                        if k % 2 == 0:
                            emptied(*[("ffT", l, k // 2, c) for c in range(3)])
                        for c in range(3):
                            for f in range(2):
                                last = nc.tensor.matmul(psum[2 * c + f][0:ROWS[c], :], midT[:, k, COLS[c]],
                                                        w[:, k % 4, f * 512:(f + 1) * 512], start=(k == 0), stop=(k == NK - 1))
                                if k == NK - 1:
                                    last.then_inc(bank_filled[2 * c + f], 1)
                        if k == NK - 1:
                            last_read(("ff_down", l, k // 4), ("ff_out", l, 2, 1))
                        elif k % 4 == 3:
                            last.then_inc(down_read, 1)
                            freed_by[("ff_down", l, k // 4)] = k // 4 + 1
                    continue

                emptied(*[(("hT", l, "ffn"), c, f) for c in range(3) for f in range(2)])
                ps = job("router", 0)
                for c in range(3):
                    last = product(ps[0:ROWS[c], c * NE:(c + 1) * NE],
                                   [(hT[:, k, COLS[c]], router_w[:, k, :]) for k in range(KD)])
                    if c < W_CREDIT:
                        last.then_inc(w_read, 1)
                last.then_inc(bank_filled[0], 1)
                pe.wait_ge(picks_ready, 1)
                chosen = route[5]
                ps = job("ranks", 1)
                for c in range(3):
                    last = product(ps[:, c * NE:(c + 1) * NE],
                                   [(ones[:, :], chosen[:, c2, :]) for c2 in range(c)] + [(before[:, :], chosen[:, c, :])])
                last = product(ps[:, 3 * NE:4 * NE], [(ones[:, :], chosen[:, c, :]) for c in range(3)])
                last.then_inc(bank_filled[1], 1)

            pe.wait_ge(items_ready, 1)
            n_items = pe.value_load(items[0:1, 0:1], min_val=NE, max_val=MAX_ITEMS)
            with pe.Fori(0, n_items) as i:
                def e_job(key):
                    bank, n = e_jobs[key]
                    pe.wait_ge(bank_emptied[bank], i * e_per[bank] + (per_bank[bank] + n))
                    return psum[bank]

                def e_emptied_wait(key):
                    bank, n = e_jobs[key]
                    pe.wait_ge(bank_emptied[bank], i * e_per[bank] + (per_bank[bank] + n + 1))

                def split_half(m, n):
                    for s in w_lo_made:
                        pe.wait_ge(s, i * HALVES + (m + 1))
                    return [t[m % SPLIT][:, :].rearrange("p (k n) -> p k n", k=n) for t in (w_hi, w_lo)]

                def split_product(out, a_hi, a_lo, b_hi, b_lo, start, stop):
                    nc.tensor.matmul(out, a_hi, b_hi, start=start, stop=False)
                    nc.tensor.matmul(out, a_hi, b_lo, start=False, stop=False)
                    return nc.tensor.matmul(out, a_lo, b_hi, start=False, stop=stop)

                pe.wait_ge(e_pick_ready, i + 1)
                for f in range(2):
                    ps = e_job(("take", f))
                    for q in range(4):
                        k = 4 * f + q
                        last = product(ps[:, q * P:(q + 1) * P],
                                       [(h[0:ROWS[c], c, k * P:(k + 1) * P], e_pick[0:ROWS[c], c, :]) for c in range(3)])
                    last.then_inc(bank_filled[6 + f], 1)
                ps = e_job(("giveT",))
                for c in range(3):
                    last = nc.tensor.transpose(ps[:, c * P:c * P + ROWS[c]], e_give[0:ROWS[c], c, :], ident[0:ROWS[c], 0:ROWS[c]])
                last.then_inc(bank_filled[2], 1)
                pe.wait_ge(xT_ready, i + 1)
                for g in range(NEG_G + 1):
                    if g < NEG_G:
                        ps = e_job(("up", g))
                        for half in range(2):
                            hi, lo = split_half(2 * g + half, 4)
                            for q in range(4):
                                k = 4 * half + q
                                last = split_product(ps[:, :], e_xT_hi[:, k, :], e_xT_lo[:, k, :], hi[:, q, :], lo[:, q, :],
                                                     k == 0, k == KD - 1)
                            last.then_inc(bank_filled[g % 2] if half else w_read, 1)
                    if g:
                        e_emptied_wait(("up", g - 1))
                        ps = e_job(("midT", g - 1))
                        for j in range(2):
                            last = nc.tensor.transpose(ps[:, j * P:(j + 1) * P], e_mid[:, (g - 1) % 2, j * P:(j + 1) * P], ident[:, :])
                        last.then_inc(bank_filled[e_jobs[("midT", g - 1)][0]], 1)
                e_job(("down", 0))
                e_job(("down", 1))
                for m in range(UP_HALVES, HALVES):
                    hi, lo = split_half(m, 2)
                    e_emptied_wait(("midT", m - UP_HALVES))
                    for q in range(2):
                        k = 2 * (m - UP_HALVES) + q
                        for f in range(2):
                            cols = slice(f * 512, (f + 1) * 512)
                            last = split_product(psum[4 + f][:, :], e_midT_hi[:, k, :], e_midT_lo[:, k, :],
                                                 hi[:, q, cols], lo[:, q, cols], k == 0, k == EF // P - 1)
                            if k == EF // P - 1:
                                last.then_inc(bank_filled[4 + f], 1)
                    if m < HALVES - 1:
                        last.then_inc(w_read, 1)
                e_emptied_wait(("giveT",))
                for f in range(2):
                    e_emptied_wait(("down", f))
                    for c in range(3):
                        ps = e_job(("give", c, f))
                        nc.tensor.matmul(ps[0:ROWS[c], :], e_giveT[:, c, 0:ROWS[c]], e_y[:, f, :], start=True, stop=True)\
                            .then_inc(bank_filled[e_jobs[("give", c, f)][0]], 1)


        @block.vector
        def _(dve):
            steps, told = [0], [0]

            def mark(ins):
                steps[0] += 1
                ins.then_inc(vector_step, 1)
                return steps[0]

            def link(ins):
                dve.wait_ge(vector_step, mark(ins))

            def tell(s):
                told[0] += 1
                nc.vector.memset(note[:, told[0] % 16:told[0] % 16 + 1], 0.0).then_inc(s, 1)

            V = nc.vector

            def wide(a, *shape):
                return a.unsqueeze(2).to_broadcast(list(shape))

            dve.wait_ge(idx_loaded, 32)
            V.tensor_scalar(page_idx[NS:P, :], page_idx[NS:P, :], float(N_PHYS), None, ALU.add).then_inc(idx_ready, 1)
            dve.wait_ge(consts_made, 1)
            V.tensor_reduce(step_of[:, :], ident[0:NS, 0:NS].rearrange("p (b t) -> p t b", b=DB), AX.X, ALU.add)
            V.tensor_reduce(batch_of[:, :], ident[0:NS, 0:NS].rearrange("p (b t) -> p b t", b=DB), AX.X, ALU.add)
            bank = filled(dve, "gains")
            V.tensor_copy(gains[:, :], psum[bank][:, 0:DEPTH * N_GAINS]).then_inc(bank_emptied[bank], 1)
            bank = filled(dve, "conv_w")
            V.tensor_copy(conv_w[:, :, :], psum[bank][:, 0:DEPTH * P].rearrange("p (l r) -> p l r", l=DEPTH))\
                .then_inc(bank_emptied[bank], 1)
            bank = filled(dve, "masks")
            V.tensor_copy(new_mask[:, :, :], psum[bank][:, 0:NS].unsqueeze(1).to_broadcast([P, PAIRS, NS]))
            V.tensor_copy(pair_rows[:, :, :], psum[bank][:, NS:2 * NS].unsqueeze(1).to_broadcast([P, PAIRS, NS]))
            V.tensor_copy(quad_rows[:, :, :], psum[bank][:, NS:2 * NS].unsqueeze(1).to_broadcast([P, QUADS, NS]))\
                .then_inc(bank_emptied[bank], 1)
            tell(masks_spread)
            dve.wait_ge(pages_gathered, 16)
            for hd in range(NH):
                V.tensor_tensor_scan(lf_sum[:, hd, :], ones[:, :], lf_pages[:, :, hd], 0.0, ALU.mult, ALU.add)
            tell(decay_made)
            bank = filled(dve, "suffix")
            suffix = stat("suffix", NH)
            link(V.tensor_copy(suffix, psum[bank][:, 0:NH]))
            V.tensor_tensor(lf_decay[:, :, :], wide(suffix, P, NH, PAGE), lf_sum[:, :, :], ALU.subtract)\
                .then_inc(bank_emptied[bank], 1)
            tell(decay_made)
            for c in range(2):
                dve.wait_ge(mem_std, c + 1)
                link(V.reciprocal(stat(("mem_rstd", c)), stat(("mem_std", c))))
                V.tensor_scalar(mem[:, c, :], mem[:, c, :], stat(("mem_rstd", c)), None, ALU.mult).then_inc(mem_ready, 1)

            def norm_rows(l, s):
                n = NORM_AT[(l, s)]
                for c in range(3):
                    r = ROWS[c]
                    dve.wait_ge(std_ready, 3 * n + c + 1)
                    link(V.reciprocal(stat(("rstd", n, c), rows=r), stat(("std", n, c), rows=r)))
                    V.tensor_scalar(h[0:r, c, :], x[0:r, c, :], stat(("rstd", n, c), rows=r), None, ALU.mult)\
                        .then_inc(h_ready, 1)
                gained_columns(l, s)

            def gained_columns(l, s):
                g0 = l * N_GAINS + GAIN_AT[s]
                for c in range(3):
                    for f in range(2):
                        bank = filled(dve, (("hT", l, s), c, f))
                        V.tensor_tensor(hT[:, 4 * f:4 * f + 4, COLS[c]],
                                        psum[bank][:, 0:4 * ROWS[c]].rearrange("p (k t) -> p k t", k=4),
                                        wide(gains[:, g0 + 4 * f:g0 + 4 * f + 4], P, 4, ROWS[c]), ALU.mult)\
                            .then_inc(bank_emptied[bank], 1)

            def add_to_x(key, c, f):
                bank = filled(dve, key)
                r = ROWS[c]
                xs = x[0:r, c, f * 512:(f + 1) * 512]
                V.tensor_tensor(xs, xs, psum[bank][0:r, :], ALU.add).then_inc(bank_emptied[bank], 1)

            for l in range(DEPTH):
                norm_rows(l, "mix")
                for c in range(3):
                    bank = filled(dve, (("q", l), c))
                    V.tensor_scalar(qkv[0:ROWS[c], c, 0:AW], psum[bank][0:ROWS[c], :], Q_SCALE, None, ALU.mult)\
                        .then_inc(bank_emptied[bank], 1)
                bank = filled(dve, ("forget", l))
                parts = [(P, slice(0, 2), 2), (NS, slice(2, 3), 1)]
                for r, cs, n in parts:
                    pf = psum[bank][0:r, 0:3 * NH].rearrange("p (c n) -> p c n", c=3)[:, cs, :]
                    bias = forget_b[0:r, l, :].unsqueeze(1).to_broadcast([r, n, NH])
                    link(V.tensor_tensor(logf[0:r, cs, :], pf, bias, ALU.add))
                    last = V.scalar_tensor_tensor(out=log_tmp[0:r, 0, cs, :], in0=logf[0:r, cs, :], scalar=-1.0,
                                                  in1=logf[0:r, cs, :], op0=ALU.mult, op1=ALU.max)
                last.then_inc(bank_emptied[bank], 1)
                tell(abs_ready)
                dve.wait_ge(softplus_ready, l + 1)
                for r, cs, n in parts:
                    last = V.scalar_tensor_tensor(out=logf[0:r, cs, :], in0=logf[0:r, cs, :], scalar=0.0,
                                                  in1=log_tmp[0:r, 1, cs, :], op0=ALU.min, op1=ALU.subtract)
                last.then_inc(logf_ready, 1)
                for c in range(3):
                    bank = filled(dve, (("value", l), c))
                    uc = u[0:ROWS[c], c, :]
                    V.tensor_tensor(uc, psum[bank][0:ROWS[c], :], uc, ALU.mult).then_inc(bank_emptied[bank], 1)
                bank = filled(dve, ("cumT", l))
                V.tensor_copy(cumT[:, :], psum[bank][0:NH, 0:SEQ])
                V.tensor_scalar(neg_cumT[:, :], psum[bank][0:NH, 0:SEQ], -1.0, None, ALU.mult).then_inc(bank_emptied[bank], 1)
                bank = filled(dve, ("cum_s", l))
                link(V.tensor_copy(cum_s[:, :], psum[bank][0:NS, 0:NH]))
                V.tensor_tensor(cum_rows[:, :, :], wide(cum_s[:, :], NS, NH, DS),
                                step_of[:, :].unsqueeze(1).to_broadcast([NS, NH, DS]), ALU.mult)
                V.tensor_scalar(neg_cum_rows[:, :, :], wide(cum_s[:, :], NS, NH, DS), -1.0, None, ALU.mult)\
                    .then_inc(bank_emptied[bank], 1)
                tell(cum_ready)
                dve.wait_ge(q_zeroed, 2 * l + 1)
                for c in range(2):
                    bank = filled(dve, ("qT", l, c))
                    src = psum[bank][:, :].rearrange("p (j t) -> p j t", j=4)
                    dst = q_heads.rearrange("p (j two) t -> p j two t", two=2)
                    V.tensor_copy(dst[0:64, :, 0, COLS[c]], src[0:64, :, :])
                    V.tensor_copy(dst[64:P, :, 1, COLS[c]], src[64:P, :, :]).then_inc(bank_emptied[bank], 1)
                bank = filled(dve, ("qT", l, 2))
                for j in range(4):
                    for a in range(2):
                        hd = 2 * j + a
                        last = V.tensor_copy(q_rows[64 * a:64 * a + 64, j, :, hd * DS:(hd + 1) * DS],
                                             psum[bank][64 * a:64 * a + 64, j * NS:(j + 1) * NS]
                                             .rearrange("p (b t) -> p b t", b=DB))
                last.then_inc(bank_emptied[bank], 1)
                for c in range(2):
                    bank = filled(dve, ("uT", l, c))
                    V.tensor_copy(up[:, :, HIST + c * P:HIST + (c + 1) * P],
                                  psum[bank][:, :].rearrange("p (j t) -> p j t", j=4)).then_inc(bank_emptied[bank], 1)
                bank = filled(dve, ("uT", l, 2))
                for j in range(4):
                    last = V.tensor_copy(us[:, j, :, HIST:HIST + DS],
                                         psum[bank][:, j * NS:(j + 1) * NS].rearrange("p (b t) -> p b t", b=DB))
                last.then_inc(bank_emptied[bank], 1)
                bank = filled(dve, ("own_cum", l))
                V.tensor_copy(own_cum[:, :], psum[bank][:, 0:PAIRS]).then_inc(bank_emptied[bank], 1)

                for i in range(2):
                    keys = (i + 1) * P
                    per = 512 // keys
                    for g in range(NH // per):
                        bank = filled(dve, ("scores", l, i, g))
                        s3 = psum[bank][:, :].rearrange("p (a k) -> p a k", a=per)
                        own = s3[:, :, i * P:(i + 1) * P]
                        link(V.tensor_tensor(own, own, causal[:, :].unsqueeze(1).to_broadcast([P, per, P]), ALU.add))
                        top = stat(("pmax", l, i, g), per)
                        link(V.tensor_reduce(top, s3, AX.X, ALU.max))
                        V.tensor_scalar(stat(("pbias", l, i, g), per), top, -1.0, None, ALU.mult).then_inc(pmax_ready, 1)
                for i in range(2):
                    bank = filled(dve, ("o_prompt", l, i))
                    per = 4 // (i + 1)
                    for g in range(NH // per):
                        last = V.reciprocal(stat(("pinv", l, i), NH)[:, g * per:(g + 1) * per], stat(("psum", l, i, g), per))
                    link(last)
                    V.tensor_tensor(h[:, i, 0:AW].rearrange("p (a k) -> p a k", a=NH),
                                    psum[bank][:, :].rearrange("p (a k) -> p a k", a=NH),
                                    wide(stat(("pinv", l, i), NH), P, NH, DH), ALU.mult).then_inc(bank_emptied[bank], 1)
                tell(oattn_ready)

                def taps(first, end):
                    if first == 0:
                        bank = filled(dve, ("histT", l, 1))
                        dve.wait_ge(hist_ready, l + 1)
                    for tap in range(first, end):
                        for j in range(4):
                            w = conv_w[:, l, 4 * tap + j:4 * tap + j + 1]
                            for src, dst in ((up[:, j, tap:tap + SEQ], conv_z[:, j, 0:SEQ]),
                                             (us[:, j, :, tap:tap + DS],
                                              conv_z[:, j, SEQ:NTOK].rearrange("p (b t) -> p b t", b=DB))):
                                if tap == 0:
                                    mark(V.tensor_scalar(dst, src, w, conv_w[:, l, 4 * CONV_K + j:4 * CONV_K + j + 1],
                                                         ALU.mult, ALU.add))
                                else:
                                    dve.wait_ge(vector_step, steps[0] - 7)
                                    mark(V.scalar_tensor_tensor(out=dst, in0=src, scalar=w, in1=dst,
                                                                op0=ALU.mult, op1=ALU.add))
                    if end == CONV_K:
                        tell(conv_done)

                cuts = [0, 5, 10, 14, 18, 21, 24, 28, 31]

                def row_maxima(p):
                    top = stat(("smax", l, p), 3)
                    for half in range(2):
                        bank = filled(dve, ("past", l, p, half))
                        V.tensor_reduce(top[:, half:half + 1], psum[bank][:, :], AX.X, ALU.max)
                    bank = filled(dve, ("new", l, p))
                    link(V.tensor_tensor(probs[:, PAST:PAST + NS], psum[bank][:, 0:NS], new_mask[:, p, :], ALU.add))
                    link(V.tensor_reduce(top[:, 2:3], probs[:, PAST:PAST + NS], AX.X, ALU.max))
                    m = stat(("stop", l, p), 2)
                    link(V.tensor_reduce(m[:, 0:1], top, AX.X, ALU.max))
                    link(V.tensor_tensor(m[:, 1:2], m[:, 0:1], own_cum[:, p:p + 1], ALU.add))
                    V.tensor_tensor(stat(("sbias", l, p)), own_cum[:, p:p + 1], m[:, 1:2], ALU.subtract)\
                        .then_inc(bank_emptied[bank], 1)
                    tell(smax_ready)

                def own_heads(p):
                    dve.wait_ge(sexp_ready, PAIRS * l + p + 1)
                    link(V.tensor_reduce(stat(("ssum1", l, p)), stat(("ssum", l, p), 3), AX.X, ALU.add))
                    link(V.reciprocal(stat(("sinv", l, p)), stat(("ssum1", l, p))))
                    bank = filled(dve, ("o_pair", l, p))
                    V.scalar_tensor_tensor(out=o_masked.rearrange("p (a k) -> p a k", a=NH),
                                           in0=psum[bank][:, :].rearrange("p (a k) -> p a k", a=NH),
                                           scalar=stat(("sinv", l, p)), in1=wide(own_head[:, :], P, NH, DH),
                                           op0=ALU.mult, op1=ALU.mult).then_inc(bank_emptied[bank], 1)

                for p in range(PAIRS + 1):
                    if p < PAIRS:
                        taps(cuts[2 * p], cuts[2 * p + 1])
                        row_maxima(p)
                        taps(cuts[2 * p + 1], cuts[2 * p + 2])
                    if p:
                        own_heads(p - 1)
                bank = filled(dve, ("o_sample", l))
                V.tensor_copy(h[0:NS, 2, 0:AW], psum[bank][0:NS, :]).then_inc(bank_emptied[bank], 1)
                tell(oattn_ready)

                for c in range(3):
                    r = ROWS[c]
                    bank = filled(dve, ("z", l, c))
                    link(V.bn_stats(stat(("zst", l, c), 6, r), psum[bank][0:r, :]))
                    V.bn_aggr(stat(("zmv", l, c), 2, r), stat(("zst", l, c), 6, r)).then_inc(zvar_ready, 1)
                    dve.wait_ge(zstd_ready, 3 * l + c + 1)
                    dve.wait_ge(u_stored, u_waits * (l + 1))
                    dve.wait_ge(conv_norm_loaded, 32 * (l + 1))
                    link(V.reciprocal(stat(("zrs", l, c), rows=r), stat(("zstd", l, c), rows=r)))
                    zt = u[0:r, c, :]
                    link(V.tensor_scalar(zt, psum[bank][0:r, :], stat(("zmv", l, c), 2, r)[:, 0:1],
                                         stat(("zrs", l, c), rows=r), ALU.subtract, ALU.mult))
                    link(V.tensor_tensor(zt, zt, conv_norm[0:r, 0, :], ALU.mult))
                    V.tensor_tensor(zt, zt, conv_norm[0:r, 1, :], ALU.add).then_inc(bank_emptied[bank], 1)
                    tell(znorm_ready)
                for c in range(3):
                    r = ROWS[c]
                    dve.wait_ge(mstd_ready, 3 * l + c + 1)
                    link(V.reciprocal(stat(("mrs", l, c), 2, r), stat(("mstd", l, c), 2, r)))
                    for f in range(2):
                        part = h[0:r, c, f * 512:(f + 1) * 512]
                        last = V.tensor_scalar(part, part, stat(("mrs", l, c), 2, r)[:, f:f + 1], None, ALU.mult)
                    last.then_inc(h_ready, 1)
                gained_columns(l, "merged")
                dve.wait_ge(kv_stored, kv_waits * (l + 1))
                g0 = l * N_GAINS + GAIN_AT["mem"]
                V.tensor_tensor(mem_g, memT[:, :, :], wide(gains[:, g0:g0 + KD], P, KD, NMEM), ALU.mult)\
                    .then_inc(mem_g_ready, 1)
                for g in range(2):
                    for c in range(3):
                        add_to_x((("out", l, g), c), c, g)
                        if g == 1:
                            tell(x_ready)
                norm_rows(l, "cross")
                for c in range(2):
                    bank = filled(dve, (("xq", l), c))
                    V.tensor_copy(xq[:, c, :], psum[bank][:, :]).then_inc(bank_emptied[bank], 1)
                bank = filled(dve, (("xq", l), 2))
                V.tensor_copy(xq[0:NS, 2, :], psum[bank][0:NS, :]).then_inc(bank_emptied[bank], 1)
                for c in range(2):
                    bank = filled(dve, ("xqT", l, c))
                    V.tensor_copy(xqT[:, :, COLS[c]], psum[bank][:, :].rearrange("p (j t) -> p j t", j=XH))\
                        .then_inc(bank_emptied[bank], 1)
                dve.wait_ge(q_zeroed, 2 * l + 2)
                bank = filled(dve, ("xqT", l, 2))
                for j in range(XH):
                    last = V.tensor_copy(xq_rows[:, j, :, j * DS:(j + 1) * DS],
                                         psum[bank][:, j * NS:(j + 1) * NS].rearrange("p (b t) -> p b t", b=DB))
                last.then_inc(bank_emptied[bank], 1)
                for quad in range(QUADS):
                    bank = filled(dve, ("xs", l, quad))
                    link(V.tensor_reduce(stat(("xmax", l, quad)), psum[bank][:, 0:NMEM], AX.X, ALU.max))
                    V.tensor_scalar(stat(("xbias", l, quad)), stat(("xmax", l, quad)), -X_SCALE, None, ALU.mult)\
                        .then_inc(xmax_ready, 1)
                for i in range(2):
                    for g in range(2):
                        bank = filled(dve, ("xscores", l, i, g))
                        link(V.tensor_reduce(stat(("xpmax", l, i, g), 2), psum[bank][:, :].rearrange("p (a k) -> p a k", a=2),
                                             AX.X, ALU.max))
                        V.tensor_scalar(stat(("xpbias", l, i, g), 2), stat(("xpmax", l, i, g), 2), -X_SCALE, None, ALU.mult)\
                            .then_inc(xmax_ready, 1)
                for quad in range(QUADS):
                    bank = filled(dve, ("xo_quad", l, quad))
                    link(V.reciprocal(stat(("xinv", l, quad)), stat(("xsum", l, quad))))
                    V.scalar_tensor_tensor(out=xo_masked[:, quad, :].rearrange("p (a k) -> p a k", a=XH),
                                           in0=psum[bank][:, :].rearrange("p (a k) -> p a k", a=XH),
                                           scalar=stat(("xinv", l, quad)), in1=wide(own_xhead[:, :], P, XH, P),
                                           op0=ALU.mult, op1=ALU.mult).then_inc(bank_emptied[bank], 1)
                for i in range(2):
                    bank = filled(dve, ("xo_prompt", l, i))
                    link(V.reciprocal(stat(("xpinv", l, i), XH), stat(("xpsum", l, i), XH)))
                    V.tensor_tensor(xo[:, i, :].rearrange("p (a k) -> p a k", a=XH),
                                    psum[bank][:, :].rearrange("p (a k) -> p a k", a=XH),
                                    wide(stat(("xpinv", l, i), XH), P, XH, P), ALU.mult).then_inc(bank_emptied[bank], 1)
                bank = filled(dve, ("xo_sample", l))
                V.tensor_copy(xo[0:NS, 2, :], psum[bank][0:NS, :]).then_inc(bank_emptied[bank], 1)
                for g in range(2):
                    for c in range(3):
                        add_to_x((("co", l, g), c), c, g)
                        if g == 1:
                            tell(x_ready)
                norm_rows(l, "ffn")
                if l % 2 == 0:
                    dve.wait_ge(mkv_stored, 32 * (l + 1))
                    for g in range(NFG + 1):
                        if g < NFG:
                            for c in range(3):
                                r = ROWS[c]
                                bank = filled(dve, (("ff", l, g), c))
                                dve.wait_ge(silu_ready, 3 * g + c + 1)
                                V.tensor_tensor(mid[0:r, g % 2, c, :], silu[0:r, g % 2, c, :], psum[bank][0:r, 256:512],
                                                ALU.mult).then_inc(bank_emptied[bank], 1)
                        if g:
                            for c in range(3):
                                bank = filled(dve, ("ffT", l, g - 1, c))
                                V.tensor_copy(midT[:, 2 * g - 2:2 * g, COLS[c]],
                                              psum[bank][:, 0:2 * ROWS[c]].rearrange("p (j t) -> p j t", j=2))\
                                    .then_inc(bank_emptied[bank], 1)
                    for c in range(3):
                        for f in range(2):
                            add_to_x(("ff_out", l, c, f), c, f)
                        tell(x_ready)
                    continue

                prob, eq, cand, first, second, chosen, gate, left, ranked, top_p, e2, sm = route
                link(V.memset(prob, 0.0))
                bank = filled(dve, "router")
                for r, cs, n in parts:
                    pl = psum[bank][0:r, 0:3 * NE].rearrange("p (c n) -> p c n", c=3)[:, cs, :]
                    last = V.tensor_tensor(prob[0:r, cs, :], pl, router_b[0:r, :].unsqueeze(1).to_broadcast([r, n, NE]), ALU.add)
                link(last)
                m3 = stat("rmax", 3)
                link(V.tensor_reduce(m3, prob, AX.X, ALU.max))
                V.tensor_tensor(prob, prob, wide(m3, P, 3, NE), ALU.subtract).then_inc(bank_emptied[bank], 1)
                tell(rmax_ready)
                dve.wait_ge(rexp_ready, 1)
                link(V.tensor_reduce(stat("rsum", 3), prob, AX.X, ALU.add))
                link(V.reciprocal(stat("rinv", 3), stat("rsum", 3)))
                link(V.tensor_tensor(prob, prob, wide(stat("rinv", 3), P, 3, NE), ALU.mult))
                ids = iota8[:, :].unsqueeze(1).to_broadcast([P, 3, NE])

                def largest(src, out, name):
                    top = stat("top" + name, 3)
                    at = stat("at" + name, 3)
                    link(V.tensor_reduce(top, src, AX.X, ALU.max))
                    link(V.tensor_tensor(eq, src, wide(top, P, 3, NE), ALU.is_equal))
                    link(V.tensor_scalar(cand, eq, -float(NE), float(NE), ALU.mult, ALU.add))
                    link(V.tensor_tensor(eq, eq, ids, ALU.mult))
                    link(V.tensor_tensor(cand, cand, eq, ALU.add))
                    link(V.tensor_reduce(at, cand, AX.X, ALU.min))
                    link(V.tensor_tensor(out, ids, wide(at, P, 3, NE), ALU.is_equal))
                    return top

                top1 = largest(prob, first, "1")
                link(V.tensor_scalar(left, first, -2.0, None, ALU.mult))
                link(V.tensor_tensor(left, left, prob, ALU.add))
                top2 = largest(left, second, "2")
                link(V.tensor_tensor(chosen, first, second, ALU.add))
                link(V.memset(chosen[NS:P, 2, :], 0.0))
                link(V.tensor_tensor(stat("tsum", 3), top1, top2, ALU.add))
                link(V.reciprocal(stat("tinv", 3), stat("tsum", 3)))
                link(V.tensor_tensor(gate, first, wide(top1, P, 3, NE), ALU.mult))
                link(V.tensor_tensor(top_p, second, wide(top2, P, 3, NE), ALU.mult))
                link(V.tensor_tensor(gate, gate, top_p, ALU.add))
                link(V.tensor_tensor(gate, gate, wide(stat("tinv", 3), P, 3, NE), ALU.mult))
                tell(picks_ready)
                bank = filled(dve, "ranks")
                link(V.tensor_copy(cnt, psum[bank][:, 3 * NE:4 * NE]))
                link(V.tensor_tensor(ranked, psum[bank][:, 0:3 * NE].rearrange("p (c n) -> p c n", c=3), chosen, ALU.mult))
                link(V.tensor_scalar(e2, chosen, 1000.0, -1000.0, ALU.mult, ALU.add))
                link(V.tensor_tensor(ranked, ranked, e2, ALU.add))
                link(V.tensor_scalar(nch, cnt, float(P), None, ALU.is_gt))
                link(V.tensor_scalar(starts, cnt, float(2 * P), 1.0, ALU.is_gt, ALU.add))
                link(V.tensor_tensor(nch, nch, starts, ALU.add))
                link(V.tensor_tensor_scan(ends, ones[:, 0:NE], nch, 0.0, ALU.mult, ALU.add))
                link(V.tensor_tensor(starts, ends, nch, ALU.subtract))
                turns3 = [P, MAX_ITEMS, NE]
                link(V.tensor_tensor(item_t, wide(item_ids[:, :], *turns3), starts.unsqueeze(1).to_broadcast(turns3), ALU.is_ge))
                link(V.tensor_reduce(item_e, item_t, AX.X, ALU.add))
                link(V.tensor_scalar(item_e, item_e, -1.0, None, ALU.add))
                link(V.tensor_tensor(item_oh, iota8[:, :].unsqueeze(1).to_broadcast(turns3), wide(item_e, *turns3), ALU.is_equal))
                link(V.tensor_tensor(item_t, item_oh, starts.unsqueeze(1).to_broadcast(turns3), ALU.mult))
                link(V.tensor_reduce(item_c, item_t, AX.X, ALU.add))
                link(V.tensor_tensor(item_c, item_ids[:, :], item_c, ALU.subtract))
                link(V.tensor_scalar(item_c, item_c, float(P), None, ALU.mult))
                for src, dst in ((ranked, rank_i), (gate, gate_i)):
                    for c in range(3):
                        link(V.tensor_tensor(route4[:, c, :, :], item_oh, src[:, c, :].unsqueeze(1).to_broadcast(turns3), ALU.mult))
                    link(V.tensor_reduce(dst, route4, AX.X, ALU.add))
                link(V.tensor_tensor(rank_i, rank_i, item_c.unsqueeze(1).to_broadcast([P, 3, MAX_ITEMS]), ALU.subtract))
                link(V.tensor_copy(items[0:1, 0:1], ends[0:1, NE - 1:NE]))
                link(V.tensor_scalar(items[0:1, 1 + MAX_ITEMS:2 + MAX_ITEMS], ends[0:1, NE - 1:NE], -1.0, None, ALU.add))
                V.tensor_copy(items[0:1, 1:1 + MAX_ITEMS], item_e[0:1, :]).then_inc(bank_emptied[bank], 1)
                tell(items_ready)

            dve.wait_ge(items_ready, 1)
            dve.wait_ge(iota_made, 1)
            n_items = dve.value_load(items[0:1, 0:1], min_val=NE, max_val=MAX_ITEMS)
            with dve.Fori(0, n_items) as i:
                for c in range(3):
                    r = ROWS[c]
                    V.tensor_scalar(e_pick[0:r, c, :], iota_row[0:r, :], rank_i[0:r, c, bass.ds(i, 1)], None, ALU.is_equal)
                    V.tensor_scalar(e_give[0:r, c, :], iota_row[0:r, :], rank_i[0:r, c, bass.ds(i, 1)],
                                    gate_i[0:r, c, bass.ds(i, 1)], ALU.is_equal, ALU.mult)
                tell(e_pick_ready)
                g0 = (DEPTH - 1) * N_GAINS + GAIN_AT["ffn"]
                for f in range(2):
                    bank = e_filled_wait(dve, ("take", f), i)
                    ks = slice(4 * f, 4 * f + 4)
                    ps = psum[bank][:, :].rearrange("p (k t) -> p k t", k=4)
                    V.tensor_tensor(ps, ps, wide(gains[:, g0 + 4 * f:g0 + 4 * f + 4], P, 4, P), ALU.mult)\
                        .then_inc(column_step, 1)
                    dve.wait_ge(column_step, i * COLUMN_STEPS + (2 * f + 1))
                    V.tensor_copy(e_xT_hi[:, ks, :], ps).then_inc(column_step, 1)
                    dve.wait_ge(column_step, i * COLUMN_STEPS + (2 * f + 2))
                    V.tensor_tensor(e_xT_lo[:, ks, :], ps, e_xT_hi[:, ks, :].bitcast(F32), ALU.subtract)\
                        .then_inc(bank_emptied[bank], 1)
                tell(xT_ready)
                bank = e_filled_wait(dve, ("giveT",), i)
                V.tensor_copy(e_giveT.rearrange("p c t -> p (c t)")[:, 0:NTOK], psum[bank][:, 0:NTOK]).then_inc(bank_emptied[bank], 1)
                for step in range(HALVES // 2):
                    for m in (2 * step, 2 * step + 1):
                        dve.wait_ge(w_hi_made, i * HALVES + (m + 1))
                        V.tensor_tensor(w_lo[m % SPLIT][:, 0:DVE_COLS], raw_half[m % MOE_RING][:, 0:DVE_COLS],
                                        w_hi[m % SPLIT][:, 0:DVE_COLS].bitcast(F32), ALU.subtract).then_inc(w_lo_made[0], 1)
                    g = step - 1
                    if 0 <= g < NEG_G:
                        bank = e_filled_wait(dve, ("up", g), i)
                        dve.wait_ge(e_silu_ready, i * NEG_G + (g + 1))
                        V.tensor_tensor(e_mid[:, g % 2, :], e_silu[:, g % 2, :], psum[bank][:, 256:512], ALU.mult)\
                            .then_inc(bank_emptied[bank], 1)
                    g = step - 2
                    if 0 <= g < NEG_G:
                        dve.wait_ge(midT_hi_made, i * NEG_G + (g + 1))
                        bank = e_jobs[("midT", g)][0]
                        V.tensor_tensor(e_midT_lo[:, 2 * g:2 * g + 2, :], psum[bank][:, 0:256].rearrange("p (j t) -> p j t", j=2),
                                        e_midT_hi[:, 2 * g:2 * g + 2, :].bitcast(F32), ALU.subtract)\
                            .then_inc(bank_emptied[bank], 1)
                bank = e_filled_wait(dve, ("down", 0), i)
                V.tensor_copy(e_y[:, 0, :], psum[bank][:, :]).then_inc(bank_emptied[bank], 1)
                for f in range(2):
                    for c in range(3):
                        r = ROWS[c]
                        bank = e_filled_wait(dve, ("give", c, f), i)
                        xs = x[0:r, c, f * 512:(f + 1) * 512]
                        V.tensor_tensor(xs, xs, psum[bank][0:r, :], ALU.add).then_inc(bank_emptied[bank], 1)
            tell(x_ready)
            dve.wait_ge(gfin_loaded, 16)
            for c in range(3):
                r = ROWS[c]
                dve.wait_ge(std_ready, 3 * len(NORMS) + c + 1)
                link(V.reciprocal(stat(("rstd", "f", c), rows=r), stat(("std", "f", c), rows=r)))
                V.scalar_tensor_tensor(out=h[0:r, c, :], in0=x[0:r, c, :], scalar=stat(("rstd", "f", c), rows=r),
                                       in1=g_final[0:r, :], op0=ALU.mult, op1=ALU.mult).then_inc(out_ready, 1)

        @block.scalar
        def _(act):
            steps, told = [0], [0]
            S = nc.scalar

            def link(ins):
                steps[0] += 1
                ins.then_inc(scalar_step, 1)
                act.wait_ge(scalar_step, steps[0])

            def tell(s):
                told[0] += 1
                S.activation(note[:, 16 + told[0] % 8:17 + told[0] % 8], eps[:, :], ACT.Copy).then_inc(s, 1)

            def empty(key, dst, src, func=ACT.Copy):
                bank = filled(act, key)
                S.activation(dst, src(psum[bank]), func).then_inc(bank_emptied[bank], 1)

            act.wait_ge(consts_made, 1)
            for c in range(2):
                act.wait_ge(mem_loaded, 16)
                link(S.activation(h[:, c, :], mem[:, c, :], ACT.Square, accum_out=stat(("mem_ss", c))))
                S.activation(stat(("mem_std", c)), stat(("mem_ss", c)), ACT.Sqrt, bias=eps[:, :], scale=1.0 / D).then_inc(mem_std, 1)

            def row_std(n, c, key=None):
                r = ROWS[c]
                key = n if key is None else key
                link(S.activation(h[0:r, c, :], x[0:r, c, :], ACT.Square, accum_out=stat(("ss", key, c), rows=r)))
                S.activation(stat(("std", key, c), rows=r), stat(("ss", key, c), rows=r), ACT.Sqrt, bias=eps[0:r, :],
                             scale=1.0 / D).then_inc(std_ready, 1)

            x_seen = [0]

            def stage_std(n, each=1):
                for c in range(3):
                    x_seen[0] += 1
                    act.wait_ge(x_ready, x_seen[0])
                    row_std(n, c)

            act.wait_ge(x_loaded, 32)
            act.wait_ge(mem_ready, 2)
            for c in range(3):
                row_std(0, c)
            for c in range(2):
                for f in range(2):
                    empty(("memT", c, f), memT[:, 4 * f:4 * f + 4, COLS[c]],
                          lambda ps: ps[:, :].rearrange("p (k t) -> p k t", k=4))
            for l in range(DEPTH):
                for n, part in ((1, "k"), (2, "v")):
                    for c in range(3):
                        r = ROWS[c]
                        empty(((part, l), c), qkv[0:r, c, n * AW:(n + 1) * AW], lambda ps: ps[0:r, :])
                    if n == 1:
                        act.wait_ge(abs_ready, l + 1)
                        for r, cs in ((P, slice(0, 2)), (NS, slice(2, 3))):
                            link(S.activation(log_tmp[0:r, 1, cs, :], log_tmp[0:r, 0, cs, :], ACT.Exp, scale=-1.0))
                            last = S.activation(log_tmp[0:r, 1, cs, :], log_tmp[0:r, 1, cs, :], ACT.Ln, bias=1.0)
                        last.then_inc(softplus_ready, 1)
                for c in range(3):
                    r = ROWS[c]
                    empty((("gate", l), c), u[0:r, c, :], lambda ps: ps[0:r, :], ACT.Sigmoid)
                for c in range(3):
                    empty(("kT", l, c), kT[:, :, COLS[c]], lambda ps: ps[:, 0:4 * ROWS[c]].rearrange("p (j t) -> p j t", j=4))
                for b in range(2):
                    bank = filled(act, ("histT", l, b))
                    for j in range(4):
                        last = S.activation(us[:, j, 4 * b:4 * b + 4, 0:HIST],
                                            psum[bank][:, j * 4 * HIST:(j + 1) * 4 * HIST].rearrange("p (b t) -> p b t", b=4), ACT.Copy)
                    last.then_inc(bank_emptied[bank], 1)
                tell(hist_ready)
                n = 0
                for i in range(2):
                    keys = (i + 1) * P
                    per = 512 // keys
                    for g in range(NH // per):
                        n += 1
                        act.wait_ge(pmax_ready, 6 * l + n)
                        bank = jobs[("scores", l, i, g)][0]
                        for a in range(per):
                            last = S.activation(p_prompt[i][:, g * per + a, :], psum[bank][:, a * keys:(a + 1) * keys], ACT.Exp,
                                                bias=stat(("pbias", l, i, g), per)[:, a:a + 1],
                                                accum_out=stat(("psum", l, i, g), per)[:, a:a + 1])
                        last.then_inc(bank_emptied[bank], 1)
                for n in range(6):
                    empty(("pT", l, n), PT[:, 4 * (n % 2):4 * (n % 2) + 4, :], lambda ps: ps[:, :].rearrange("p (j t) -> p j t", j=4))

                def key_columns(n):
                    b, half = n // 2, n % 2
                    for pg in range(4 * half, 4 * half + 4):
                        empty(("KT", l, b, pg), KT[:, n % 2, :, (pg % 4) * P:(pg % 4 + 1) * P],
                              lambda ps: ps[:, :].rearrange("p (j t) -> p j t", j=4))

                def exps(p):
                    act.wait_ge(smax_ready, PAIRS * l + p + 1)
                    bias, sums = stat(("sbias", l, p)), stat(("ssum", l, p), 3)
                    for half in range(2):
                        bank = jobs[("past", l, p, half)][0]
                        S.activation(probs[:, half * 512:(half + 1) * 512], psum[bank][:, :], ACT.Exp, bias=bias,
                                     accum_out=sums[:, half:half + 1]).then_inc(bank_emptied[bank], 1)
                    S.activation(probs[:, PAST:PAST + NS], probs[:, PAST:PAST + NS], ACT.Exp, bias=bias,
                                 accum_out=sums[:, 2:3]).then_inc(sexp_ready, 1)

                def probs_columns(p):
                    for t in range(2):
                        empty(("PT", l, p, t), PT[:, 4 * t:4 * t + 4, :], lambda ps: ps[:, :].rearrange("p (j t) -> p j t", j=4))
                    empty(("PT", l, p, 2), PT[0:NS, 8, :], lambda ps: ps[0:NS, 0:P])

                key_columns(0)
                for p in range(PAIRS + 1):
                    if p < PAIRS:
                        for n in range(4 * p, 4 * p + 4):
                            if n % 4 == 2 and p:
                                probs_columns(p - 1)
                            if n + 1 < 4 * p + 4:
                                key_columns(n + 1)
                        if p == 0:
                            key_columns(4)
                        exps(p)
                    else:
                        probs_columns(p - 1)
                    if p and p + 1 < PAIRS:
                        key_columns(4 * (p + 1))

                for c in range(3):
                    r = ROWS[c]
                    act.wait_ge(zvar_ready, 3 * l + c + 1)
                    S.activation(stat(("zstd", l, c), rows=r), stat(("zmv", l, c), 2, r)[:, 1:2], ACT.Sqrt, bias=eps[0:r, :])\
                        .then_inc(zstd_ready, 1)
                for c in range(3):
                    r = ROWS[c]
                    act.wait_ge(znorm_ready, 3 * l + c + 1)
                    link(S.activation(h[0:r, c, 512:D], u[0:r, c, :], ACT.Silu))
                act.wait_ge(oattn_ready, 2 * l + 2)
                for c in range(3):
                    r = ROWS[c]
                    for f in range(2):
                        link(S.activation(u[0:r, c, :], h[0:r, c, f * 512:(f + 1) * 512], ACT.Square,
                                          accum_out=stat(("mss", l, c), 2, r)[:, f:f + 1]))
                    S.activation(stat(("mstd", l, c), 2, r), stat(("mss", l, c), 2, r), ACT.Sqrt, bias=eps[0:r, :],
                                 scale=1.0 / AW).then_inc(mstd_ready, 1)
                for g in range(2):
                    for c in range(2):
                        empty((("mkv", l, g), c), mkv[:, c, g * 512:(g + 1) * 512], lambda ps: ps[:, :])
                stage_std(NORM_AT[(l, "cross")])
                for m in range(2):
                    empty(("mkT", l, m), mkT[:, :, m * P:(m + 1) * P], lambda ps: ps[:, :].rearrange("p (j t) -> p j t", j=XH))
                for b in range(DB):
                    for m in range(2):
                        empty(("xKT", l, b, m), xKT[:, b % 2, :, m * P:(m + 1) * P],
                              lambda ps: ps[:, :].rearrange("p (j t) -> p j t", j=XH))
                for quad in range(QUADS):
                    act.wait_ge(xmax_ready, 6 * l + quad + 1)
                    bank = jobs[("xs", l, quad)][0]
                    S.activation(xp[:, quad, :], psum[bank][:, 0:NMEM], ACT.Exp, bias=stat(("xbias", l, quad)), scale=X_SCALE,
                                 accum_out=stat(("xsum", l, quad))).then_inc(bank_emptied[bank], 1)
                for i in range(2):
                    for g in range(2):
                        act.wait_ge(xmax_ready, 6 * l + 2 + 2 * i + g + 1)
                        bank = jobs[("xscores", l, i, g)][0]
                        for a in range(2):
                            last = S.activation(xp_prompt[:, i, 2 * g + a, :], psum[bank][:, a * NMEM:(a + 1) * NMEM], ACT.Exp,
                                                bias=stat(("xpbias", l, i, g), 2)[:, a:a + 1], scale=X_SCALE,
                                                accum_out=stat(("xpsum", l, i), XH)[:, 2 * g + a:2 * g + a + 1])
                        last.then_inc(bank_emptied[bank], 1)
                for quad in range(QUADS):
                    empty(("xPT", l, quad), xPT[:, quad, 0:2, :], lambda ps: ps[:, 0:2 * P].rearrange("p (j t) -> p j t", j=2))
                for n in range(4):
                    empty(("xpT", l, n), xPT[:, 2 + n % 2, :, :], lambda ps: ps[:, :].rearrange("p (j t) -> p j t", j=4))
                for c in range(3):
                    empty(("xoT", l, c), hT[:, 0:XH, COLS[c]], lambda ps: ps[:, 0:4 * ROWS[c]].rearrange("p (j t) -> p j t", j=4))
                stage_std(NORM_AT[(l, "ffn")])
                if l % 2 == 0:
                    for g in range(NFG):
                        for c in range(3):
                            r = ROWS[c]
                            bank = filled(act, (("ff", l, g), c))
                            S.activation(silu[0:r, g % 2, c, :], psum[bank][0:r, 0:256], ACT.Silu).then_inc(silu_ready, 1)
                    stage_std(NORM_AT[(l + 1, "mix")])
                    continue
                act.wait_ge(rmax_ready, 1)
                S.activation(route[0], route[0], ACT.Exp).then_inc(rexp_ready, 1)

            act.wait_ge(mkv_stored, 32 * DEPTH)
            act.wait_ge(items_ready, 1)
            n_items = act.value_load(items[0:1, 0:1], min_val=NE, max_val=MAX_ITEMS)
            with act.Fori(0, n_items) as i:
                for step in range(HALVES // 2):
                    for m in (2 * step, 2 * step + 1):
                        act.wait_ge(e_landed[m % MOE_RING], i * e_bytes[m % MOE_RING] + e_done[m])
                        half_read_wait(act, i, m - SPLIT)
                        S.activation(w_hi[m % SPLIT][:, :], raw_half[m % MOE_RING], ACT.Copy).then_inc(w_hi_made, 1)
                    g = step - 1
                    if 0 <= g < NEG_G:
                        bank = e_filled_wait(act, ("up", g), i)
                        S.activation(e_silu[:, g % 2, :], psum[bank][:, 0:256], ACT.Silu).then_inc(e_silu_ready, 1)
                    g = step - 2
                    if 0 <= g < NEG_G:
                        bank = e_filled_wait(act, ("midT", g), i)
                        S.activation(e_midT_hi[:, 2 * g:2 * g + 2, :], psum[bank][:, 0:256].rearrange("p (j t) -> p j t", j=2),
                                     ACT.Copy).then_inc(midT_hi_made, 1)
                bank = e_filled_wait(act, ("down", 1), i)
                S.activation(e_y[:, 1, :], psum[bank][:, :], ACT.Copy).then_inc(bank_emptied[bank], 1)
            x_seen[0] += 1
            act.wait_ge(x_ready, x_seen[0])
            for c in range(3):
                row_std(None, c, "f")

        @block.gpsimd
        def _(pool):
            steps = [0]
            G = nc.gpsimd

            def link(ins):
                steps[0] += 1
                ins.then_inc(pool_step, 1)
                pool.wait_ge(pool_step, steps[0])

            def select(t, pattern, base, mult, op, fill):
                link(G.affine_select(out=t, in_=t, compare_op=op, fill=fill, base=base, pattern=pattern,
                                     channel_multiplier=mult))

            link(G.memset(ident[:, :], 0.0))
            select(ident[:, :], [[-1, P]], 0, 1, ALU.not_equal, 1.0)
            for t in (ones[:, :], upto[:, :], before[:, :], block_upto[:, :], page_suffix, own_head[:, :], own_xhead[:, :]):
                link(G.memset(t, 1.0))
            link(G.memset(causal[:, :], 0.0))
            link(G.memset(eps[:, :], EPS))
            link(G.memset(spread8, 0.0))
            link(G.memset(small8[:, :, :, :], 0.0))
            select(upto[:, :], [[1, P]], 0, -1, ALU.is_ge, 0.0)
            select(before[:, :], [[1, P]], -1, -1, ALU.is_ge, 0.0)
            select(causal[:, :], [[-1, P]], 0, 1, ALU.is_ge, NEG)
            bu = block_upto[:, :].rearrange("p (b t) -> p b t", b=DB)
            select(block_upto[:, :], [[1, NS]], 0, -1, ALU.is_ge, 0.0)
            select(bu, [[-DS, DB], [0, DS]], 0, 1, ALU.is_ge, 0.0)
            ps = page_suffix.rearrange("p (b g) -> p b g", g=NPG)
            select(page_suffix, [[-1, P]], 0, 1, ALU.is_ge, 0.0)
            select(ps, [[NPG, P // NPG], [0, NPG]], NPG - 1, -1, ALU.is_ge, 0.0)
            link(G.memset(decay_rows[:, :, :, :], 0.0))
            select(decay_rows[:, :, :, :].rearrange("p l b (h t) -> p l b h t", h=NH),
                   [[-NS, DEPTH], [-NH, DB], [-1, NH], [0, DS]], 0, 1, ALU.not_equal, 1.0)
            select(spread8.rearrange("p (a t) -> p a t", t=DS), [[0, P // DS], [-1, DS]], 0, 1, ALU.not_equal, 1.0)
            select(small8[:, 0, :, :], [[0, DB], [-1, DS]], 0, 1, ALU.is_ge, NEG)
            select(small8[:, 1, :, :], [[0, DB], [-1, DS]], 0, 1, ALU.not_equal, 1.0)
            for n in range(2):
                t = own_head[n * NS:(n + 1) * NS, :]
                select(t, [[-DS, NH]], 0, 1, ALU.is_ge, 0.0)
                select(t, [[DS, NH]], DS - 1, -1, ALU.is_ge, 0.0)
            for n in range(4):
                t = own_xhead[32 * n:32 * n + 32, :]
                select(t, [[-DS, XH]], 0, 1, ALU.is_ge, 0.0)
                select(t, [[DS, XH]], DS - 1, -1, ALU.is_ge, 0.0)
            link(G.memset(up[:, :, 0:HIST], 0.0))
            link(G.iota(item_ids[:, :], [[1, MAX_ITEMS]], base=0, channel_multiplier=0, allow_small_or_imprecise_dtypes=True))
            G.iota(iota8[:, :], [[1, NE]], base=0, channel_multiplier=0, allow_small_or_imprecise_dtypes=True).then_inc(consts_made, 1)
            pool.wait_ge(idx_ready, 1)
            G.indirect_dma_start(out=arena[:, 0:PAGE * NH], out_offset=None,
                                 in_=d["cache_logf"].rearrange("l n s h -> (l n) (s h)"),
                                 in_offset=bass.IndirectOffsetOnAxis(ap=page_idx[:, :].bitcast(U32), axis=0))\
                .then_inc(pages_gathered, 16)
            pool.wait_ge(masks_spread, 1)
            for t, n, per, fill in ((new_mask, PAIRS, NS, NEG), (pair_rows, PAIRS, NS, 0.0), (quad_rows, QUADS, 32, 0.0)):
                v = t[:, :, :].rearrange("p a (b t) -> p a b t", b=DB)
                select(v, [[P, n], [-per, DB], [0, DS]], 0, 1, ALU.is_ge, fill)
                select(v, [[-P, n], [per, DB], [0, DS]], per - 1, -1, ALU.is_ge, fill)
            G.memset(note2[:, :], 0.0).then_inc(masks_made, 1)
            pool.wait_ge(decay_made, 2)
            G.dma_start(scratch, lf_decay.rearrange("p h s -> p (h s)")).then_inc(decay_stored, 16)
            pool.wait_ge(decay_stored, 16)
            for n in range(DEPTH * DB):
                G.dma_start(past_decay[n * NH:(n + 1) * NH, :].rearrange("h (g s) -> h g s", g=NPG),
                            scratch[n * NPG:(n + 1) * NPG, :].rearrange("g (h s) -> h g s", h=NH)).then_inc(decay_loaded, 16)

            def store(dst, src, s):
                G.dma_start(dst, src).then_inc(s, 16)

            for l in range(DEPTH):
                if l:
                    pool.wait_ge(x_ready, 3 * NORM_AT[(l, "mix")])
                    link(G.memset(up[:, :, 0:HIST], 0.0))
                link(G.memset(q_rows, 0.0))
                G.memset(q_heads, 0.0).then_inc(q_zeroed, 1)
                for b in range(2):
                    G.dma_start(hist_in[0:4 * HIST, b, :], d["cache_conv"][l, 4 * b:4 * b + 4].rearrange("b t c -> (b t) c"))\
                        .then_inc(conv_hist_loaded, 16)
                pool.wait_ge(logf_ready, l + 1)
                store(d["new_logf_prompt"][l, 0].rearrange("(c p) n -> p c n", p=P), logf[:, 0:2, :], kv_stored)
                store(d["new_logf_sample"][l].rearrange("b t n -> (b t) n"), logf[0:NS, 2, :], kv_stored)
                for c in range(3):
                    filled(pool, ("kT", l, c))
                    for n, name in ((1, "k"), (2, "v")):
                        out = d[f"new_{name}_prompt"][l, 0, c * P:(c + 1) * P] if c < 2 else \
                            d[f"new_{name}_sample"][l].rearrange("b t h e -> (b t) h e")
                        store(out.rearrange("p h e -> p (h e)"), qkv[0:ROWS[c], c, n * AW:(n + 1) * AW], kv_stored)
                filled(pool, ("uT", l, 2))
                store(d["new_conv_prompt"][l, 0], u[P - HIST:P, 1, :], u_stored)
                for b in range(DB):
                    store(d["new_conv_sample"][l, b, HIST - DS:HIST], u[b * DS:(b + 1) * DS, 2, :], u_stored)
                store(d["new_conv_sample"][l, :, 0:HIST - DS], d["cache_conv"][l, :, DS:HIST], u_stored)
                filled(pool, ("past", l, PAIRS - 1, 1))
                for n, name in enumerate(("g_cln", "b_cln")):
                    G.dma_start(conv_norm[:, n, :], d[name][l:l + 1, :].to_broadcast([P, CW])).then_inc(conv_norm_loaded, 16)
                pool.wait_ge(h_ready, 3 * STAGE_AT[(l, "merged")] + 3)
                G.memset(xq_rows, 0.0).then_inc(q_zeroed, 1)
                filled(pool, ("mkT", l, 1))
                for n, name in enumerate(("k", "v")):
                    store(d[f"new_mem_{name}_prompt"][l, 0].rearrange("(c p) h e -> p c (h e)", p=P),
                          mkv[:, :, n * XW:(n + 1) * XW], mkv_stored)
            pool.wait_ge(x_ready, 3 * (len(NORMS) - 1))
            G.iota(iota_row[:, :], [[1, P]], base=0, channel_multiplier=0, allow_small_or_imprecise_dtypes=True)\
                .then_inc(iota_made, 1)
            pool.wait_ge(items_ready, 1)
            n_items = pool.value_load(items[0:1, 0:1], min_val=NE, max_val=MAX_ITEMS)
            with pool.Fori(0, n_items) as i:
                for m in range(HALVES):
                    pool.wait_ge(w_hi_made, i * HALVES + (m + 1))
                    G.tensor_tensor(w_lo[m % SPLIT][:, DVE_COLS:HALF], raw_half[m % MOE_RING][:, DVE_COLS:HALF],
                                    w_hi[m % SPLIT][:, DVE_COLS:HALF].bitcast(F32), ALU.subtract).then_inc(w_lo_made[1], 1)
            pool.wait_ge(mkv_stored, 16 * 4)
            pool.wait_ge(kv_stored, kv_waits * DEPTH)
            pool.wait_ge(u_stored, u_waits * DEPTH)

        @block.sync
        def _(sp):
            def load(dst, src, s):
                sp.dma_start(dst, src).then_inc(s, 16)

            page_rows = d["page_table"].rearrange("b (g o) -> (b g) o", o=1)
            load(page_idx[0:NS, :], page_rows, idx_loaded)
            load(page_idx[NS:P, :], page_rows, idx_loaded)
            load(x[:, 0:2, :], d["x_prompt"][0].rearrange("(c p) n -> p c n", p=P), x_loaded)
            load(x[0:NS, 2, :], d["x_sample"].rearrange("b t n -> (b t) n"), x_loaded)
            load(mem, d["mem_prompt"][0].rearrange("(c p) n -> p c n", p=P), mem_loaded)
            for l in range(DEPTH):
                at = l * N_GAINS
                for name in ("g_mix", "g_attn_out", "g_conv_out", "g_cross", "g_mem", "g_ffn"):
                    rows = d[name].shape[1] // P
                    load(gain_rows[at:at + rows, :], d[name][l].rearrange("(k p) -> k p", p=P), rows_loaded)
                    at += rows
                load(dw_rows[0:4 * CONV_K, l, :], d["w_dw"][l].rearrange("k (j c) -> (k j) c", c=P), rows_loaded)
                load(dw_rows[4 * CONV_K:P, l, :], d["b_dw"][l].rearrange("(j c) -> j c", c=P), rows_loaded)
                load(forget_w[:, l, :, :], d["w_in"][l, :, 3 * AW:3 * AW + NH].rearrange("(k p) n -> p k n", p=P), small_loaded)
                load(forget_b[:, l, :], d["b_fgate"][l:l + 1, :].to_broadcast([P, NH]), small_loaded)
            load(router_w[:, :, :], d["w_router"][0].rearrange("(k p) n -> p k n", p=P), small_loaded)
            load(router_b[:, :], d["b_router"][0:1, :].to_broadcast([P, NE]), small_loaded)

            def rows_of(name, l, lo, n):
                return d[name][l, :, lo:lo + n].rearrange("(k p) n -> p k n", p=P)

            glu = 3 * AW + NH
            col_of = {"q": 0, "k": AW, "v": 2 * AW, "value": glu, "gate": glu + CW}
            page_regs = None
            for n, (key, dmas) in enumerate(units):
                s = n % RING
                slot = ring[:, s * SLOT:(s + 1) * SLOT]
                if n >= RING:
                    by = freed_by[units[n - RING][0]]
                    if isinstance(by, int):
                        sp.wait_ge(down_read, by)
                    else:
                        filled(sp, by)
                k8 = slot.rearrange("p (k n) -> p k n", k=8)
                k4 = slot.rearrange("p (k n) -> p k n", k=4)
                kind, l = key[0], key[1]
                if kind == "w_in":
                    load(k8, rows_of("w_in", l, col_of[key[2]], 512), slot_landed[s])
                elif kind in ("w_out", "w_ckv"):
                    load(k8, rows_of(kind, l, 512 * key[2], 512), slot_landed[s])
                elif kind == "w_cq":
                    load(k8, rows_of(kind, l, 0, 512), slot_landed[s])
                elif kind == "w_co":
                    load(k4, rows_of(kind, l, 0, D), slot_landed[s])
                elif kind in "KV":
                    cache = d["cache_k" if kind == "K" else "cache_v"]
                    for g in range(NPG):
                        page = sp.value_load(d["page_table"][key[2]:key[2] + 1, g:g + 1], min_val=0, max_val=N_PHYS - 1)
                        load(k8[:, g, :], cache[l, bass.ds(page, 1)].rearrange("o s h e -> (o s) (h e)"), slot_landed[s])
                elif kind == "mem_kv":
                    for b2 in range(2):
                        for n2, name in enumerate(("cache_mem_k", "cache_mem_v")):
                            at = 4 * b2 + 2 * n2
                            load(k8[:, at:at + 2, :], d[name][l, key[2] + b2].rearrange("(m p) h e -> p m (h e)", p=P), slot_landed[s])
                elif kind == "ff_up":
                    for half in range(2):
                        load(k8[:, :, 256 * half:256 * half + 256], rows_of("w_ff_gu", l // 2, half * FF + 256 * key[2], 256),
                             slot_landed[s])
                elif kind == "ff_down":
                    nk = min(4, FF // P - 4 * key[2])
                    load(k4[:, 0:nk, :], d["w_ff_down"][l // 2, 512 * key[2]:512 * key[2] + nk * P, :]
                         .rearrange("(k p) n -> p k n", p=P), slot_landed[s])

            def expert_half(e, m):
                dst = raw_half[m % MOE_RING]
                if m < UP_HALVES:
                    lo, col = 512 * (m % 2), 256 * (m // 2)
                    for part in range(2):
                        load(dst.rearrange("p (k h n) -> p k h n", k=4, h=2)[:, :, part, :],
                             d["w_e_gu"][0, bass.ds(e, 1), lo:lo + 512, part * EF + col:part * EF + col + 256]
                             .rearrange("o (k p) n -> p (o k) n", p=P), e_landed[m % MOE_RING])
                else:
                    lo = 256 * (m - UP_HALVES)
                    load(dst.rearrange("p (k n) -> p k n", k=2),
                         d["w_e_down"][0, bass.ds(e, 1), lo:lo + 256, :].rearrange("o (k p) n -> p (o k) n", p=P),
                         e_landed[m % MOE_RING])

            def half_split(i, m):
                for s in w_lo_made:
                    sp.wait_ge(s, i * HALVES + (m + 1))

            def rest(i, e):
                for m in range(MOE_RING, HALVES):
                    half_split(i, m - MOE_RING)
                    expert_half(e, m)

            for m in range(MOE_RING):
                if m % 2 == 0:
                    filled(sp, freed_by[units[max(n for n in range(len(units)) if n % RING == m // 2)][0]])
                expert_half(0, m)
            sp.wait_ge(items_ready, 1)
            n_turns = sp.value_load(items[0:1, 0:1], min_val=NE, max_val=MAX_ITEMS)
            with sp.Fori(0, n_turns - 1) as i:
                rest(i, sp.value_load(items[0:1, bass.ds(i + 1, 1)], min_val=0, max_val=NE - 1))
                following = sp.value_load(items[0:1, bass.ds(i + 2, 1)], min_val=0, max_val=NE - 1)
                for m in range(MOE_RING):
                    half_split(i, HALVES - MOE_RING + m)
                    expert_half(following, m)
            last_turn = sp.value_load(items[0:1, 1 + MAX_ITEMS:2 + MAX_ITEMS], min_val=NE - 1, max_val=MAX_ITEMS - 1)
            rest(last_turn, sp.value_load(items[0:1, bass.ds(last_turn + 1, 1)], min_val=0, max_val=NE - 1))
            sp.wait_ge(x_ready, 3 * (len(NORMS) - 1) + 1)
            load(g_final[:, :], d["g_final"].rearrange("(a n) -> a n", a=1).to_broadcast([P, D]), gfin_loaded)
            for c in range(3):
                sp.wait_ge(out_ready, c + 1)
                out = d["y_prompt"][0, c * P:(c + 1) * P] if c < 2 else d["y_sample"].rearrange("b t n -> (b t) n")
                load(out, h[0:ROWS[c], c, :], out_stored)
            sp.wait_ge(out_stored, 48)


_OUTS = ["y_prompt", "y_sample", "new_k_prompt", "new_v_prompt", "new_logf_prompt", "new_conv_prompt",
         "new_mem_k_prompt", "new_mem_v_prompt", "new_k_sample", "new_v_sample", "new_logf_sample", "new_conv_sample"]


def kernel(**inputs):
    import numpy as np
    import concourse.bacc as bacc
    from concourse.bass_utils import run_bass_kernel_spmd

    xp, xs = inputs["x_prompt"].shape, inputs["x_sample"].shape
    L, _, _, NH, DH = inputs["cache_k"].shape
    NM, XH, XD = inputs["cache_mem_k"].shape[2:]
    hist, cw = inputs["cache_conv"].shape[2:]
    shapes = [xp, xs, (L, xp[0], xp[1], NH, DH), (L, xp[0], xp[1], NH, DH), (L, xp[0], xp[1], NH), (L, xp[0], hist, cw),
              (L, xp[0], NM, XH, XD), (L, xp[0], NM, XH, XD), (L, xs[0], xs[1], NH, DH), (L, xs[0], xs[1], NH, DH),
              (L, xs[0], xs[1], NH), (L, xs[0], hist, cw)]
    nc = bacc.Bacc("TRN2", target_bir_lowering=False, num_devices=1)
    arrays, d = {}, {}
    for name, a in inputs.items():
        a = np.ascontiguousarray(a)
        arrays["in_" + name] = a
        d[name] = nc.dram_tensor("in_" + name, a.shape, mybir.dt.from_np(a.dtype), kind="ExternalInput").ap()
    for name, shape in zip(_OUTS, shapes):
        d[name] = nc.dram_tensor("out_" + name, shape, F32, kind="ExternalOutput").ap()
    build_program(nc, d)
    r = run_bass_kernel_spmd(nc, [arrays], core_ids=[0])
    return tuple(r.results[0]["out_" + name] for name in _OUTS)
```

```python
from contextlib import ExitStack

import concourse.bass as bass
from concourse import mybir

F32 = mybir.dt.float32
F32R = mybir.dt.float32r
I32 = mybir.dt.int32
U32 = mybir.dt.uint32
ALU = mybir.AluOpType
ACT = mybir.ActivationFunctionType
AX = mybir.AxisListType

P = 128
NEG = -1.0e30
EPS = 1e-6


def build_program(nc, d):
    DEPTH, N_PHYS, PAGE, NH, DH = d["cache_k"].shape
    _, SEQ, D = d["x_prompt"].shape
    DB, DS, _ = d["x_sample"].shape
    NPG = d["page_table"].shape[1]
    PAST = NPG * PAGE
    AW = NH * DH
    CONV_K, CW = d["w_dw"].shape[1:]
    HIST = CONV_K - 1
    XH = d["cache_mem_k"].shape[3]
    NMEM = d["cache_mem_k"].shape[2]
    XW = XH * P
    FF = d["w_ff_down"].shape[1]
    NE, EF = d["w_e_down"].shape[1:3]
    NS = DB * DS
    assert SEQ == 2 * P and NS == 64 and D == 1024 and AW == CW == XW == 512 and PAGE == P
    assert NMEM == 2 * P and DH == 64 and DS == 8 and DB == 8 and DEPTH == 2 and NPG == 8
    KD = D // P
    ROWS = [P, P, NS]
    COLS = [slice(0, P), slice(P, 2 * P), slice(2 * P, 2 * P + NS)]
    NTOK = SEQ + NS
    NFG = FF // 256
    NEG_G = EF // 256
    MAX_ITEMS = NE + 4
    PICKS = MAX_ITEMS + 1
    X_SCALE = float(P) ** -0.5
    Q_SCALE = float(DH) ** -0.5
    PAIRS, QUADS = DB // 2, DB // 4
    RING = 4
    MOE_RING = 7
    SPLIT = 3
    DVE_COLS = 1664
    SLOT = 4096
    HALF = SLOT // 2
    STAGES = [(l, s) for l in range(DEPTH) for s in ("mix", "merged", "cross", "ffn")]
    STAGE_AT = {k: n for n, k in enumerate(STAGES)}
    NORMS = [(l, s) for l in range(DEPTH) for s in ("mix", "cross", "ffn")]
    NORM_AT = {k: n for n, k in enumerate(NORMS)}
    GAIN_AT = {"mix": 0, "merged": 8, "cross": 16, "mem": 24, "ffn": 32}
    N_GAINS = 40

    ctx = ExitStack()
    with ctx:
        def sb(name, shape, dt=F32):
            return ctx.enter_context(nc.sbuf_tensor(name, shape, dt))

        def sb_at(name, base, at, shape):
            return nc.alloc_sbuf_tensor_at(name, shape, F32R, offset=base + 4 * at)

        def sem(name):
            return ctx.enter_context(nc.semaphore(name))

        ring = sb("ring", [P, RING * SLOT])
        ring_base = nc.sbuf_base - 4 * RING * SLOT
        x = sb("x", [P, 3, D])
        h = sb("h", [P, 3, D])
        hT = sb("hT", [P, KD, NTOK])
        hT_base = nc.sbuf_base - 4 * KD * NTOK
        memT = sb("memT", [P, KD, NMEM])
        mem_base = nc.sbuf_base - 4 * KD * NMEM
        ARENA = 20728
        arena = sb("arena", [P, ARENA])
        arena_base = nc.sbuf_base - 4 * ARENA
        past_decay = sb("past_decay", [P, PAST])
        ident = sb("ident", [P, P])
        ones = sb("ones", [P, P])
        upto = sb("upto", [P, P])
        before = sb("before", [P, P])
        causal = sb("causal", [P, P])
        block_upto = sb("block_upto", [NS, NS])
        new_mask = sb("new_mask", [P, PAIRS, NS])
        pair_rows = sb("pair_rows", [P, PAIRS, NS])
        quad_rows = sb("quad_rows", [P, QUADS, NS])
        own_head = sb("own_head", [P, NH])
        own_xhead = sb("own_xhead", [P, XH])
        note = sb("note", [P, 24])
        step_of = sb("step_of", [NS, DS])
        batch_of = sb("batch_of", [NS, DB])
        gains = sb("gains", [P, DEPTH * N_GAINS])
        conv_w = sb("conv_w", [P, DEPTH, P])
        forget_w = sb("forget_w", [P, DEPTH, KD, NH])
        router_w = sb("router_w", [P, KD, NE])
        forget_b = sb("forget_b", [P, DEPTH, NH])
        router_b = sb("router_b", [P, NE])
        decay_rows = sb("decay_rows", [P, DEPTH, DB, NS])
        eps = sb("eps", [P, 1])
        item_ids = sb("item_ids", [P, PICKS])
        iota8 = sb("iota8", [P, NE])
        stats = sb("stats", [P, 512])
        logf = sb("logf", [P, 3, NH])
        log_tmp = sb("log_tmp", [P, 2, 3, NH])
        cum_and_pages = sb("cum_and_pages", [P, SEQ])
        cumT = cum_and_pages[0:NH, :]
        page_row = cum_and_pages[NS:NS + 1, 0:DB * NPG].bitcast(I32)
        neg_cumT = sb("neg_cumT", [NH, SEQ])
        cum_rows = sb("cum_rows", [NS, NH, DS])
        neg_cum_rows = sb("neg_cum_rows", [NS, NH, DS])
        cum_s = sb("cum_s", [NS, NH])
        own_cum = sb("own_cum", [P, PAIRS])


        def carve(at, *shape, rows=P):
            n = 1
            for s in shape:
                n *= s
            assert at + n <= ARENA, (at, n)
            v = arena[0:rows, at:at + n]
            names = " ".join(f"d{i}" for i in range(len(shape)))
            return v if len(shape) == 1 else v.rearrange(
                f"p ({names}) -> p {names}", **{f"d{i}": s for i, s in enumerate(shape)})

        qkv = carve(0, 3, 3 * AW)
        u = carve(4608, 3, CW)
        up = carve(6144, 4, HIST + SEQ)
        us = carve(7288, 4, DB, HIST + DS)
        q_heads = carve(8504, NH, SEQ)
        conv_z = carve(8504, 4, NTOK)
        q_rows = carve(10552, 4, DB, NH * DS)
        kT = carve(12600, 4, NTOK)
        KT = carve(13880, 2, 4, 512)
        conv_norm = carve(13880, 2, CW)
        p_prompt = [carve(13880, NH, P), carve(13880 + NH * P, NH, 2 * P)]
        uT = carve(14904, 4, NTOK)
        PT = carve(17976, 9, P)
        probs = carve(19128, PAST + NS)
        o_masked = carve(20216, AW)
        hist_in = carve(17976, 2, CW)
        lf_pages = carve(13880, PAGE, NH)
        lf_decay = carve(13880, NH, PAGE)
        lf_sum = carve(14904, NH, PAGE)
        mem = carve(15928, 2, D)
        gain_rows = carve(19128, P)
        dw_rows = carve(19256, DEPTH, P)
        page_suffix = carve(19512, P)
        spread8 = carve(19640, P, rows=DS)
        small8 = carve(19768, 2, DB, DS, rows=DS)
        mem_squares = carve(4608, D)
        mem_g = carve(0, KD, NMEM)
        mkv = carve(2048, 2, 2 * XW)
        mkT = carve(4096, XH, NMEM)
        xqT = carve(6656, XH, SEQ)
        xq_rows = carve(7680, XH, DB, XH * DS)
        xKT = carve(8704, 2, XH, NMEM)
        xp = carve(10752, QUADS, NMEM)
        xp_prompt = carve(11264, 2, XH, NMEM)
        xPT = carve(13312, 4, 4, P)
        xo_masked = carve(15360, QUADS, XW)
        xo = carve(16384, 3, XW)
        ff_rows = h[:, :, :].rearrange("p c n -> p (c n)")[:, 0:8 * NTOK].rearrange("p (m g j t) -> p m g j t", m=2, g=2, j=2)
        silu, mid = ff_rows[:, 0, :, :, :], ff_rows[:, 1, :, :, :]
        FF_RAW_AT, FF_HI_AT = [0, 2, 3, 6, 7], [1, 4, 5]
        FF_RAW, FF_HI = len(FF_RAW_AT), len(FF_HI_AT)
        ff_raw = [ring[:, a * HALF:(a + 1) * HALF] for a in FF_RAW_AT]
        ff_lo = [sb_at(f"ff_lo{n}", ring_base, a * HALF, [P, HALF]) for n, a in enumerate(FF_RAW_AT)]
        ff_hi = [sb_at(f"ff_hi{n}", ring_base, a * HALF, [P, HALF]) for n, a in enumerate(FF_HI_AT)]
        midT_hi = sb_at("midT_hi", arena_base, 0, [P, FF // P, NTOK])
        midT_lo = sb_at("midT_lo", arena_base, FF // P * NTOK, [P, FF // P, NTOK])
        hT_hi = sb_at("hT_hi", hT_base, 0, [P, KD, NTOK])
        hT_lo = sb_at("hT_lo", arena_base, 2 * (FF // P) * NTOK, [P, KD, NTOK])
        assert (2 * (FF // P) + KD) * NTOK <= ARENA
        PART_COLS = [slice(NS, NS + P), slice(NS + P, NS + 2 * P), slice(0, NS)]
        PART_WIDE = [PART_COLS[0], PART_COLS[1], slice(0, P)]
        FF_UP_HALVES = 2 * NFG
        FF_OUT_BANK = [4, 5, 6, 7, 0, 1] if NFG % 2 else [0, 1, 2, 3, 4, 5]
        FF_HALVES = FF_UP_HALVES + FF // 256
        raw_half = [ring[:, s * HALF:(s + 1) * HALF] for s in range(MOE_RING)]
        w_hi = [sb_at(f"w_hi{s}", arena_base, s * HALF, [P, HALF]) for s in range(SPLIT)]
        w_lo = [sb_at(f"w_lo{s}", arena_base, (SPLIT + s) * HALF, [P, HALF]) for s in range(SPLIT)]
        M0 = 2 * SPLIT * HALF
        e_midT_hi = sb_at("e_midT_hi", arena_base, M0, [P, EF // P, P])
        e_midT_lo = sb_at("e_midT_lo", arena_base, M0 + EF, [P, EF // P, P])
        e_xT_hi = sb_at("e_xT_hi", mem_base, 0, [P, KD, P])
        e_xT_lo = sb_at("e_xT_lo", mem_base, D, [P, KD, P])
        e_y = past_decay[:, :].rearrange("p (f n) -> p f n", f=2)
        e_rows = decay_rows[:, :, :, :].rearrange("p l b t -> p (l b t)").rearrange("p (m g n) -> p m g n", m=2, g=2)
        e_silu, e_mid = e_rows[:, 0, :, :], e_rows[:, 1, :, :]
        spare = ring[:, MOE_RING * HALF:RING * SLOT]
        e_pick, e_give, e_giveT = [spare[:, n * 3 * P:(n + 1) * 3 * P].rearrange("p (c t) -> p c t", c=3) for n in range(3)]
        iota_row = spare[:, 9 * P:10 * P]
        R0 = M0 + 2 * EF
        route = [carve(R0 + 24 * i, 3, NE) for i in range(12)]
        cnt = carve(R0 + 288, NE)
        nch = carve(R0 + 296, NE)
        ends = carve(R0 + 304, NE)
        starts = carve(R0 + 312, NE)
        item_e = carve(R0 + 320, PICKS)
        item_c = carve(R0 + 336, PICKS)
        item_oh = carve(R0 + 352, PICKS, NE)
        item_t = carve(R0 + 456, PICKS, NE)
        rank_i = carve(R0 + 560, 3, PICKS)
        gate_i = carve(R0 + 600, 3, PICKS)
        route4 = carve(R0 + 640, 3, PICKS, NE)
        items = sb("items", [1, 2 + MAX_ITEMS], I32)
        page_idx = sb("page_idx", [P, 1], I32)
        scratch = nc.dram_tensor("decay_scratch", [P, NH * PAGE], F32, kind="Internal").ap()

        psum = [ctx.enter_context(nc.psum_tensor(f"bank{b}", [P, 512], F32)) for b in range(8)]

        bank_filled = [sem(f"bank_filled{b}") for b in range(8)]
        bank_emptied = [sem(f"bank_emptied{b}") for b in range(8)]
        slot_landed = [sem(f"slot_landed{s}") for s in range(RING)]
        ff_landed = [sem(f"ff_half_landed{s}") for s in range(FF_RAW)]
        ff_hi_made = sem("ff_hi_made")
        ff_lo_made = sem("ff_lo_made")
        ff_read = sem("ff_read")
        ff_midT_hi_made = sem("ff_midT_hi_made")
        e_landed = [sem(f"expert_half_landed{s}") for s in range(MOE_RING)]
        w_hi_made = sem("w_hi_made")
        w_lo_made = [sem("w_lo_made_by_vector"), sem("w_lo_made_by_pool")]
        w_read = sem("w_read")
        xT_ready = sem("expert_columns_ready")
        column_step = sem("expert_column_step")
        midT_hi_made = sem("midT_hi_made")
        x_loaded = sem("x_loaded")
        mem_loaded = sem("mem_loaded")
        rows_loaded = sem("rows_loaded")
        small_loaded = sem("small_loaded")
        idx_loaded = sem("idx_loaded")
        page_row_loaded = sem("page_row_loaded")
        idx_ready = sem("idx_ready")
        pages_gathered = sem("pages_gathered")
        decay_made = sem("decay_made")
        decay_stored = sem("decay_stored")
        decay_loaded = sem("decay_loaded")
        ident_made = sem("ident_made")
        consts_made = sem("consts_made")
        masks_spread = sem("masks_spread")
        masks_made = sem("masks_made")
        pool_step = sem("pool_step")
        vector_step = sem("vector_step")
        scalar_step = sem("scalar_step")
        x_ready = sem("x_ready")
        std_ready = sem("std_ready")
        h_ready = sem("h_ready")
        mem_std = sem("mem_std")
        mem_ready = sem("mem_ready")
        mem_g_ready = sem("mem_g_ready")
        abs_ready = sem("abs_ready")
        softplus_ready = sem("softplus_ready")
        logf_ready = sem("logf_ready")
        cum_ready = sem("cum_ready")
        q_zeroed = sem("q_zeroed")
        conv_hist_loaded = sem("conv_hist_loaded")
        conv_norm_loaded = sem("conv_norm_loaded")
        u_stored = sem("u_stored")
        kv_stored = sem("kv_stored")
        mkv_stored = sem("mkv_stored")
        pmax_ready = sem("pmax_ready")
        smax_ready = sem("smax_ready")
        sexp_ready = sem("sexp_ready")
        conv_done = sem("conv_done")
        zvar_ready = sem("zvar_ready")
        zstd_ready = sem("zstd_ready")
        znorm_ready = sem("znorm_ready")
        oattn_ready = sem("oattn_ready")
        mstd_ready = sem("mstd_ready")
        xmax_ready = sem("xmax_ready")
        ff_mid_made = sem("ff_mid_made")
        ff_midT_made = sem("ff_midT_made")
        rmax_ready = sem("rmax_ready")
        rexp_ready = sem("rexp_ready")
        picks_ready = sem("picks_ready")
        items_ready = sem("items_ready")
        e_pick_ready = sem("expert_picks_ready")
        e_silu_ready = sem("expert_silu_ready")
        gfin_loaded = sem("gfin_loaded")
        hist_ready = sem("hist_ready")
        iota_made = sem("iota_made")
        out_ready = sem("out_ready")
        out_stored = sem("out_stored")

        units = []
        for l in range(DEPTH):
            units += [(("w_in", l, g), 1) for g in ("q", "k", "v", "gate", "value")]
            kv = [("K", l, 0), ("K", l, 1)]
            for p in range(1, PAIRS):
                kv += [("K", l, 2 * p), ("K", l, 2 * p + 1), ("V", l, 2 * p - 2), ("V", l, 2 * p - 1)]
            kv += [("V", l, DB - 2), ("V", l, DB - 1)]
            units += [(k, NPG) for k in kv]
            units += [(("w_ckv", l, 0), 1)]
            units += [(("w_out", l, g), 1) for g in range(2)]
            units += [(("w_ckv", l, 1), 1)]
            units += [(("w_cq", l), 1)]
            units += [(("mem_kv", l, b), 4) for b in range(0, DB, 2)]
            units += [(("w_co", l), 1)]
        unit_at, landed_at, per_slot = {}, {}, [0] * RING
        for n, (key, dmas) in enumerate(units):
            per_slot[n % RING] += 16 * dmas
            unit_at[key] = n
            landed_at[key] = per_slot[n % RING]

        jobs, per_bank = {}, [0] * 8
        freed_by = {}

        def filled(eng, key):
            bank, n = jobs[key]
            eng.wait_ge(bank_filled[bank], n + 1)
            return bank

        ff_bytes, ff_done = [0] * FF_RAW, {}
        for m in range(FF_HALVES):
            ff_bytes[m % FF_RAW] += 16 * (2 if m < FF_UP_HALVES else 1)
            ff_done[m] = ff_bytes[m % FF_RAW]

        def last_reader(l, s):
            return freed_by[units[max(n for n, u in enumerate(units) if n % RING == s and u[0][1] == l)][0]]

        def last_half_of_slot(s):
            return max(m for m in range(FF_HALVES)
                       if s in (FF_RAW_AT[m % FF_RAW] // 2, FF_HI_AT[m % FF_HI] // 2))

        def ff_half_read(eng, l, m):
            if m == FF_HALVES - 1:
                filled(eng, ("ff_out", l, 2, 1))
            elif m < FF_UP_HALVES and m % 2:
                filled(eng, (("ff", l, m // 2), 3))
            else:
                eng.wait_ge(ff_read, m // 2 + 1 if m < FF_UP_HALVES else m + 1 - NFG)

        e_plan = []
        for g in range(NEG_G):
            e_plan.append((("up", g), g % 2))
            if g == 1:
                e_plan.append((("giveT",), 2))
            if g:
                e_plan.append((("midT", g - 1), 2 + g % 2))
        e_plan += [(("midT", NEG_G - 1), 2 + NEG_G % 2), (("down", 0), 4), (("down", 1), 5),
                   (("take", 0), 6), (("take", 1), 7)]
        e_plan += [(("give", c, f), (0, 1, 2, 3, 6, 7)[2 * c + f]) for c in range(3) for f in range(2)]
        e_jobs, e_per = {}, [0] * 8
        for key, bank in e_plan:
            e_jobs[key] = (bank, e_per[bank])
            e_per[bank] += 1
        UP_HALVES = 2 * NEG_G
        HALVES = UP_HALVES + EF // 256
        assert HALVES % MOE_RING == 0 and HALVES % SPLIT == 0
        W_READS = NEG_G + EF // 256 - 1
        W_CREDIT = 2

        def e_filled_wait(eng, key, i):
            bank, n = e_jobs[key]
            eng.wait_ge(bank_filled[bank], i * e_per[bank] + (per_bank[bank] + n + 1))
            return bank

        e_bytes, e_done = [0] * MOE_RING, {}
        for m in range(HALVES):
            e_bytes[m % MOE_RING] += 16 * (2 if m < UP_HALVES else 1)
            e_done[m] = e_bytes[m % MOE_RING]
        COLUMN_STEPS = 4
        PICK_STEP = 17

        def half_read_wait(eng, i, m):
            if m < 0:
                i, m = i - 1, m + HALVES
            if m == HALVES - 1:
                e_filled_wait(eng, ("down", 1), i)
            elif m < UP_HALVES and m % 2:
                e_filled_wait(eng, ("up", m // 2), i)
            else:
                eng.wait_ge(w_read, i * W_READS + W_CREDIT + (m // 2 + 1 if m < UP_HALVES else m + 1 - NEG_G))

        def half_split_wait(eng, i, m):
            for s in w_lo_made:
                eng.wait_ge(s, i * HALVES + (m + 1))

        g_final = memT[:, 0:KD // 2, :].rearrange("p k t -> p (k t)")
        kv_waits, u_waits = 16 * (2 + 6), 16 * (1 + DB + 1)
        note2 = sb("note2", [P, 1])
        stat_at = {}

        def stat(key, n=1, rows=P):
            if key not in stat_at:
                used = sum(m for _, m in stat_at.values())
                assert used + n <= 512
                stat_at[key] = (used, n)
            at, m = stat_at[key]
            assert m == n
            return stats[0:rows, at:at + n]

        block = ctx.enter_context(nc.Block())

        @block.tensor
        def _(pe):
            used = [0]
            turn = [0]

            def job(key, bank):
                n = per_bank[bank]
                jobs[key] = (bank, n)
                per_bank[bank] = n + 1
                if n:
                    pe.wait_ge(bank_emptied[bank], n)
                return psum[bank]

            def emptied(*keys):
                for key in keys:
                    bank, n = jobs[key]
                    pe.wait_ge(bank_emptied[bank], n + 1)

            def unit(key):
                n = unit_at[key]
                if n == used[0]:
                    used[0] += 1
                    pe.wait_ge(slot_landed[n % RING], landed_at[key])
                assert n < used[0], (key, n, used[0])
                return ring[:, (n % RING) * SLOT:(n % RING + 1) * SLOT]

            def transposes(key, parts):
                turn[0] += 1
                bank = 6 + turn[0] % 2
                ps = job(key, bank)
                at = 0
                for a, rows in parts:
                    last = nc.tensor.transpose(ps[0:a.shape[1], at:at + rows], a, ident[0:rows, 0:rows])
                    at += rows
                last.then_inc(bank_filled[bank], 1)

            def product(out, pairs):
                for n, (a, b) in enumerate(pairs):
                    last = nc.tensor.matmul(out, a, b, start=(n == 0), stop=(n == len(pairs) - 1))
                return last

            def turn_rows(name, src, ready, first, halves=KD // 4):
                for c in range(3):
                    pe.wait_ge(ready, first + c + 1)
                    for f in range(halves):
                        transposes((name, c, f), [(src[0:ROWS[c], c, (4 * f + q) * P:(4 * f + q + 1) * P], ROWS[c])
                                                  for q in range(4)])

            def turn_stage(l, s):
                turn_rows(("hT", l, s), h, h_ready, 3 * STAGE_AT[(l, s)])

            def project(name, g, src, n_k, weights, chunks=range(3), stage=None):
                for c in chunks:
                    bank = 3 * (g % 2) + c
                    if stage and g == 0:
                        emptied(*[(stage, c, f) for f in range(n_k // 4)])
                    ps = job((name, c), bank)
                    last = product(ps[0:ROWS[c], :], [(src[:, k, COLS[c]], weights[:, k, :]) for k in range(n_k)])
                    last.then_inc(bank_filled[bank], 1)

            def split_product(out, a_hi, a_lo, b_hi, b_lo, start, stop):
                nc.tensor.matmul(out, a_hi, b_hi, start=start, stop=False)
                nc.tensor.matmul(out, a_hi, b_lo, start=False, stop=False)
                return nc.tensor.matmul(out, a_lo, b_hi, start=False, stop=stop)

            def project_columns(name, src, stage, weights, banks):
                emptied(*[(stage, c, f) for c in range(3) for f in range(KD // 4)])
                for j, bank in enumerate(banks):
                    ps = job((name, j), bank)
                    product(ps[:, 0:NTOK], [(weights[:, k, j * P:(j + 1) * P], src[:, k, :]) for k in range(KD)])\
                        .then_inc(bank_filled[bank], 1)

            def last_read(key, job_key):
                freed_by[key] = job_key

            pe.wait_ge(ident_made, 1)
            pe.wait_ge(rows_loaded, 16 * (12 + 4))
            transposes("gains", [(gain_rows[0:DEPTH * N_GAINS, :], DEPTH * N_GAINS)])
            transposes("conv_w", [(dw_rows[:, l, :], P) for l in range(DEPTH)])
            COLUMN_BANKS = {"q": (0, 1, 2, 3), "gate": (3, 4, 5, 7), "value": (0, 1, 2, 6)}
            for l in range(DEPTH):
                turn_stage(l, "mix")
                for g, part in enumerate(("q", "k", "v", "gate", "value")):
                    w = unit(("w_in", l, part)).rearrange("p (k n) -> p k n", k=KD)
                    if part == "value":
                        emptied(*[(("gate", l), j) for j in range(4)])
                    if part in COLUMN_BANKS:
                        project_columns((part, l), hT, ("hT", l, "mix"), w, COLUMN_BANKS[part])
                        last_read(("w_in", l, part), ((part, l), 3))
                    else:
                        project((part, l), g, hT, KD, w)
                        last_read(("w_in", l, part), ((part, l), 2))
                    if g == 0:
                        if l == 0:
                            pe.wait_ge(small_loaded, 16 * 6)
                        ps = job(("forget", l), 5)
                        for c in range(3):
                            last = product(ps[0:ROWS[c], c * NH:(c + 1) * NH],
                                           [(hT[:, k, COLS[c]], forget_w[:, l, k, :]) for k in range(KD)])
                        last.then_inc(bank_filled[5], 1)
                        if l == 0:
                            pe.wait_ge(consts_made, 1)
                            ps = job("masks", 0)
                            nc.tensor.matmul(ps[:, 0:2 * NS], spread8, small8[:, :, :, :].rearrange("t a b s -> t (a b s)"),
                                             start=True, stop=True).then_inc(bank_filled[0], 1)
                            ps = job("suffix", 1)
                            pe.wait_ge(decay_made, 1)
                            nc.tensor.matmul(ps[:, 0:NH], page_suffix, lf_sum[:, :, PAGE - 1],
                                             start=True, stop=True).then_inc(bank_filled[1], 1)
                            for c in range(2):
                                pe.wait_ge(mem_ready, c + 1)
                                for f in range(2):
                                    transposes(("memT", c, f), [(mem[:, c, (4 * f + q) * P:(4 * f + q + 1) * P], P) for q in range(4)])

                pe.wait_ge(logf_ready, l + 1)
                ps = job(("cumT", l), 0)
                product(ps[0:NH, 0:P], [(logf[:, 0, :], upto[:, :])])
                product(ps[0:NH, P:2 * P], [(logf[:, 0, :], ones[:, :]), (logf[:, 1, :], upto[:, :])])\
                    .then_inc(bank_filled[0], 1)
                ps = job(("cum_s", l), 1)
                product(ps[0:NS, 0:NH], [(block_upto[:, :], logf[0:NS, 2, :])]).then_inc(bank_filled[1], 1)
                for c in range(3):
                    emptied((("k", l), c), (("v", l), c))
                    transposes(("kT", l, c), [(qkv[0:ROWS[c], c, AW + j * P:AW + (j + 1) * P], ROWS[c]) for j in range(4)])
                emptied(*[(("value", l), j) for j in range(4)])
                for c in (1, 2):
                    turn[0] += 1
                    bank = 6 + turn[0] % 2
                    ps = job(("u_rows", l, c), bank)
                    for j in range(4):
                        a = up[:, j, HIST + P:HIST + 2 * P] if c == 1 else uT[:, j, SEQ:NTOK]
                        last = nc.tensor.transpose(ps[0:ROWS[c], j * P:(j + 1) * P], a, ident[:, :])
                    last.then_inc(bank_filled[bank], 1)
                pe.wait_ge(conv_hist_loaded, 32 * (l + 1))
                for b in range(2):
                    transposes(("histT", l, b), [(hist_in[0:4 * HIST, b, j * P:(j + 1) * P], 4 * HIST) for j in range(4)])
                pe.wait_ge(cum_ready, l + 1)
                ps = job(("own_cum", l), 2)
                for b2 in range(2):
                    last = product(ps[b2 * NS:(b2 + 1) * NS, 0:PAIRS],
                                   [(cum_rows[:, :, :].rearrange("p h t -> p (h t)"), batch_of[:, b2:DB:2])])
                last.then_inc(bank_filled[2], 1)

                if l == 0:
                    pe.wait_ge(masks_made, 1)
                    pe.wait_ge(decay_loaded, 16 * 2 * DB)
                emptied(*[(("q", l), j) for j in range(4)], *[("kT", l, c) for c in range(2)], ("cumT", l))
                n = 0
                for i in range(2):
                    keys = (i + 1) * P
                    per = 512 // keys
                    for g in range(NH // per):
                        bank = 3 + n % 3
                        ps = job(("scores", l, i, g), bank)
                        for a in range(per):
                            hd = g * per + a
                            pick = ident[0:NH, hd:hd + 1]
                            last = product(ps[:, a * keys:(a + 1) * keys],
                                           [(q_heads[:, hd, i * P:(i + 1) * P], kT[:, hd // 2, 0:keys]),
                                            (pick.to_broadcast([NH, P]), neg_cumT[:, 0:keys]),
                                            (cumT[:, i * P:(i + 1) * P], pick.to_broadcast([NH, keys]))])
                        last.then_inc(bank_filled[bank], 1)
                        n += 1
                turns = [(i, t) for i in range(2) for t in range(2 * (i + 1))]
                for n in range(len(turns) + 1):
                    if n < len(turns):
                        i, t = turns[n]
                        emptied(("scores", l, i, t))
                        if i == 0:
                            parts = [(p_prompt[0][:, 4 * t + a, :], P) for a in range(4)]
                        else:
                            parts = [(p_prompt[1][:, 2 * t + a, kk * P:(kk + 1) * P], P) for a in range(2) for kk in range(2)]
                        transposes(("pT", l, n), parts)
                    if n:
                        i, t = turns[n - 1]
                        emptied(("pT", l, n - 1))
                        if t == 0:
                            ps = job(("o_prompt", l, i), 1 + i)
                        at = 4 * ((n - 1) % 2)
                        per = 4 // (i + 1)
                        for a in range(per):
                            hd = t * per + a
                            last = product(ps[:, hd * DH:(hd + 1) * DH],
                                           [(PT[:, at + a * (i + 1) + kk, :], qkv[:, kk, 2 * AW + hd * DH:2 * AW + (hd + 1) * DH])
                                            for kk in range(i + 1)])
                        if t == 2 * (i + 1) - 1:
                            last.then_inc(bank_filled[1 + i], 1)

                def key_columns(l, n):
                    b, half = n // 2, n % 2
                    K = unit(("K", l, b)).rearrange("p (g n) -> p g n", g=NPG)
                    for pg in range(4 * half, 4 * half + 4):
                        transposes(("KT", l, b, pg), [(K[:, pg, j * P:(j + 1) * P], P) for j in range(4)])
                    last_read(("K", l, b), ("KT", l, b, NPG - 1))

                def past_scores(l, n):
                    b, half = n // 2, n % 2
                    p, b2 = b // 2, b % 2
                    rows = slice(b2 * NS, (b2 + 1) * NS)
                    if b2 == 0:
                        job(("past", l, p, half), half)
                    emptied(*[("KT", l, b, pg) for pg in range(4 * half, 4 * half + 4)])
                    last = product(psum[half][rows, :],
                                   [(q_rows[:, j, b, :], KT[:, n % 2, j, :]) for j in range(4)]
                                   + [(decay_rows[:, l, b, :],
                                       past_decay[:, half * 512:(half + 1) * 512])])
                    if b2 == 1:
                        last.then_inc(bank_filled[half], 1)

                def new_scores(l, p):
                    ps = job(("new", l, p), 2)
                    for b2 in range(2):
                        last = product(ps[b2 * NS:(b2 + 1) * NS, 0:NS],
                                       [(q_rows[:, j, 2 * p + b2, :], kT[:, j, SEQ:NTOK]) for j in range(4)]
                                       + [(neg_cum_rows[:, :, :].rearrange("p h t -> p (h t)"), ident[0:NS, 0:NS])])
                    last.then_inc(bank_filled[2], 1)

                def probs_columns(l, p):
                    pe.wait_ge(sexp_ready, PAIRS * l + p + 1)
                    for t in range(2):
                        transposes(("PT", l, p, t), [(probs[:, (4 * t + q) * P:(4 * t + q + 1) * P], P) for q in range(4)])
                    transposes(("PT", l, p, 2), [(probs[:, PAST:PAST + NS], P)])

                def weigh_values(l, p):
                    emptied(*[("PT", l, p, t) for t in range(3)])
                    ps = job(("o_pair", l, p), 3)
                    for b2 in range(2):
                        V = unit(("V", l, 2 * p + b2)).rearrange("p (g n) -> p g n", g=NPG)
                        rows = slice(b2 * NS, (b2 + 1) * NS)
                        last = product(ps[rows, :], [(PT[:, pg, rows], V[:, pg, :]) for pg in range(NPG)]
                                       + [(PT[0:NS, 8, rows], qkv[0:NS, 2, 2 * AW:3 * AW])])
                        if b2 == 1:
                            last.then_inc(bank_filled[3], 1)
                        last_read(("V", l, 2 * p + b2), ("o_pair", l, p))

                def gather_rows(l, p):
                    emptied(("o_pair", l, p))
                    if p == 0:
                        job(("o_sample", l), 4)
                    last = nc.tensor.matmul(psum[4][0:NS, :], pair_rows[:, p, :], o_masked[:, :],
                                            start=(p == 0), stop=(p == PAIRS - 1))
                    if p == PAIRS - 1:
                        last.then_inc(bank_filled[4], 1)

                emptied(("kT", l, 2))
                key_columns(l, 0)
                for p in range(PAIRS + 1):
                    if p < PAIRS:
                        for n in range(4 * p, 4 * p + 4):
                            if n % 4 == 2:
                                if p:
                                    probs_columns(l, p - 1)
                                new_scores(l, p)
                            if n + 1 < 4 * p + 4:
                                key_columns(l, n + 1)
                            past_scores(l, n)
                        if p + 1 < PAIRS and p == 0:
                            key_columns(l, 4)
                    else:
                        probs_columns(l, p - 1)
                    if p:
                        if p >= 2:
                            gather_rows(l, p - 2)
                        weigh_values(l, p - 1)
                        if p + 1 < PAIRS:
                            key_columns(l, 4 * (p + 1))
                gather_rows(l, PAIRS - 1)

                pe.wait_ge(conv_done, l + 1)
                for c in range(3):
                    turn[0] += 1
                    bank = 6 + turn[0] % 2
                    ps = job(("z", l, c), bank)
                    for j in range(4):
                        last = nc.tensor.transpose(ps[0:ROWS[c], j * P:(j + 1) * P], conv_z[:, j, COLS[c]], ident[:, :])
                    last.then_inc(bank_filled[bank], 1)
                def memory_projection(g):
                    w = unit(("w_ckv", l, g)).rearrange("p (k n) -> p k n", k=KD)
                    project(("mkv", l, g), g, mem_g, KD, w, chunks=range(2))
                    last_read(("w_ckv", l, g), (("mkv", l, g), 1))

                pe.wait_ge(mem_g_ready, l + 1)
                memory_projection(0)
                turn_stage(l, "merged")
                for g in range(2):
                    w = unit(("w_out", l, g)).rearrange("p (k n) -> p k n", k=KD)
                    project(("out", l, g), g, hT, KD, w, stage=("hT", l, "merged"))
                    last_read(("w_out", l, g), (("out", l, g), 2))

                memory_projection(1)
                turn_stage(l, "cross")
                w = unit(("w_cq", l)).rearrange("p (k n) -> p k n", k=KD)
                project_columns(("xq", l), hT, ("hT", l, "cross"), w, (0, 1, 2, 3))
                last_read(("w_cq", l), (("xq", l), 3))
                for m in range(2):
                    emptied((("mkv", l, 0), m), (("mkv", l, 1), m))
                    transposes(("mkT", l, m), [(mkv[:, m, j * P:(j + 1) * P], P) for j in range(XH)])

                def memory_columns(l, b):
                    kv = unit(("mem_kv", l, b - b % 2)).rearrange("p (s n) -> p s n", s=8)
                    for m in range(2):
                        transposes(("xKT", l, b, m), [(kv[:, 4 * (b % 2) + m, j * P:(j + 1) * P], P) for j in range(XH)])

                memory_columns(l, 0)
                emptied(*[(("xq", l), j) for j in range(XH)])
                for b in range(DB):
                    if b + 1 < DB:
                        memory_columns(l, b + 1)
                    quad, b4 = b // 4, b % 4
                    if b4 == 0:
                        job(("xs", l, quad), quad)
                    emptied(("xKT", l, b, 0), ("xKT", l, b, 1))
                    last = product(psum[quad][32 * b4:32 * b4 + 32, 0:NMEM],
                                   [(xq_rows[:, j, b, :], xKT[:, b % 2, j, :]) for j in range(XH)])
                    if b4 == 3:
                        last.then_inc(bank_filled[quad], 1)
                emptied(("mkT", l, 0), ("mkT", l, 1))
                for i in range(2):
                    for g in range(2):
                        bank = 2 + (2 * i + g) % 4
                        ps = job(("xscores", l, i, g), bank)
                        for a in range(2):
                            last = product(ps[:, a * NMEM:(a + 1) * NMEM],
                                           [(xqT[:, 2 * g + a, i * P:(i + 1) * P], mkT[:, 2 * g + a, :])])
                        last.then_inc(bank_filled[bank], 1)
                for quad in range(QUADS):
                    emptied(("xs", l, quad))
                    transposes(("xPT", l, quad), [(xp[:, quad, m * P:(m + 1) * P], P) for m in range(2)])
                for b in range(DB):
                    quad, b4 = b // 4, b % 4
                    if b4 == 0:
                        emptied(("xPT", l, quad))
                        job(("xo_quad", l, quad), quad)
                    if b % 2 == 0:
                        kv = unit(("mem_kv", l, b)).rearrange("p (s n) -> p s n", s=8)
                    last = product(psum[quad][32 * b4:32 * b4 + 32, :],
                                   [(xPT[:, quad, m, 32 * b4:32 * b4 + 32], kv[:, 4 * (b % 2) + 2 + m, :]) for m in range(2)])
                    if b4 == 3:
                        last.then_inc(bank_filled[quad], 1)
                    last_read(("mem_kv", l, b - b % 2), ("xo_quad", l, quad))
                for n in range(5):
                    if n < 4:
                        i, g = n // 2, n % 2
                        emptied(("xscores", l, i, g))
                        transposes(("xpT", l, n), [(xp_prompt[:, i, 2 * g + a, m * P:(m + 1) * P], P)
                                                   for a in range(2) for m in range(2)])
                    if n:
                        i, g = (n - 1) // 2, (n - 1) % 2
                        emptied(("xpT", l, n - 1), (("mkv", l, 1), 0), (("mkv", l, 1), 1))
                        if g == 0:
                            ps = job(("xo_prompt", l, i), 2 + i)
                        for a in range(2):
                            hd = 2 * g + a
                            last = product(ps[:, hd * P:(hd + 1) * P],
                                           [(xPT[:, 2 + (n - 1) % 2, 2 * a + m, :], mkv[:, m, XW + hd * P:XW + (hd + 1) * P])
                                            for m in range(2)])
                        if g == 1:
                            last.then_inc(bank_filled[2 + i], 1)
                job(("xo_sample", l), 4)
                emptied(("xo_quad", l, 0), ("xo_quad", l, 1))
                product(psum[4][0:NS, :], [(quad_rows[:, q, :], xo_masked[:, q, :]) for q in range(QUADS)])\
                    .then_inc(bank_filled[4], 1)
                for c in range(3):
                    emptied(("xo_prompt", l, c) if c < 2 else ("xo_sample", l))
                    transposes(("xoT", l, c), [(xo[0:ROWS[c], c, j * P:(j + 1) * P], ROWS[c]) for j in range(XH)])
                w = unit(("w_co", l)).rearrange("p (k n) -> p k n", k=XH)
                emptied(*[("xoT", l, c) for c in range(3)])
                for g in range(2):
                    project(("co", l, g), g, hT, XH, w[:, :, g * 512:(g + 1) * 512])
                last_read(("w_co", l), (("co", l, 1), 2))

                turn_stage(l, "ffn")
                if l % 2 == 0:
                    def ff_half(m, n):
                        pe.wait_ge(ff_lo_made, m + 1)
                        return [t[:, :].rearrange("p (k n) -> p k n", k=n) for t in (ff_hi[m % FF_HI], ff_lo[m % FF_RAW])]

                    emptied(*[(("hT", l, "ffn"), c, 0) for c in range(3)])
                    for g in range(NFG):
                        for half in range(2):
                            if g == 0 and half:
                                emptied(*[(("hT", l, "ffn"), c, 1) for c in range(3)])
                            hi, lo = ff_half(2 * g + half, 4)
                            for j in range(4):
                                bank = 4 * (g % 2) + j
                                cols = slice(j * P, (j + 1) * P)
                                if half == 0:
                                    job((("ff", l, g), j), bank)
                                for q in range(4):
                                    k = 4 * half + q
                                    last = split_product(psum[bank][:, 0:NTOK], hi[:, q, cols], lo[:, q, cols],
                                                         hT_hi[:, k, :], hT_lo[:, k, :], k == 0, k == KD - 1)
                                if half:
                                    last.then_inc(bank_filled[bank], 1)
                            if half == 0:
                                last.then_inc(ff_read, 1)
                    for m in range(FF_UP_HALVES, FF_HALVES):
                        hi, lo = ff_half(m, 2)
                        pe.wait_ge(ff_midT_made, m - FF_UP_HALVES + 1)
                        for q in range(2):
                            k = 2 * (m - FF_UP_HALVES) + q
                            for c in range(3):
                                for f in range(2):
                                    cols = slice(f * 512, (f + 1) * 512)
                                    bank = FF_OUT_BANK[2 * c + f]
                                    if k == 0:
                                        job(("ff_out", l, c, f), bank)
                                    last = split_product(psum[bank][:, :], midT_hi[:, k, PART_WIDE[c]], midT_lo[:, k, PART_WIDE[c]],
                                                         hi[:, q, cols], lo[:, q, cols], k == 0, k == FF // P - 1)
                                    if k == FF // P - 1:
                                        last.then_inc(bank_filled[bank], 1)
                        if m < FF_HALVES - 1:
                            last.then_inc(ff_read, 1)
                    continue

                emptied(*[(("hT", l, "ffn"), c, f) for c in range(3) for f in range(2)])
                ps = job("router", 0)
                for c in range(3):
                    last = product(ps[0:ROWS[c], c * NE:(c + 1) * NE],
                                   [(hT[:, k, COLS[c]], router_w[:, k, :]) for k in range(KD)])
                    if c < W_CREDIT:
                        last.then_inc(w_read, 1)
                last.then_inc(bank_filled[0], 1)
                pe.wait_ge(picks_ready, 1)
                chosen = route[5]
                ps = job("ranks", 1)
                for c in range(3):
                    last = product(ps[:, c * NE:(c + 1) * NE],
                                   [(ones[:, :], chosen[:, c2, :]) for c2 in range(c)] + [(before[:, :], chosen[:, c, :])])
                last = product(ps[:, 3 * NE:4 * NE], [(ones[:, :], chosen[:, c, :]) for c in range(3)])
                last.then_inc(bank_filled[1], 1)

            def take(ps, f):
                for q in range(4):
                    k = 4 * f + q
                    last = product(ps[:, q * P:(q + 1) * P],
                                   [(h[0:ROWS[c], c, k * P:(k + 1) * P], e_pick[0:ROWS[c], c, :]) for c in range(3)])
                last.then_inc(bank_filled[6 + f], 1)

            pe.wait_ge(e_pick_ready, 1)
            for f in range(2):
                take(job(("first_take", f), 6 + f), f)

            pe.wait_ge(items_ready, 1)
            n_items = pe.value_load(items[0:1, 0:1], min_val=NE, max_val=MAX_ITEMS)
            with pe.Fori(0, n_items) as i:
                def e_job(key):
                    bank, n = e_jobs[key]
                    pe.wait_ge(bank_emptied[bank], i * e_per[bank] + (per_bank[bank] + n))
                    return psum[bank]

                def e_emptied_wait(key):
                    bank, n = e_jobs[key]
                    pe.wait_ge(bank_emptied[bank], i * e_per[bank] + (per_bank[bank] + n + 1))

                def split_half(m, n):
                    half_split_wait(pe, i, m)
                    return [t[m % SPLIT][:, :].rearrange("p (k n) -> p k n", k=n) for t in (w_hi, w_lo)]

                def turn_e_mid(g):
                    e_emptied_wait(("up", g))
                    ps = e_job(("midT", g))
                    for j in range(2):
                        last = nc.tensor.transpose(ps[:, j * P:(j + 1) * P], e_mid[:, g % 2, j * P:(j + 1) * P], ident[:, :])
                    last.then_inc(bank_filled[e_jobs[("midT", g)][0]], 1)

                pe.wait_ge(xT_ready, i + 1)
                for g in range(NEG_G):
                    ps = e_job(("up", g))
                    for half in range(2):
                        hi, lo = split_half(2 * g + half, 4)
                        for q in range(4):
                            k = 4 * half + q
                            last = split_product(ps[:, :], e_xT_hi[:, k, :], e_xT_lo[:, k, :], hi[:, q, :], lo[:, q, :],
                                                 k == 0, k == KD - 1)
                        last.then_inc(bank_filled[g % 2] if half else w_read, 1)
                    if g == 1:
                        ps = e_job(("giveT",))
                        for c in range(3):
                            last = nc.tensor.transpose(ps[:, c * P:c * P + ROWS[c]], e_give[0:ROWS[c], c, :],
                                                       ident[0:ROWS[c], 0:ROWS[c]])
                        last.then_inc(bank_filled[2], 1)
                    if g:
                        turn_e_mid(g - 1)
                e_job(("down", 0))
                e_job(("down", 1))
                for m in range(UP_HALVES, HALVES):
                    hi, lo = split_half(m, 2)
                    e_emptied_wait(("midT", m - UP_HALVES))
                    for q in range(2):
                        k = 2 * (m - UP_HALVES) + q
                        for f in range(2):
                            cols = slice(f * 512, (f + 1) * 512)
                            last = split_product(psum[4 + f][:, :], e_midT_hi[:, k, :], e_midT_lo[:, k, :],
                                                 hi[:, q, cols], lo[:, q, cols], k == 0, k == EF // P - 1)
                            if k == EF // P - 1:
                                last.then_inc(bank_filled[4 + f], 1)
                    if m < HALVES - 1:
                        last.then_inc(w_read, 1)
                    if m == UP_HALVES:
                        turn_e_mid(NEG_G - 1)
                pe.wait_ge(e_pick_ready, i + 2)
                for f in range(2):
                    take(e_job(("take", f)), f)
                e_emptied_wait(("giveT",))
                for f in range(2):
                    e_emptied_wait(("down", f))
                    for c in range(3):
                        ps = e_job(("give", c, f))
                        nc.tensor.matmul(ps[0:ROWS[c], :], e_giveT[:, c, 0:ROWS[c]], e_y[:, f, :], start=True, stop=True)\
                            .then_inc(bank_filled[e_jobs[("give", c, f)][0]], 1)


        @block.vector
        def _(dve):
            steps, told = [0], [0]

            def mark(ins):
                steps[0] += 1
                ins.then_inc(vector_step, 1)
                return steps[0]

            def link(ins):
                dve.wait_ge(vector_step, mark(ins))

            def tell(s):
                told[0] += 1
                nc.vector.memset(note[:, told[0] % 16:told[0] % 16 + 1], 0.0).then_inc(s, 1)

            V = nc.vector

            def wide(a, *shape):
                return a.unsqueeze(2).to_broadcast(list(shape))

            dve.wait_ge(idx_loaded, 32)
            V.tensor_scalar(page_idx[NS:P, :], page_idx[NS:P, :], float(N_PHYS), None, ALU.add).then_inc(idx_ready, 1)
            dve.wait_ge(ident_made, 1)
            V.tensor_reduce(step_of[:, :], ident[0:NS, 0:NS].rearrange("p (b t) -> p t b", b=DB), AX.X, ALU.add)
            V.tensor_reduce(batch_of[:, :], ident[0:NS, 0:NS].rearrange("p (b t) -> p b t", b=DB), AX.X, ALU.add)
            bank = filled(dve, "gains")
            V.tensor_copy(gains[:, :], psum[bank][:, 0:DEPTH * N_GAINS]).then_inc(bank_emptied[bank], 1)
            bank = filled(dve, "conv_w")
            V.tensor_copy(conv_w[:, :, :], psum[bank][:, 0:DEPTH * P].rearrange("p (l r) -> p l r", l=DEPTH))\
                .then_inc(bank_emptied[bank], 1)
            def norm_rows(l, s):
                n = NORM_AT[(l, s)]
                for c in range(3):
                    r = ROWS[c]
                    dve.wait_ge(std_ready, 3 * n + c + 1)
                    link(V.reciprocal(stat(("rstd", n, c), rows=r), stat(("std", n, c), rows=r)))
                    V.tensor_scalar(h[0:r, c, :], x[0:r, c, :], stat(("rstd", n, c), rows=r), None, ALU.mult)\
                        .then_inc(h_ready, 1)
                if s == "ffn" and l % 2 == 0:
                    split_columns(l)
                else:
                    gained_columns(l, s)

            def split_columns(l):
                g0 = l * N_GAINS + GAIN_AT["ffn"]
                for c in range(3):
                    for f in range(2):
                        bank = filled(dve, (("hT", l, "ffn"), c, f))
                        ps = psum[bank][:, 0:4 * ROWS[c]].rearrange("p (k t) -> p k t", k=4)
                        link(V.tensor_tensor(ps, ps, wide(gains[:, g0 + 4 * f:g0 + 4 * f + 4], P, 4, ROWS[c]), ALU.mult))
                        link(V.tensor_copy(hT_hi[:, 4 * f:4 * f + 4, PART_COLS[c]], ps))
                        V.tensor_tensor(hT_lo[:, 4 * f:4 * f + 4, PART_COLS[c]], ps,
                                        hT_hi[:, 4 * f:4 * f + 4, PART_COLS[c]].bitcast(F32), ALU.subtract)\
                            .then_inc(bank_emptied[bank], 1)

            def gained_columns(l, s):
                g0 = l * N_GAINS + GAIN_AT[s]
                for c in range(3):
                    for f in range(2):
                        bank = filled(dve, (("hT", l, s), c, f))
                        V.tensor_tensor(hT[:, 4 * f:4 * f + 4, COLS[c]],
                                        psum[bank][:, 0:4 * ROWS[c]].rearrange("p (k t) -> p k t", k=4),
                                        wide(gains[:, g0 + 4 * f:g0 + 4 * f + 4], P, 4, ROWS[c]), ALU.mult)\
                            .then_inc(bank_emptied[bank], 1)

            def add_to_x(key, c, f):
                bank = filled(dve, key)
                r = ROWS[c]
                xs = x[0:r, c, f * 512:(f + 1) * 512]
                V.tensor_tensor(xs, xs, psum[bank][0:r, :], ALU.add).then_inc(bank_emptied[bank], 1)

            def make_picks(ranks, gates):
                for c in range(3):
                    r = ROWS[c]
                    V.tensor_scalar(e_pick[0:r, c, :], iota_row[0:r, :], ranks[0:r, c, :], None, ALU.is_equal)
                    V.tensor_scalar(e_give[0:r, c, :], iota_row[0:r, :], ranks[0:r, c, :], gates[0:r, c, :],
                                    ALU.is_equal, ALU.mult)
                tell(e_pick_ready)

            def split_taken(bank, f, steps_before):
                g0 = (DEPTH - 1) * N_GAINS + GAIN_AT["ffn"] + 4 * f
                ks = slice(4 * f, 4 * f + 4)
                ps = psum[bank][:, :].rearrange("p (k t) -> p k t", k=4)
                V.tensor_tensor(ps, ps, wide(gains[:, g0:g0 + 4], P, 4, P), ALU.mult).then_inc(column_step, 1)
                dve.wait_ge(column_step, steps_before + (2 * f + 1))
                V.tensor_copy(e_xT_hi[:, ks, :], ps).then_inc(column_step, 1)
                dve.wait_ge(column_step, steps_before + (2 * f + 2))
                V.tensor_tensor(e_xT_lo[:, ks, :], ps, e_xT_hi[:, ks, :].bitcast(F32), ALU.subtract)\
                    .then_inc(bank_emptied[bank], 1)

            for l in range(DEPTH):
                norm_rows(l, "mix")
                dve.wait_ge(q_zeroed, 2 * l + 1)
                for j in range(4):
                    bank = filled(dve, (("q", l), j))
                    for a in range(2):
                        rows, hd = slice(64 * a, 64 * a + 64), 2 * j + a
                        V.tensor_scalar(q_heads[rows, hd, :], psum[bank][rows, 0:SEQ], Q_SCALE, None, ALU.mult)
                        last = V.tensor_scalar(q_rows[rows, j, :, hd * DS:(hd + 1) * DS],
                                               psum[bank][rows, SEQ:NTOK].rearrange("p (b t) -> p b t", b=DB),
                                               Q_SCALE, None, ALU.mult)
                    last.then_inc(bank_emptied[bank], 1)
                bank = filled(dve, ("forget", l))
                parts = [(P, slice(0, 2), 2), (NS, slice(2, 3), 1)]
                for r, cs, n in parts:
                    pf = psum[bank][0:r, 0:3 * NH].rearrange("p (c n) -> p c n", c=3)[:, cs, :]
                    bias = forget_b[0:r, l, :].unsqueeze(1).to_broadcast([r, n, NH])
                    link(V.tensor_tensor(logf[0:r, cs, :], pf, bias, ALU.add))
                    last = V.scalar_tensor_tensor(out=log_tmp[0:r, 0, cs, :], in0=logf[0:r, cs, :], scalar=-1.0,
                                                  in1=logf[0:r, cs, :], op0=ALU.mult, op1=ALU.max)
                last.then_inc(bank_emptied[bank], 1)
                tell(abs_ready)
                if l == 0:
                    dve.wait_ge(consts_made, 1)
                    bank = filled(dve, "masks")
                    V.tensor_copy(new_mask[:, :, :], psum[bank][:, 0:NS].unsqueeze(1).to_broadcast([P, PAIRS, NS]))
                    V.tensor_copy(pair_rows[:, :, :], psum[bank][:, NS:2 * NS].unsqueeze(1).to_broadcast([P, PAIRS, NS]))
                    V.tensor_copy(quad_rows[:, :, :], psum[bank][:, NS:2 * NS].unsqueeze(1).to_broadcast([P, QUADS, NS]))\
                        .then_inc(bank_emptied[bank], 1)
                    tell(masks_spread)
                    dve.wait_ge(pages_gathered, 16)
                    for hd in range(NH):
                        V.tensor_tensor_scan(lf_sum[:, hd, :], ones[:, :], lf_pages[:, :, hd], 0.0, ALU.mult, ALU.add)
                    tell(decay_made)
                    bank = filled(dve, "suffix")
                    suffix = stat("suffix", NH)
                    link(V.tensor_copy(suffix, psum[bank][:, 0:NH]))
                    V.tensor_tensor(lf_decay[:, :, :], wide(suffix, P, NH, PAGE), lf_sum[:, :, :], ALU.subtract)\
                        .then_inc(bank_emptied[bank], 1)
                    tell(decay_made)
                    for c in range(2):
                        dve.wait_ge(mem_std, c + 1)
                        link(V.reciprocal(stat(("mem_rstd", c)), stat(("mem_std", c))))
                        V.tensor_scalar(mem[:, c, :], mem[:, c, :], stat(("mem_rstd", c)), None, ALU.mult).then_inc(mem_ready, 1)
                dve.wait_ge(softplus_ready, l + 1)
                for r, cs, n in parts:
                    last = V.scalar_tensor_tensor(out=logf[0:r, cs, :], in0=logf[0:r, cs, :], scalar=0.0,
                                                  in1=log_tmp[0:r, 1, cs, :], op0=ALU.min, op1=ALU.subtract)
                last.then_inc(logf_ready, 1)
                for j in range(4):
                    bank = filled(dve, (("value", l), j))
                    V.tensor_tensor(up[:, j, HIST:HIST + SEQ], psum[bank][:, 0:SEQ], uT[:, j, 0:SEQ], ALU.mult)
                    V.tensor_tensor(us[:, j, :, HIST:HIST + DS], psum[bank][:, SEQ:NTOK].rearrange("p (b t) -> p b t", b=DB),
                                    uT[:, j, SEQ:NTOK].rearrange("p (b t) -> p b t", b=DB), ALU.mult)
                    V.tensor_tensor(uT[:, j, SEQ:NTOK], psum[bank][:, SEQ:NTOK], uT[:, j, SEQ:NTOK], ALU.mult)\
                        .then_inc(bank_emptied[bank], 1)
                bank = filled(dve, ("cumT", l))
                V.tensor_copy(cumT[:, :], psum[bank][0:NH, 0:SEQ])
                V.tensor_scalar(neg_cumT[:, :], psum[bank][0:NH, 0:SEQ], -1.0, None, ALU.mult).then_inc(bank_emptied[bank], 1)
                bank = filled(dve, ("cum_s", l))
                link(V.tensor_copy(cum_s[:, :], psum[bank][0:NS, 0:NH]))
                V.tensor_tensor(cum_rows[:, :, :], wide(cum_s[:, :], NS, NH, DS),
                                step_of[:, :].unsqueeze(1).to_broadcast([NS, NH, DS]), ALU.mult)
                V.tensor_scalar(neg_cum_rows[:, :, :], wide(cum_s[:, :], NS, NH, DS), -1.0, None, ALU.mult)\
                    .then_inc(bank_emptied[bank], 1)
                tell(cum_ready)
                for c in (1, 2):
                    bank = filled(dve, ("u_rows", l, c))
                    V.tensor_copy(u[0:ROWS[c], c, :], psum[bank][0:ROWS[c], :]).then_inc(bank_emptied[bank], 1)
                bank = filled(dve, ("own_cum", l))
                V.tensor_copy(own_cum[:, :], psum[bank][:, 0:PAIRS]).then_inc(bank_emptied[bank], 1)

                for i in range(2):
                    keys = (i + 1) * P
                    per = 512 // keys
                    for g in range(NH // per):
                        bank = filled(dve, ("scores", l, i, g))
                        s3 = psum[bank][:, :].rearrange("p (a k) -> p a k", a=per)
                        own = s3[:, :, i * P:(i + 1) * P]
                        link(V.tensor_tensor(own, own, causal[:, :].unsqueeze(1).to_broadcast([P, per, P]), ALU.add))
                        top = stat(("pmax", l, i, g), per)
                        link(V.tensor_reduce(top, s3, AX.X, ALU.max))
                        V.tensor_scalar(stat(("pbias", l, i, g), per), top, -1.0, None, ALU.mult).then_inc(pmax_ready, 1)
                for i in range(2):
                    bank = filled(dve, ("o_prompt", l, i))
                    per = 4 // (i + 1)
                    for g in range(NH // per):
                        last = V.reciprocal(stat(("pinv", l, i), NH)[:, g * per:(g + 1) * per], stat(("psum", l, i, g), per))
                    link(last)
                    V.tensor_tensor(h[:, i, 0:AW].rearrange("p (a k) -> p a k", a=NH),
                                    psum[bank][:, :].rearrange("p (a k) -> p a k", a=NH),
                                    wide(stat(("pinv", l, i), NH), P, NH, DH), ALU.mult).then_inc(bank_emptied[bank], 1)
                tell(oattn_ready)

                def taps(first, end):
                    if first == 0:
                        bank = filled(dve, ("histT", l, 1))
                        dve.wait_ge(hist_ready, l + 1)
                    for tap in range(first, end):
                        for j in range(4):
                            w = conv_w[:, l, 4 * tap + j:4 * tap + j + 1]
                            for src, dst in ((up[:, j, tap:tap + SEQ], conv_z[:, j, 0:SEQ]),
                                             (us[:, j, :, tap:tap + DS],
                                              conv_z[:, j, SEQ:NTOK].rearrange("p (b t) -> p b t", b=DB))):
                                if tap == 0:
                                    mark(V.tensor_scalar(dst, src, w, conv_w[:, l, 4 * CONV_K + j:4 * CONV_K + j + 1],
                                                         ALU.mult, ALU.add))
                                else:
                                    dve.wait_ge(vector_step, steps[0] - 7)
                                    mark(V.scalar_tensor_tensor(out=dst, in0=src, scalar=w, in1=dst,
                                                                op0=ALU.mult, op1=ALU.add))
                    if end == CONV_K:
                        tell(conv_done)

                cuts = [0, 5, 10, 14, 18, 21, 24, 28, 31]

                def row_maxima(p):
                    top = stat(("smax", l, p), 3)
                    for half in range(2):
                        bank = filled(dve, ("past", l, p, half))
                        V.tensor_reduce(top[:, half:half + 1], psum[bank][:, :], AX.X, ALU.max)
                    bank = filled(dve, ("new", l, p))
                    link(V.tensor_tensor(probs[:, PAST:PAST + NS], psum[bank][:, 0:NS], new_mask[:, p, :], ALU.add))
                    link(V.tensor_reduce(top[:, 2:3], probs[:, PAST:PAST + NS], AX.X, ALU.max))
                    m = stat(("stop", l, p), 2)
                    link(V.tensor_reduce(m[:, 0:1], top, AX.X, ALU.max))
                    link(V.tensor_tensor(m[:, 1:2], m[:, 0:1], own_cum[:, p:p + 1], ALU.add))
                    V.tensor_tensor(stat(("sbias", l, p)), own_cum[:, p:p + 1], m[:, 1:2], ALU.subtract)\
                        .then_inc(bank_emptied[bank], 1)
                    tell(smax_ready)

                def own_heads(p):
                    dve.wait_ge(sexp_ready, PAIRS * l + p + 1)
                    link(V.tensor_reduce(stat(("ssum1", l, p)), stat(("ssum", l, p), 3), AX.X, ALU.add))
                    link(V.reciprocal(stat(("sinv", l, p)), stat(("ssum1", l, p))))
                    bank = filled(dve, ("o_pair", l, p))
                    V.scalar_tensor_tensor(out=o_masked.rearrange("p (a k) -> p a k", a=NH),
                                           in0=psum[bank][:, :].rearrange("p (a k) -> p a k", a=NH),
                                           scalar=stat(("sinv", l, p)), in1=wide(own_head[:, :], P, NH, DH),
                                           op0=ALU.mult, op1=ALU.mult).then_inc(bank_emptied[bank], 1)

                for p in range(PAIRS + 1):
                    if p < PAIRS:
                        taps(cuts[2 * p], cuts[2 * p + 1])
                        row_maxima(p)
                        taps(cuts[2 * p + 1], cuts[2 * p + 2])
                    else:
                        dve.wait_ge(kv_stored, kv_waits * (l + 1))
                        g0 = l * N_GAINS + GAIN_AT["mem"]
                        V.tensor_tensor(mem_g, memT[:, :, :], wide(gains[:, g0:g0 + KD], P, KD, NMEM), ALU.mult)\
                            .then_inc(mem_g_ready, 1)
                    if p:
                        own_heads(p - 1)
                bank = filled(dve, ("o_sample", l))
                V.tensor_copy(h[0:NS, 2, 0:AW], psum[bank][0:NS, :]).then_inc(bank_emptied[bank], 1)
                tell(oattn_ready)

                for c in range(3):
                    r = ROWS[c]
                    bank = filled(dve, ("z", l, c))
                    link(V.bn_stats(stat(("zst", l, c), 6, r), psum[bank][0:r, :]))
                    V.bn_aggr(stat(("zmv", l, c), 2, r), stat(("zst", l, c), 6, r)).then_inc(zvar_ready, 1)
                    dve.wait_ge(zstd_ready, 3 * l + c + 1)
                    dve.wait_ge(u_stored, u_waits * (l + 1))
                    dve.wait_ge(conv_norm_loaded, 32 * (l + 1))
                    link(V.reciprocal(stat(("zrs", l, c), rows=r), stat(("zstd", l, c), rows=r)))
                    zt = u[0:r, c, :]
                    link(V.tensor_scalar(zt, psum[bank][0:r, :], stat(("zmv", l, c), 2, r)[:, 0:1],
                                         stat(("zrs", l, c), rows=r), ALU.subtract, ALU.mult))
                    link(V.tensor_tensor(zt, zt, conv_norm[0:r, 0, :], ALU.mult))
                    V.tensor_tensor(zt, zt, conv_norm[0:r, 1, :], ALU.add).then_inc(bank_emptied[bank], 1)
                    tell(znorm_ready)
                for c in range(3):
                    r = ROWS[c]
                    dve.wait_ge(mstd_ready, 3 * l + c + 1)
                    link(V.reciprocal(stat(("mrs", l, c), 2, r), stat(("mstd", l, c), 2, r)))
                    for f in range(2):
                        part = h[0:r, c, f * 512:(f + 1) * 512]
                        last = V.tensor_scalar(part, part, stat(("mrs", l, c), 2, r)[:, f:f + 1], None, ALU.mult)
                    last.then_inc(h_ready, 1)
                gained_columns(l, "merged")
                for g in range(2):
                    for c in range(3):
                        add_to_x((("out", l, g), c), c, g)
                        if g == 1:
                            tell(x_ready)
                norm_rows(l, "cross")
                dve.wait_ge(q_zeroed, 2 * l + 2)
                for j in range(XH):
                    bank = filled(dve, (("xq", l), j))
                    V.tensor_copy(xqT[:, j, :], psum[bank][:, 0:SEQ])
                    V.tensor_copy(xq_rows[:, j, :, j * DS:(j + 1) * DS],
                                  psum[bank][:, SEQ:NTOK].rearrange("p (b t) -> p b t", b=DB)).then_inc(bank_emptied[bank], 1)
                for quad in range(QUADS):
                    bank = filled(dve, ("xs", l, quad))
                    link(V.tensor_reduce(stat(("xmax", l, quad)), psum[bank][:, 0:NMEM], AX.X, ALU.max))
                    V.tensor_scalar(stat(("xbias", l, quad)), stat(("xmax", l, quad)), -X_SCALE, None, ALU.mult)\
                        .then_inc(xmax_ready, 1)
                for i in range(2):
                    for g in range(2):
                        bank = filled(dve, ("xscores", l, i, g))
                        link(V.tensor_reduce(stat(("xpmax", l, i, g), 2), psum[bank][:, :].rearrange("p (a k) -> p a k", a=2),
                                             AX.X, ALU.max))
                        V.tensor_scalar(stat(("xpbias", l, i, g), 2), stat(("xpmax", l, i, g), 2), -X_SCALE, None, ALU.mult)\
                            .then_inc(xmax_ready, 1)
                for quad in range(QUADS):
                    bank = filled(dve, ("xo_quad", l, quad))
                    link(V.reciprocal(stat(("xinv", l, quad)), stat(("xsum", l, quad))))
                    V.scalar_tensor_tensor(out=xo_masked[:, quad, :].rearrange("p (a k) -> p a k", a=XH),
                                           in0=psum[bank][:, :].rearrange("p (a k) -> p a k", a=XH),
                                           scalar=stat(("xinv", l, quad)), in1=wide(own_xhead[:, :], P, XH, P),
                                           op0=ALU.mult, op1=ALU.mult).then_inc(bank_emptied[bank], 1)
                for i in range(2):
                    bank = filled(dve, ("xo_prompt", l, i))
                    link(V.reciprocal(stat(("xpinv", l, i), XH), stat(("xpsum", l, i), XH)))
                    V.tensor_tensor(xo[:, i, :].rearrange("p (a k) -> p a k", a=XH),
                                    psum[bank][:, :].rearrange("p (a k) -> p a k", a=XH),
                                    wide(stat(("xpinv", l, i), XH), P, XH, P), ALU.mult).then_inc(bank_emptied[bank], 1)
                bank = filled(dve, ("xo_sample", l))
                V.tensor_copy(xo[0:NS, 2, :], psum[bank][0:NS, :]).then_inc(bank_emptied[bank], 1)
                for g in range(2):
                    for c in range(3):
                        add_to_x((("co", l, g), c), c, g)
                        if g == 1:
                            tell(x_ready)
                norm_rows(l, "ffn")
                if l % 2 == 0:
                    dve.wait_ge(mkv_stored, 32 * (l + 1))
                    for step in range((FF_HALVES + 1) // 2):
                        for m in range(2 * step, min(2 * step + 2, FF_HALVES)):
                            dve.wait_ge(ff_hi_made, m + 1)
                            V.tensor_tensor(ff_lo[m % FF_RAW][:, :], ff_raw[m % FF_RAW], ff_hi[m % FF_HI][:, :].bitcast(F32),
                                            ALU.subtract).then_inc(ff_lo_made, 1)
                        g = step - 1
                        if 0 <= g < NFG:
                            if g >= 2:
                                dve.wait_ge(ff_midT_made, g - 1)
                            for j in range(2):
                                gate_bank, gate_n = jobs[(("ff", l, g), j)]
                                dve.wait_ge(bank_emptied[gate_bank], gate_n + 1)
                                bank = filled(dve, (("ff", l, g), 2 + j))
                                V.tensor_tensor(mid[:, g % 2, j, :], silu[:, g % 2, j, :], psum[bank][:, 0:NTOK], ALU.mult)\
                                    .then_inc(bank_emptied[bank], 1)
                            tell(ff_mid_made)
                        g = step - 2
                        if 0 <= g < NFG:
                            dve.wait_ge(ff_midT_hi_made, g + 1)
                            V.tensor_tensor(midT_lo[:, 2 * g:2 * g + 2, :], mid[:, g % 2, :, :],
                                            midT_hi[:, 2 * g:2 * g + 2, :].bitcast(F32), ALU.subtract).then_inc(ff_midT_made, 1)
                    for c in range(3):
                        for f in range(2):
                            add_to_x(("ff_out", l, c, f), c, f)
                        tell(x_ready)
                    continue

                prob, eq, cand, first, second, chosen, gate, left, ranked, top_p, e2, sm = route
                link(V.memset(prob, 0.0))
                bank = filled(dve, "router")
                for r, cs, n in parts:
                    pl = psum[bank][0:r, 0:3 * NE].rearrange("p (c n) -> p c n", c=3)[:, cs, :]
                    last = V.tensor_tensor(prob[0:r, cs, :], pl, router_b[0:r, :].unsqueeze(1).to_broadcast([r, n, NE]), ALU.add)
                link(last)
                m3 = stat("rmax", 3)
                link(V.tensor_reduce(m3, prob, AX.X, ALU.max))
                V.tensor_tensor(prob, prob, wide(m3, P, 3, NE), ALU.subtract).then_inc(bank_emptied[bank], 1)
                tell(rmax_ready)
                dve.wait_ge(rexp_ready, 1)
                link(V.tensor_reduce(stat("rsum", 3), prob, AX.X, ALU.add))
                link(V.reciprocal(stat("rinv", 3), stat("rsum", 3)))
                link(V.tensor_tensor(prob, prob, wide(stat("rinv", 3), P, 3, NE), ALU.mult))
                ids = iota8[:, :].unsqueeze(1).to_broadcast([P, 3, NE])

                def largest(src, out, name):
                    top = stat("top" + name, 3)
                    at = stat("at" + name, 3)
                    link(V.tensor_reduce(top, src, AX.X, ALU.max))
                    link(V.tensor_tensor(eq, src, wide(top, P, 3, NE), ALU.is_equal))
                    link(V.tensor_scalar(cand, eq, -float(NE), float(NE), ALU.mult, ALU.add))
                    link(V.tensor_tensor(eq, eq, ids, ALU.mult))
                    link(V.tensor_tensor(cand, cand, eq, ALU.add))
                    link(V.tensor_reduce(at, cand, AX.X, ALU.min))
                    link(V.tensor_tensor(out, ids, wide(at, P, 3, NE), ALU.is_equal))
                    return top

                top1 = largest(prob, first, "1")
                link(V.tensor_scalar(left, first, -2.0, None, ALU.mult))
                link(V.tensor_tensor(left, left, prob, ALU.add))
                top2 = largest(left, second, "2")
                link(V.tensor_tensor(chosen, first, second, ALU.add))
                link(V.memset(chosen[NS:P, 2, :], 0.0))
                tell(picks_ready)
                link(V.tensor_tensor(stat("tsum", 3), top1, top2, ALU.add))
                link(V.reciprocal(stat("tinv", 3), stat("tsum", 3)))
                link(V.tensor_tensor(gate, first, wide(top1, P, 3, NE), ALU.mult))
                link(V.tensor_tensor(top_p, second, wide(top2, P, 3, NE), ALU.mult))
                link(V.tensor_tensor(gate, gate, top_p, ALU.add))
                link(V.tensor_tensor(gate, gate, wide(stat("tinv", 3), P, 3, NE), ALU.mult))
                bank = filled(dve, "ranks")
                link(V.tensor_copy(cnt, psum[bank][:, 3 * NE:4 * NE]))
                link(V.tensor_tensor(ranked, psum[bank][:, 0:3 * NE].rearrange("p (c n) -> p c n", c=3), chosen, ALU.mult))
                link(V.tensor_scalar(e2, chosen, 1000.0, -1000.0, ALU.mult, ALU.add))
                link(V.tensor_tensor(ranked, ranked, e2, ALU.add))
                dve.wait_ge(iota_made, 1)
                make_picks(ranked[:, :, 0:1], gate[:, :, 0:1])
                link(V.tensor_scalar(nch, cnt, float(P), None, ALU.is_gt))
                link(V.tensor_scalar(starts, cnt, float(2 * P), 1.0, ALU.is_gt, ALU.add))
                link(V.tensor_tensor(nch, nch, starts, ALU.add))
                link(V.tensor_tensor_scan(ends, ones[:, 0:NE], nch, 0.0, ALU.mult, ALU.add))
                link(V.tensor_tensor(starts, ends, nch, ALU.subtract))
                turns3 = [P, PICKS, NE]
                link(V.tensor_tensor(item_t, wide(item_ids[:, :], *turns3), starts.unsqueeze(1).to_broadcast(turns3), ALU.is_ge))
                link(V.tensor_reduce(item_e, item_t, AX.X, ALU.add))
                link(V.tensor_scalar(item_e, item_e, -1.0, None, ALU.add))
                link(V.tensor_tensor(item_oh, iota8[:, :].unsqueeze(1).to_broadcast(turns3), wide(item_e, *turns3), ALU.is_equal))
                link(V.tensor_tensor(item_t, item_oh, starts.unsqueeze(1).to_broadcast(turns3), ALU.mult))
                link(V.tensor_reduce(item_c, item_t, AX.X, ALU.add))
                link(V.tensor_tensor(item_c, item_ids[:, :], item_c, ALU.subtract))
                link(V.tensor_scalar(item_c, item_c, float(P), None, ALU.mult))
                for src, dst in ((ranked, rank_i), (gate, gate_i)):
                    for c in range(3):
                        link(V.tensor_tensor(route4[:, c, :, :], item_oh, src[:, c, :].unsqueeze(1).to_broadcast(turns3), ALU.mult))
                    link(V.tensor_reduce(dst, route4, AX.X, ALU.add))
                link(V.tensor_tensor(rank_i, rank_i, item_c.unsqueeze(1).to_broadcast([P, 3, PICKS]), ALU.subtract))
                link(V.tensor_copy(items[0:1, 0:1], ends[0:1, NE - 1:NE]))
                link(V.tensor_scalar(items[0:1, 1 + MAX_ITEMS:2 + MAX_ITEMS], ends[0:1, NE - 1:NE], -1.0, None, ALU.add))
                V.tensor_copy(items[0:1, 1:1 + MAX_ITEMS], item_e[0:1, 0:MAX_ITEMS]).then_inc(bank_emptied[bank], 1)
                tell(items_ready)

            for f in range(2):
                split_taken(filled(dve, ("first_take", f)), f, 0)
            tell(xT_ready)
            tell(w_lo_made[0])
            dve.wait_ge(items_ready, 1)
            n_items = dve.value_load(items[0:1, 0:1], min_val=NE, max_val=MAX_ITEMS)

            with dve.Fori(0, n_items) as i:
                for step in range(HALVES // 2):
                    for m in (2 * step, 2 * step + 1):
                        if m == 0:
                            continue
                        dve.wait_ge(w_hi_made, i * HALVES + (m + 1))
                        V.tensor_tensor(w_lo[m % SPLIT][:, 0:DVE_COLS], raw_half[m % MOE_RING][:, 0:DVE_COLS],
                                        w_hi[m % SPLIT][:, 0:DVE_COLS].bitcast(F32), ALU.subtract).then_inc(w_lo_made[0], 1)
                    if step == 2:
                        bank = e_filled_wait(dve, ("giveT",), i)
                        V.tensor_copy(e_giveT.rearrange("p c t -> p (c t)")[:, 0:NTOK], psum[bank][:, 0:NTOK])\
                            .then_inc(bank_emptied[bank], 1)
                    if step == PICK_STEP:
                        make_picks(rank_i[:, :, bass.ds(i + 1, 1)], gate_i[:, :, bass.ds(i + 1, 1)])
                    g = step - 1
                    if 0 <= g < NEG_G:
                        bank = e_filled_wait(dve, ("up", g), i)
                        dve.wait_ge(e_silu_ready, i * NEG_G + (g + 1))
                        V.tensor_tensor(e_mid[:, g % 2, :], e_silu[:, g % 2, :], psum[bank][:, 256:512], ALU.mult)\
                            .then_inc(bank_emptied[bank], 1)
                    g = step - 2
                    if 0 <= g < NEG_G:
                        dve.wait_ge(midT_hi_made, i * NEG_G + (g + 1))
                        bank = e_jobs[("midT", g)][0]
                        V.tensor_tensor(e_midT_lo[:, 2 * g:2 * g + 2, :], psum[bank][:, 0:256].rearrange("p (j t) -> p j t", j=2),
                                        e_midT_hi[:, 2 * g:2 * g + 2, :].bitcast(F32), ALU.subtract)\
                            .then_inc(bank_emptied[bank], 1)
                bank = e_filled_wait(dve, ("down", 0), i)
                V.tensor_copy(e_y[:, 0, :], psum[bank][:, :]).then_inc(bank_emptied[bank], 1)
                for f in range(2):
                    split_taken(e_filled_wait(dve, ("take", f), i), f, (i + 1) * COLUMN_STEPS)
                tell(xT_ready)
                tell(w_lo_made[0])
                for f in range(2):
                    for c in range(3):
                        r = ROWS[c]
                        bank = e_filled_wait(dve, ("give", c, f), i)
                        xs = x[0:r, c, f * 512:(f + 1) * 512]
                        V.tensor_tensor(xs, xs, psum[bank][0:r, :], ALU.add).then_inc(bank_emptied[bank], 1)
            tell(x_ready)
            dve.wait_ge(gfin_loaded, 16)
            for c in range(3):
                r = ROWS[c]
                dve.wait_ge(std_ready, 3 * len(NORMS) + c + 1)
                link(V.reciprocal(stat(("rstd", "f", c), rows=r), stat(("std", "f", c), rows=r)))
                V.scalar_tensor_tensor(out=h[0:r, c, :], in0=x[0:r, c, :], scalar=stat(("rstd", "f", c), rows=r),
                                       in1=g_final[0:r, :], op0=ALU.mult, op1=ALU.mult).then_inc(out_ready, 1)

        @block.scalar
        def _(act):
            steps, told = [0], [0]
            S = nc.scalar

            def link(ins):
                steps[0] += 1
                ins.then_inc(scalar_step, 1)
                act.wait_ge(scalar_step, steps[0])

            def tell(s):
                told[0] += 1
                S.activation(note[:, 16 + told[0] % 8:17 + told[0] % 8], eps[:, :], ACT.Copy).then_inc(s, 1)

            def empty(key, dst, src, func=ACT.Copy):
                bank = filled(act, key)
                S.activation(dst, src(psum[bank]), func).then_inc(bank_emptied[bank], 1)

            act.wait_ge(ident_made, 1)
            def row_std(n, c, key=None):
                r = ROWS[c]
                key = n if key is None else key
                link(S.activation(h[0:r, c, :], x[0:r, c, :], ACT.Square, accum_out=stat(("ss", key, c), rows=r)))
                S.activation(stat(("std", key, c), rows=r), stat(("ss", key, c), rows=r), ACT.Sqrt, bias=eps[0:r, :],
                             scale=1.0 / D).then_inc(std_ready, 1)

            x_seen = [0]

            def stage_std(n):
                for c in range(3):
                    x_seen[0] += 1
                    act.wait_ge(x_ready, x_seen[0])
                    row_std(n, c)

            act.wait_ge(x_loaded, 32)
            for c in range(3):
                row_std(0, c)
            for c in range(2):
                act.wait_ge(mem_loaded, 16)
                link(S.activation(mem_squares, mem[:, c, :], ACT.Square, accum_out=stat(("mem_ss", c))))
                S.activation(stat(("mem_std", c)), stat(("mem_ss", c)), ACT.Sqrt, bias=eps[:, :], scale=1.0 / D).then_inc(mem_std, 1)
            for c in range(2):
                for f in range(2):
                    empty(("memT", c, f), memT[:, 4 * f:4 * f + 4, COLS[c]],
                          lambda ps: ps[:, :].rearrange("p (k t) -> p k t", k=4))
            for l in range(DEPTH):
                for n, part in ((1, "k"), (2, "v")):
                    for c in range(3):
                        r = ROWS[c]
                        empty(((part, l), c), qkv[0:r, c, n * AW:(n + 1) * AW], lambda ps: ps[0:r, :])
                    if n == 1:
                        act.wait_ge(abs_ready, l + 1)
                        for r, cs in ((P, slice(0, 2)), (NS, slice(2, 3))):
                            link(S.activation(log_tmp[0:r, 1, cs, :], log_tmp[0:r, 0, cs, :], ACT.Exp, scale=-1.0))
                            last = S.activation(log_tmp[0:r, 1, cs, :], log_tmp[0:r, 1, cs, :], ACT.Ln, bias=1.0)
                        last.then_inc(softplus_ready, 1)
                for j in range(4):
                    empty((("gate", l), j), uT[:, j, :], lambda ps: ps[:, 0:NTOK], ACT.Sigmoid)
                for c in range(3):
                    empty(("kT", l, c), kT[:, :, COLS[c]], lambda ps: ps[:, 0:4 * ROWS[c]].rearrange("p (j t) -> p j t", j=4))
                for b in range(2):
                    bank = filled(act, ("histT", l, b))
                    for j in range(4):
                        last = S.activation(us[:, j, 4 * b:4 * b + 4, 0:HIST],
                                            psum[bank][:, j * 4 * HIST:(j + 1) * 4 * HIST].rearrange("p (b t) -> p b t", b=4), ACT.Copy)
                    last.then_inc(bank_emptied[bank], 1)
                tell(hist_ready)
                n = 0
                for i in range(2):
                    keys = (i + 1) * P
                    per = 512 // keys
                    for g in range(NH // per):
                        n += 1
                        act.wait_ge(pmax_ready, 6 * l + n)
                        bank = jobs[("scores", l, i, g)][0]
                        for a in range(per):
                            last = S.activation(p_prompt[i][:, g * per + a, :], psum[bank][:, a * keys:(a + 1) * keys], ACT.Exp,
                                                bias=stat(("pbias", l, i, g), per)[:, a:a + 1],
                                                accum_out=stat(("psum", l, i, g), per)[:, a:a + 1])
                        last.then_inc(bank_emptied[bank], 1)
                for n in range(6):
                    empty(("pT", l, n), PT[:, 4 * (n % 2):4 * (n % 2) + 4, :], lambda ps: ps[:, :].rearrange("p (j t) -> p j t", j=4))

                def key_columns(n):
                    b, half = n // 2, n % 2
                    for pg in range(4 * half, 4 * half + 4):
                        empty(("KT", l, b, pg), KT[:, n % 2, :, (pg % 4) * P:(pg % 4 + 1) * P],
                              lambda ps: ps[:, :].rearrange("p (j t) -> p j t", j=4))

                def exps(p):
                    act.wait_ge(smax_ready, PAIRS * l + p + 1)
                    bias, sums = stat(("sbias", l, p)), stat(("ssum", l, p), 3)
                    for half in range(2):
                        bank = jobs[("past", l, p, half)][0]
                        S.activation(probs[:, half * 512:(half + 1) * 512], psum[bank][:, :], ACT.Exp, bias=bias,
                                     accum_out=sums[:, half:half + 1]).then_inc(bank_emptied[bank], 1)
                    S.activation(probs[:, PAST:PAST + NS], probs[:, PAST:PAST + NS], ACT.Exp, bias=bias,
                                 accum_out=sums[:, 2:3]).then_inc(sexp_ready, 1)

                def probs_columns(p):
                    for t in range(2):
                        empty(("PT", l, p, t), PT[:, 4 * t:4 * t + 4, :], lambda ps: ps[:, :].rearrange("p (j t) -> p j t", j=4))
                    empty(("PT", l, p, 2), PT[0:NS, 8, :], lambda ps: ps[0:NS, 0:P])

                key_columns(0)
                for p in range(PAIRS + 1):
                    if p < PAIRS:
                        for n in range(4 * p, 4 * p + 4):
                            if n % 4 == 2 and p:
                                probs_columns(p - 1)
                            if n + 1 < 4 * p + 4:
                                key_columns(n + 1)
                        if p == 0:
                            key_columns(4)
                        exps(p)
                    else:
                        probs_columns(p - 1)
                    if p and p + 1 < PAIRS:
                        key_columns(4 * (p + 1))

                for c in range(3):
                    r = ROWS[c]
                    act.wait_ge(zvar_ready, 3 * l + c + 1)
                    S.activation(stat(("zstd", l, c), rows=r), stat(("zmv", l, c), 2, r)[:, 1:2], ACT.Sqrt, bias=eps[0:r, :])\
                        .then_inc(zstd_ready, 1)
                for c in range(3):
                    r = ROWS[c]
                    act.wait_ge(znorm_ready, 3 * l + c + 1)
                    link(S.activation(h[0:r, c, 512:D], u[0:r, c, :], ACT.Silu))
                act.wait_ge(oattn_ready, 2 * l + 2)
                for c in range(3):
                    r = ROWS[c]
                    for f in range(2):
                        link(S.activation(u[0:r, c, :], h[0:r, c, f * 512:(f + 1) * 512], ACT.Square,
                                          accum_out=stat(("mss", l, c), 2, r)[:, f:f + 1]))
                    S.activation(stat(("mstd", l, c), 2, r), stat(("mss", l, c), 2, r), ACT.Sqrt, bias=eps[0:r, :],
                                 scale=1.0 / AW).then_inc(mstd_ready, 1)
                for g in range(2):
                    for c in range(2):
                        empty((("mkv", l, g), c), mkv[:, c, g * 512:(g + 1) * 512], lambda ps: ps[:, :])
                stage_std(NORM_AT[(l, "cross")])
                for m in range(2):
                    empty(("mkT", l, m), mkT[:, :, m * P:(m + 1) * P], lambda ps: ps[:, :].rearrange("p (j t) -> p j t", j=XH))
                for b in range(DB):
                    for m in range(2):
                        empty(("xKT", l, b, m), xKT[:, b % 2, :, m * P:(m + 1) * P],
                              lambda ps: ps[:, :].rearrange("p (j t) -> p j t", j=XH))
                for quad in range(QUADS):
                    act.wait_ge(xmax_ready, 6 * l + quad + 1)
                    bank = jobs[("xs", l, quad)][0]
                    S.activation(xp[:, quad, :], psum[bank][:, 0:NMEM], ACT.Exp, bias=stat(("xbias", l, quad)), scale=X_SCALE,
                                 accum_out=stat(("xsum", l, quad))).then_inc(bank_emptied[bank], 1)
                for i in range(2):
                    for g in range(2):
                        act.wait_ge(xmax_ready, 6 * l + 2 + 2 * i + g + 1)
                        bank = jobs[("xscores", l, i, g)][0]
                        for a in range(2):
                            last = S.activation(xp_prompt[:, i, 2 * g + a, :], psum[bank][:, a * NMEM:(a + 1) * NMEM], ACT.Exp,
                                                bias=stat(("xpbias", l, i, g), 2)[:, a:a + 1], scale=X_SCALE,
                                                accum_out=stat(("xpsum", l, i), XH)[:, 2 * g + a:2 * g + a + 1])
                        last.then_inc(bank_emptied[bank], 1)
                for quad in range(QUADS):
                    empty(("xPT", l, quad), xPT[:, quad, 0:2, :], lambda ps: ps[:, 0:2 * P].rearrange("p (j t) -> p j t", j=2))
                for n in range(4):
                    empty(("xpT", l, n), xPT[:, 2 + n % 2, :, :], lambda ps: ps[:, :].rearrange("p (j t) -> p j t", j=4))
                for c in range(3):
                    empty(("xoT", l, c), hT[:, 0:XH, COLS[c]], lambda ps: ps[:, 0:4 * ROWS[c]].rearrange("p (j t) -> p j t", j=4))
                stage_std(NORM_AT[(l, "ffn")])
                if l % 2 == 0:
                    act.wait_ge(mkv_stored, 32 * (l + 1))
                    for step in range((FF_HALVES + 1) // 2):
                        for m in range(2 * step, min(2 * step + 2, FF_HALVES)):
                            if m < FF_HI:
                                filled(act, last_reader(l, FF_HI_AT[m] // 2))
                            else:
                                ff_half_read(act, l, m - FF_HI)
                            act.wait_ge(ff_landed[m % FF_RAW], ff_done[m])
                            S.activation(ff_hi[m % FF_HI][:, :], ff_raw[m % FF_RAW], ACT.Copy).then_inc(ff_hi_made, 1)
                        g = step - 1
                        if 0 <= g < NFG:
                            for j in range(2):
                                empty((("ff", l, g), j), silu[:, g % 2, j, :], lambda ps: ps[:, 0:NTOK], ACT.Silu)
                        g = step - 2
                        if 0 <= g < NFG:
                            act.wait_ge(ff_mid_made, g + 1)
                            S.activation(midT_hi[:, 2 * g:2 * g + 2, :], mid[:, g % 2, :, :], ACT.Copy).then_inc(ff_midT_hi_made, 1)
                    stage_std(NORM_AT[(l + 1, "mix")])
                    continue
                act.wait_ge(rmax_ready, 1)
                S.activation(route[0], route[0], ACT.Exp).then_inc(rexp_ready, 1)

            act.wait_ge(mkv_stored, 32 * DEPTH)
            act.wait_ge(items_ready, 1)
            n_items = act.value_load(items[0:1, 0:1], min_val=NE, max_val=MAX_ITEMS)
            with act.Fori(0, n_items) as i:
                for step in range(HALVES // 2):
                    for m in (2 * step, 2 * step + 1):
                        act.wait_ge(e_landed[m % MOE_RING], i * e_bytes[m % MOE_RING] + e_done[m])
                        half_read_wait(act, i, m - SPLIT)
                        S.activation(w_hi[m % SPLIT][:, :], raw_half[m % MOE_RING], ACT.Copy).then_inc(w_hi_made, 1)
                    g = step - 1
                    if 0 <= g < NEG_G:
                        bank = e_filled_wait(act, ("up", g), i)
                        S.activation(e_silu[:, g % 2, :], psum[bank][:, 0:256], ACT.Silu).then_inc(e_silu_ready, 1)
                    g = step - 2
                    if 0 <= g < NEG_G:
                        bank = e_filled_wait(act, ("midT", g), i)
                        S.activation(e_midT_hi[:, 2 * g:2 * g + 2, :], psum[bank][:, 0:256].rearrange("p (j t) -> p j t", j=2),
                                     ACT.Copy).then_inc(midT_hi_made, 1)
                bank = e_filled_wait(act, ("down", 1), i)
                S.activation(e_y[:, 1, :], psum[bank][:, :], ACT.Copy).then_inc(bank_emptied[bank], 1)
            x_seen[0] += 1
            act.wait_ge(x_ready, x_seen[0])
            for c in range(3):
                row_std(None, c, "f")

        @block.gpsimd
        def _(pool):
            steps = [0]
            G = nc.gpsimd

            def link(ins):
                steps[0] += 1
                ins.then_inc(pool_step, 1)
                pool.wait_ge(pool_step, steps[0])

            def select(t, pattern, base, mult, op, fill):
                link(G.affine_select(out=t, in_=t, compare_op=op, fill=fill, base=base, pattern=pattern,
                                     channel_multiplier=mult))

            link(G.memset(ident[:, :], 0.0))
            select(ident[:, :], [[-1, P]], 0, 1, ALU.not_equal, 1.0)
            G.memset(eps[:, :], EPS).then_inc(ident_made, 1)
            for t in (ones[:, :], upto[:, :], before[:, :], block_upto[:, :], page_suffix, own_head[:, :], own_xhead[:, :]):
                link(G.memset(t, 1.0))
            link(G.memset(causal[:, :], 0.0))
            link(G.memset(spread8, 0.0))
            link(G.memset(small8[:, :, :, :], 0.0))
            select(upto[:, :], [[1, P]], 0, -1, ALU.is_ge, 0.0)
            select(before[:, :], [[1, P]], -1, -1, ALU.is_ge, 0.0)
            select(causal[:, :], [[-1, P]], 0, 1, ALU.is_ge, NEG)
            bu = block_upto[:, :].rearrange("p (b t) -> p b t", b=DB)
            select(block_upto[:, :], [[1, NS]], 0, -1, ALU.is_ge, 0.0)
            select(bu, [[-DS, DB], [0, DS]], 0, 1, ALU.is_ge, 0.0)
            ps = page_suffix.rearrange("p (b g) -> p b g", g=NPG)
            select(page_suffix, [[-1, P]], 0, 1, ALU.is_ge, 0.0)
            select(ps, [[NPG, P // NPG], [0, NPG]], NPG - 1, -1, ALU.is_ge, 0.0)
            link(G.memset(decay_rows[:, :, :, :], 0.0))
            select(decay_rows[:, :, :, :].rearrange("p l b (h t) -> p l b h t", h=NH),
                   [[-NS, DEPTH], [-NH, DB], [-1, NH], [0, DS]], 0, 1, ALU.not_equal, 1.0)
            select(spread8.rearrange("p (a t) -> p a t", t=DS), [[0, P // DS], [-1, DS]], 0, 1, ALU.not_equal, 1.0)
            select(small8[:, 0, :, :], [[0, DB], [-1, DS]], 0, 1, ALU.is_ge, NEG)
            select(small8[:, 1, :, :], [[0, DB], [-1, DS]], 0, 1, ALU.not_equal, 1.0)
            for n in range(2):
                t = own_head[n * NS:(n + 1) * NS, :]
                select(t, [[-DS, NH]], 0, 1, ALU.is_ge, 0.0)
                select(t, [[DS, NH]], DS - 1, -1, ALU.is_ge, 0.0)
            for n in range(4):
                t = own_xhead[32 * n:32 * n + 32, :]
                select(t, [[-DS, XH]], 0, 1, ALU.is_ge, 0.0)
                select(t, [[DS, XH]], DS - 1, -1, ALU.is_ge, 0.0)
            link(G.memset(up[:, :, 0:HIST], 0.0))
            link(G.iota(item_ids[:, :], [[1, PICKS]], base=0, channel_multiplier=0, allow_small_or_imprecise_dtypes=True))
            G.iota(iota8[:, :], [[1, NE]], base=0, channel_multiplier=0, allow_small_or_imprecise_dtypes=True).then_inc(consts_made, 1)
            pool.wait_ge(idx_ready, 1)
            G.indirect_dma_start(out=lf_pages.rearrange("p s h -> p (s h)"), out_offset=None,
                                 in_=d["cache_logf"].rearrange("l n s h -> (l n) (s h)"),
                                 in_offset=bass.IndirectOffsetOnAxis(ap=page_idx[:, :].bitcast(U32), axis=0))\
                .then_inc(pages_gathered, 16)
            link(G.memset(q_rows, 0.0))
            G.memset(q_heads, 0.0).then_inc(q_zeroed, 1)
            pool.wait_ge(masks_spread, 1)
            for t, n, per, fill in ((new_mask, PAIRS, NS, NEG), (pair_rows, PAIRS, NS, 0.0), (quad_rows, QUADS, 32, 0.0)):
                v = t[:, :, :].rearrange("p a (b t) -> p a b t", b=DB)
                select(v, [[P, n], [-per, DB], [0, DS]], 0, 1, ALU.is_ge, fill)
                select(v, [[-P, n], [per, DB], [0, DS]], per - 1, -1, ALU.is_ge, fill)
            G.memset(note2[:, :], 0.0).then_inc(masks_made, 1)
            pool.wait_ge(decay_made, 2)
            G.dma_start(scratch, lf_decay.rearrange("p h s -> p (h s)")).then_inc(decay_stored, 16)
            pool.wait_ge(decay_stored, 16)
            for n in range(DEPTH * DB):
                G.dma_start(past_decay[n * NH:(n + 1) * NH, :].rearrange("h (g s) -> h g s", g=NPG),
                            scratch[n * NPG:(n + 1) * NPG, :].rearrange("g (h s) -> h g s", h=NH)).then_inc(decay_loaded, 16)

            def store(dst, src, s):
                G.dma_start(dst, src).then_inc(s, 16)

            for l in range(DEPTH):
                if l:
                    pool.wait_ge(x_ready, 3 * NORM_AT[(l, "mix")])
                    link(G.memset(up[:, :, 0:HIST], 0.0))
                    link(G.memset(q_rows, 0.0))
                    G.memset(q_heads, 0.0).then_inc(q_zeroed, 1)
                for b in range(2):
                    G.dma_start(hist_in[0:4 * HIST, b, :], d["cache_conv"][l, 4 * b:4 * b + 4].rearrange("b t c -> (b t) c"))\
                        .then_inc(conv_hist_loaded, 16)
                pool.wait_ge(logf_ready, l + 1)
                store(d["new_logf_prompt"][l, 0].rearrange("(c p) n -> p c n", p=P), logf[:, 0:2, :], kv_stored)
                store(d["new_logf_sample"][l].rearrange("b t n -> (b t) n"), logf[0:NS, 2, :], kv_stored)
                for c in range(3):
                    filled(pool, ("kT", l, c))
                    for n, name in ((1, "k"), (2, "v")):
                        out = d[f"new_{name}_prompt"][l, 0, c * P:(c + 1) * P] if c < 2 else \
                            d[f"new_{name}_sample"][l].rearrange("b t h e -> (b t) h e")
                        store(out.rearrange("p h e -> p (h e)"), qkv[0:ROWS[c], c, n * AW:(n + 1) * AW], kv_stored)
                for c in (1, 2):
                    bank, n = jobs[("u_rows", l, c)]
                    pool.wait_ge(bank_emptied[bank], n + 1)
                store(d["new_conv_prompt"][l, 0], u[P - HIST:P, 1, :], u_stored)
                for b in range(DB):
                    store(d["new_conv_sample"][l, b, HIST - DS:HIST], u[b * DS:(b + 1) * DS, 2, :], u_stored)
                store(d["new_conv_sample"][l, :, 0:HIST - DS], d["cache_conv"][l, :, DS:HIST], u_stored)
                filled(pool, ("past", l, PAIRS - 1, 1))
                for n, name in enumerate(("g_cln", "b_cln")):
                    G.dma_start(conv_norm[:, n, :], d[name][l:l + 1, :].to_broadcast([P, CW])).then_inc(conv_norm_loaded, 16)
                pool.wait_ge(h_ready, 3 * STAGE_AT[(l, "merged")] + 3)
                G.memset(xq_rows, 0.0).then_inc(q_zeroed, 1)
                filled(pool, ("mkT", l, 1))
                for n, name in enumerate(("k", "v")):
                    store(d[f"new_mem_{name}_prompt"][l, 0].rearrange("(c p) h e -> p c (h e)", p=P),
                          mkv[:, :, n * XW:(n + 1) * XW], mkv_stored)
            pool.wait_ge(x_ready, 3 * (len(NORMS) - 1))
            G.iota(iota_row[:, :], [[1, P]], base=0, channel_multiplier=0, allow_small_or_imprecise_dtypes=True)\
                .then_inc(iota_made, 1)
            pool.wait_ge(items_ready, 1)
            n_items = pool.value_load(items[0:1, 0:1], min_val=NE, max_val=MAX_ITEMS)
            with pool.Fori(0, n_items) as i:
                for m in range(HALVES):
                    pool.wait_ge(w_hi_made, i * HALVES + (m + 1))
                    first = DVE_COLS if m else 0
                    G.tensor_tensor(w_lo[m % SPLIT][:, first:HALF], raw_half[m % MOE_RING][:, first:HALF],
                                    w_hi[m % SPLIT][:, first:HALF].bitcast(F32), ALU.subtract).then_inc(w_lo_made[1], 1)
            pool.wait_ge(mkv_stored, 16 * 4)
            pool.wait_ge(kv_stored, kv_waits * DEPTH)
            pool.wait_ge(u_stored, u_waits * DEPTH)

        @block.sync
        def _(sp):
            def load(dst, src, s):
                sp.dma_start(dst, src).then_inc(s, 16)

            page_rows = d["page_table"].rearrange("b (g o) -> (b g) o", o=1)
            load(page_idx[0:NS, :], page_rows, idx_loaded)
            load(page_idx[NS:P, :], page_rows, idx_loaded)
            load(x[:, 0:2, :], d["x_prompt"][0].rearrange("(c p) n -> p c n", p=P), x_loaded)
            load(x[0:NS, 2, :], d["x_sample"].rearrange("b t n -> (b t) n"), x_loaded)
            for l in range(DEPTH):
                at = l * N_GAINS
                for name in ("g_mix", "g_attn_out", "g_conv_out", "g_cross", "g_mem", "g_ffn"):
                    rows = d[name].shape[1] // P
                    load(gain_rows[at:at + rows, :], d[name][l].rearrange("(k p) -> k p", p=P), rows_loaded)
                    at += rows
                load(dw_rows[0:4 * CONV_K, l, :], d["w_dw"][l].rearrange("k (j c) -> (k j) c", c=P), rows_loaded)
                load(dw_rows[4 * CONV_K:P, l, :], d["b_dw"][l].rearrange("(j c) -> j c", c=P), rows_loaded)

            def rows_of(name, l, lo, n):
                return d[name][l, :, lo:lo + n].rearrange("(k p) n -> p k n", p=P)

            glu = 3 * AW + NH
            col_of = {"q": 0, "k": AW, "v": 2 * AW, "value": glu, "gate": glu + CW}

            def ff_loads(l):
                for m in range(FF_HALVES):
                    s = m % FF_RAW
                    if m < FF_RAW:
                        filled(sp, last_reader(l, FF_RAW_AT[m] // 2))
                    else:
                        ff_half_read(sp, l, m - FF_RAW)
                    if m < FF_UP_HALVES:
                        lo, col = 512 * (m % 2), 256 * (m // 2)
                        for part in range(2):
                            load(ff_raw[s].rearrange("p (k h n) -> p k h n", k=4, h=2)[:, :, part, :],
                                 d["w_ff_gu"][l // 2, lo:lo + 512, part * FF + col:part * FF + col + 256]
                                 .rearrange("(k p) n -> p k n", p=P), ff_landed[s])
                    else:
                        lo = 256 * (m - FF_UP_HALVES)
                        load(ff_raw[s].rearrange("p (k n) -> p k n", k=2),
                             d["w_ff_down"][l // 2, lo:lo + 256, :].rearrange("(k p) n -> p k n", p=P), ff_landed[s])

            def load_unit(n):
                key = units[n][0]
                s = n % RING
                slot = ring[:, s * SLOT:(s + 1) * SLOT]
                if n and key[1] != units[n - 1][0][1] and units[n - 1][0][1] % 2 == 0:
                    ff_loads(units[n - 1][0][1])
                if n >= RING:
                    before_it = units[n - RING][0]
                    if before_it[1] != key[1] and before_it[1] % 2 == 0:
                        ff_half_read(sp, before_it[1], last_half_of_slot(s))
                    else:
                        filled(sp, freed_by[before_it])
                k8 = slot.rearrange("p (k n) -> p k n", k=8)
                k4 = slot.rearrange("p (k n) -> p k n", k=4)
                kind, l = key[0], key[1]
                if kind == "w_in":
                    load(k8, rows_of("w_in", l, col_of[key[2]], 512), slot_landed[s])
                elif kind in ("w_out", "w_ckv"):
                    load(k8, rows_of(kind, l, 512 * key[2], 512), slot_landed[s])
                elif kind == "w_cq":
                    load(k8, rows_of(kind, l, 0, 512), slot_landed[s])
                elif kind == "w_co":
                    load(k4, rows_of(kind, l, 0, D), slot_landed[s])
                elif kind in "KV":
                    cache = d["cache_k" if kind == "K" else "cache_v"]
                    if key == ("K", 0, 0):
                        sp.wait_ge(page_row_loaded, 16)
                    for g in range(NPG):
                        at = key[2] * NPG + g
                        page = sp.value_load(page_row[0:1, at:at + 1], min_val=0, max_val=N_PHYS - 1)
                        load(k8[:, g, :], cache[l, bass.ds(page, 1)].rearrange("o s h e -> (o s) (h e)"), slot_landed[s])
                elif kind == "mem_kv":
                    for b2 in range(2):
                        for n2, name in enumerate(("cache_mem_k", "cache_mem_v")):
                            at = 4 * b2 + 2 * n2
                            load(k8[:, at:at + 2, :], d[name][l, key[2] + b2].rearrange("(m p) h e -> p m (h e)", p=P), slot_landed[s])

            load_unit(0)
            load(page_row, d["page_table"].rearrange("(a b) g -> a (b g)", a=1), page_row_loaded)
            for l in range(DEPTH):
                load(forget_w[:, l, :, :], d["w_in"][l, :, 3 * AW:3 * AW + NH].rearrange("(k p) n -> p k n", p=P), small_loaded)
                load(forget_b[:, l, :], d["b_fgate"][l:l + 1, :].to_broadcast([P, NH]), small_loaded)
            load(mem, d["mem_prompt"][0].rearrange("(c p) n -> p c n", p=P), mem_loaded)
            load(router_w[:, :, :], d["w_router"][0].rearrange("(k p) n -> p k n", p=P), small_loaded)
            load(router_b[:, :], d["b_router"][0:1, :].to_broadcast([P, NE]), small_loaded)
            for n in range(1, len(units)):
                load_unit(n)

            def expert_half(e, m):
                dst = raw_half[m % MOE_RING]
                if m < UP_HALVES:
                    lo, col = 512 * (m % 2), 256 * (m // 2)
                    for part in range(2):
                        load(dst.rearrange("p (k h n) -> p k h n", k=4, h=2)[:, :, part, :],
                             d["w_e_gu"][0, bass.ds(e, 1), lo:lo + 512, part * EF + col:part * EF + col + 256]
                             .rearrange("o (k p) n -> p (o k) n", p=P), e_landed[m % MOE_RING])
                else:
                    lo = 256 * (m - UP_HALVES)
                    load(dst.rearrange("p (k n) -> p k n", k=2),
                         d["w_e_down"][0, bass.ds(e, 1), lo:lo + 256, :].rearrange("o (k p) n -> p (o k) n", p=P),
                         e_landed[m % MOE_RING])

            def rest(i, e):
                for m in range(MOE_RING, HALVES):
                    half_split_wait(sp, i, m - MOE_RING)
                    expert_half(e, m)

            for m in range(MOE_RING):
                if m % 2 == 0:
                    filled(sp, freed_by[units[max(n for n in range(len(units)) if n % RING == m // 2)][0]])
                expert_half(0, m)
            sp.wait_ge(items_ready, 1)
            n_turns = sp.value_load(items[0:1, 0:1], min_val=NE, max_val=MAX_ITEMS)
            with sp.Fori(0, n_turns - 1) as i:
                rest(i, sp.value_load(items[0:1, bass.ds(i + 1, 1)], min_val=0, max_val=NE - 1))
                following = sp.value_load(items[0:1, bass.ds(i + 2, 1)], min_val=0, max_val=NE - 1)
                for m in range(MOE_RING):
                    half_split_wait(sp, i, HALVES - MOE_RING + m)
                    expert_half(following, m)
            last_turn = sp.value_load(items[0:1, 1 + MAX_ITEMS:2 + MAX_ITEMS], min_val=NE - 1, max_val=MAX_ITEMS - 1)
            rest(last_turn, sp.value_load(items[0:1, bass.ds(last_turn + 1, 1)], min_val=0, max_val=NE - 1))
            sp.wait_ge(x_ready, 3 * (len(NORMS) - 1) + 1)
            load(g_final[:, :], d["g_final"].rearrange("(a n) -> a n", a=1).to_broadcast([P, D]), gfin_loaded)
            for c in range(3):
                sp.wait_ge(out_ready, c + 1)
                out = d["y_prompt"][0, c * P:(c + 1) * P] if c < 2 else d["y_sample"].rearrange("b t n -> (b t) n")
                load(out, h[0:ROWS[c], c, :], out_stored)
            sp.wait_ge(out_stored, 48)


_OUTS = ["y_prompt", "y_sample", "new_k_prompt", "new_v_prompt", "new_logf_prompt", "new_conv_prompt",
         "new_mem_k_prompt", "new_mem_v_prompt", "new_k_sample", "new_v_sample", "new_logf_sample", "new_conv_sample"]


def kernel(**inputs):
    import numpy as np
    import concourse.bacc as bacc
    from concourse.bass_utils import run_bass_kernel_spmd

    xp, xs = inputs["x_prompt"].shape, inputs["x_sample"].shape
    L, _, _, NH, DH = inputs["cache_k"].shape
    NM, XH, XD = inputs["cache_mem_k"].shape[2:]
    hist, cw = inputs["cache_conv"].shape[2:]
    shapes = [xp, xs, (L, xp[0], xp[1], NH, DH), (L, xp[0], xp[1], NH, DH), (L, xp[0], xp[1], NH), (L, xp[0], hist, cw),
              (L, xp[0], NM, XH, XD), (L, xp[0], NM, XH, XD), (L, xs[0], xs[1], NH, DH), (L, xs[0], xs[1], NH, DH),
              (L, xs[0], xs[1], NH), (L, xs[0], hist, cw)]
    nc = bacc.Bacc("TRN2", target_bir_lowering=False, num_devices=1)
    arrays, d = {}, {}
    for name, a in inputs.items():
        a = np.ascontiguousarray(a)
        arrays["in_" + name] = a
        d[name] = nc.dram_tensor("in_" + name, a.shape, mybir.dt.from_np(a.dtype), kind="ExternalInput").ap()
    for name, shape in zip(_OUTS, shapes):
        d[name] = nc.dram_tensor("out_" + name, shape, F32, kind="ExternalOutput").ap()
    build_program(nc, d)
    r = run_bass_kernel_spmd(nc, [arrays], core_ids=[0])
    return tuple(r.results[0]["out_" + name] for name in _OUTS)
```
